# Optimizing a Trainium2 kernel written in Bass

```python
import jax, jax.numpy as jnp
from jax import lax
import numpy as np

D_MODEL = 1024
BATCH = 1
SEQ = 512
DEPTH = 1

D_MIX = D_MODEL
D_HG = D_MIX // 2
HG_HEAD_DIM = 128
HG_HEADS = D_HG // HG_HEAD_DIM
D_RG = D_MIX - D_HG
RG_BLOCKS = 8
RG_BLOCK_DIM = D_RG // RG_BLOCKS
RG_CONV_W = 4
RG_CONV_LEFT = RG_CONV_W // 2
RG_C = 8.0
D_FF = 2816
CHUNK = 64
EPS = 1e-6
N_MOD = 9
IN_COLS = 5 * D_HG + 2 * D_RG

kernel_name = "hymba_hgrn2_rglru_macaron_adaln"

def rms_norm(x, gain):
    xf = x.astype(jnp.float32)
    y = xf * lax.rsqrt(jnp.mean(xf * xf, axis=-1, keepdims=True) + EPS)
    return (y * gain.astype(jnp.float32)).astype(x.dtype)

def modulate(h, shift, scale):
    return h * (1 + scale[:, None, :]) + shift[:, None, :]

def swiglu(h, w1, w3, w2):
    return (jax.nn.silu(h @ w1) * (h @ w3)) @ w2

def gla_chunk_scan(q, k, v, log_g):
    B, T, H, dk = q.shape
    dv = v.shape[-1]
    n = T // CHUNK

    def to_chunks(a):
        return a.astype(jnp.float32).reshape(B, n, CHUNK, H, a.shape[-1]).transpose(1, 0, 3, 2, 4)

    qc, kc, vc, gc = to_chunks(q), to_chunks(k), to_chunks(v), to_chunks(log_g)
    mask = jnp.tril(jnp.ones((CHUNK, CHUNK), dtype=bool))[:, :, None]

    def step(S, inp):
        qb, kb, vb, gb = inp
        b = jnp.cumsum(gb, axis=-2)
        b_last = b[..., -1:, :]
        o_inter = jnp.einsum('bhck,bhkv->bhcv', qb * jnp.exp(b), S)
        diff = b[..., :, None, :] - b[..., None, :, :]
        decay = jnp.exp(jnp.where(mask, diff, -jnp.inf))
        scores = jnp.einsum('bhtk,bhsk,bhtsk->bhts', qb, kb, decay)
        o = o_inter + jnp.einsum('bhts,bhsv->bhtv', scores, vb)
        S = (jnp.exp(b_last[..., 0, :])[..., None] * S
             + jnp.einsum('bhck,bhcv->bhkv', kb * jnp.exp(b_last - b), vb))
        return S, o

    S0 = jnp.zeros((B, H, dk, dv), jnp.float32)
    _, o = lax.scan(step, S0, (qc, kc, vc, gc))
    return o.transpose(1, 0, 3, 2, 4).reshape(B, T, H, dv).astype(q.dtype)

def layer_lower_bound(lb_param, layer):
    s = jax.nn.softmax(lb_param.astype(jnp.float32), axis=0)
    return (jnp.cumsum(s, axis=0) - s[0])[layer + 1]

def hgrn2_mixer(q_raw, f_fwd_raw, f_bwd_raw, i_raw, g_raw, lb_fwd, lb_bwd, norm_gain):
    B, T, _ = q_raw.shape
    split = lambda a: a.reshape(B, T, HG_HEADS, HG_HEAD_DIM)
    q = split(jax.nn.silu(q_raw))
    v = split(i_raw)

    def direction(f_raw, lb, reverse):
        f = lb + (1 - lb) * jax.nn.sigmoid(f_raw.astype(jnp.float32))
        k = split((1 - f).astype(q_raw.dtype))
        lg = split(jnp.log(f))
        if reverse:
            return gla_chunk_scan(q[:, ::-1], k[:, ::-1], v[:, ::-1], lg[:, ::-1])[:, ::-1]
        return gla_chunk_scan(q, k, v, lg)

    o = direction(f_fwd_raw, lb_fwd, False) + direction(f_bwd_raw, lb_bwd, True)
    o = rms_norm(o, norm_gain).reshape(B, T, D_HG)
    return o * jax.nn.silu(g_raw)

def centred_dwconv(x, w, b):
    y = lax.conv_general_dilated(
        x, w[:, None, :].astype(x.dtype), window_strides=(1,),
        padding=[(RG_CONV_LEFT, RG_CONV_W - 1 - RG_CONV_LEFT)],
        dimension_numbers=('NWC', 'WIO', 'NWC'), feature_group_count=x.shape[-1])
    return y + b

def rglru_direction(xc, w_a, b_a, w_x, b_x, lam, reverse):
    B, T, _ = xc.shape
    xf = xc.astype(jnp.float32)
    xb = xf.reshape(B, T, RG_BLOCKS, RG_BLOCK_DIM)
    r = jax.nn.sigmoid(jnp.einsum('btnd,nde->btne', xb, w_a.astype(jnp.float32)).reshape(B, T, D_RG)
                       + b_a.astype(jnp.float32))
    i = jax.nn.sigmoid(jnp.einsum('btnd,nde->btne', xb, w_x.astype(jnp.float32)).reshape(B, T, D_RG)
                       + b_x.astype(jnp.float32))
    log_a = -RG_C * r * jax.nn.softplus(-lam.astype(jnp.float32))
    a = jnp.exp(log_a)
    u = jnp.sqrt(-jnp.expm1(2 * log_a)) * (i * xf)

    def combine(e1, e2):
        a1, b1 = e1
        a2, b2 = e2
        return a1 * a2, a2 * b1 + b2

    _, h = lax.associative_scan(combine, (a, u), axis=1, reverse=reverse)
    return h

def rglru_mixer(rx, rgate, conv_w, conv_b,
                wa_f, ba_f, wx_f, bx_f, lam_f, wa_b, ba_b, wx_b, bx_b, lam_b):
    xc = centred_dwconv(rx, conv_w, conv_b)
    h = (rglru_direction(xc, wa_f, ba_f, wx_f, bx_f, lam_f, False)
         + rglru_direction(xc, wa_b, ba_b, wx_b, bx_b, lam_b, True))
    return h.astype(rx.dtype) * jax.nn.gelu(rgate)

def setup_inputs(seed: int = 0) -> dict:
    key = jax.random.key(seed)
    ks = jax.random.split(key, 40)
    f32 = jnp.float32
    nrm = lambda k, shape, fan_in: jax.random.normal(k, shape, f32) * (fan_in ** -0.5)
    gain = lambda k, shape: 1.0 + 0.05 * jax.random.normal(k, shape, f32)
    small = lambda k, shape: 0.01 * jax.random.normal(k, shape, f32)

    def lam_init(k):
        a_c = jax.random.uniform(k, (DEPTH, D_RG), f32, 0.9, 0.999)
        a0 = a_c ** (1.0 / RG_C)
        return jnp.log(a0) - jnp.log1p(-a0)

    return {
        "x": jax.random.normal(ks[0], (BATCH, SEQ, D_MODEL), f32),
        "c": jax.random.normal(ks[1], (BATCH, D_MODEL), f32),
        "w_ada": nrm(ks[2], (DEPTH, D_MODEL, N_MOD * D_MODEL), D_MODEL),
        "b_ada": small(ks[3], (DEPTH, N_MOD * D_MODEL)),
        "ffn1_norm": gain(ks[4], (DEPTH, D_MODEL)),
        "ffn1_w1": nrm(ks[5], (DEPTH, D_MODEL, D_FF), D_MODEL),
        "ffn1_w3": nrm(ks[6], (DEPTH, D_MODEL, D_FF), D_MODEL),
        "ffn1_w2": nrm(ks[7], (DEPTH, D_FF, D_MODEL), D_FF),
        "mix_norm": gain(ks[8], (DEPTH, D_MODEL)),
        "w_in": nrm(ks[9], (DEPTH, D_MODEL, IN_COLS), D_MODEL),
        "hg_lb_fwd": jax.random.normal(ks[10], (DEPTH + 1, D_HG), f32),
        "hg_lb_bwd": jax.random.normal(ks[11], (DEPTH + 1, D_HG), f32),
        "hg_out_norm": gain(ks[12], (DEPTH, HG_HEAD_DIM)),
        "rg_conv_w": nrm(ks[13], (DEPTH, RG_CONV_W, D_RG), RG_CONV_W),
        "rg_conv_b": small(ks[14], (DEPTH, D_RG)),
        "rg_wa_fwd": nrm(ks[15], (DEPTH, RG_BLOCKS, RG_BLOCK_DIM, RG_BLOCK_DIM), RG_BLOCK_DIM),
        "rg_ba_fwd": small(ks[16], (DEPTH, D_RG)),
        "rg_wx_fwd": nrm(ks[17], (DEPTH, RG_BLOCKS, RG_BLOCK_DIM, RG_BLOCK_DIM), RG_BLOCK_DIM),
        "rg_bx_fwd": small(ks[18], (DEPTH, D_RG)),
        "rg_lam_fwd": lam_init(ks[19]),
        "rg_wa_bwd": nrm(ks[20], (DEPTH, RG_BLOCKS, RG_BLOCK_DIM, RG_BLOCK_DIM), RG_BLOCK_DIM),
        "rg_ba_bwd": small(ks[21], (DEPTH, D_RG)),
        "rg_wx_bwd": nrm(ks[22], (DEPTH, RG_BLOCKS, RG_BLOCK_DIM, RG_BLOCK_DIM), RG_BLOCK_DIM),
        "rg_bx_bwd": small(ks[23], (DEPTH, D_RG)),
        "rg_lam_bwd": lam_init(ks[24]),
        "w_out": nrm(ks[25], (DEPTH, D_MIX, D_MODEL), D_MIX),
        "ffn2_norm": gain(ks[26], (DEPTH, D_MODEL)),
        "ffn2_w1": nrm(ks[27], (DEPTH, D_MODEL, D_FF), D_MODEL),
        "ffn2_w3": nrm(ks[28], (DEPTH, D_MODEL, D_FF), D_MODEL),
        "ffn2_w2": nrm(ks[29], (DEPTH, D_FF, D_MODEL), D_FF),
        "final_norm": gain(ks[30], (D_MODEL,)),
    }

def reference(x, c, w_ada, b_ada, ffn1_norm, ffn1_w1, ffn1_w3, ffn1_w2, mix_norm, w_in,
              hg_lb_fwd, hg_lb_bwd, hg_out_norm, rg_conv_w, rg_conv_b,
              rg_wa_fwd, rg_ba_fwd, rg_wx_fwd, rg_bx_fwd, rg_lam_fwd,
              rg_wa_bwd, rg_ba_bwd, rg_wx_bwd, rg_bx_bwd, rg_lam_bwd,
              w_out, ffn2_norm, ffn2_w1, ffn2_w3, ffn2_w2, final_norm):
    split_idx = [D_HG, 2 * D_HG, 3 * D_HG, 4 * D_HG, 5 * D_HG, 5 * D_HG + D_RG]
    for l in range(DEPTH):
        mod = jax.nn.silu(c) @ w_ada[l] + b_ada[l]
        sh1, sc1, g1, sh2, sc2, g2, sh3, sc3, g3 = jnp.split(mod, N_MOD, axis=-1)

        h = modulate(rms_norm(x, ffn1_norm[l]), sh1, sc1)
        x = x + 0.5 * g1[:, None, :] * swiglu(h, ffn1_w1[l], ffn1_w3[l], ffn1_w2[l])

        h = modulate(rms_norm(x, mix_norm[l]), sh2, sc2)
        z = h @ w_in[l]
        q_raw, f_fwd_raw, f_bwd_raw, i_raw, g_raw, rx, rgate = jnp.split(z, split_idx, axis=-1)
        o_hg = hgrn2_mixer(q_raw, f_fwd_raw, f_bwd_raw, i_raw, g_raw,
                           layer_lower_bound(hg_lb_fwd, l), layer_lower_bound(hg_lb_bwd, l),
                           hg_out_norm[l])
        o_rg = rglru_mixer(rx, rgate, rg_conv_w[l], rg_conv_b[l],
                           rg_wa_fwd[l], rg_ba_fwd[l], rg_wx_fwd[l], rg_bx_fwd[l], rg_lam_fwd[l],
                           rg_wa_bwd[l], rg_ba_bwd[l], rg_wx_bwd[l], rg_bx_bwd[l], rg_lam_bwd[l])
        y = jnp.concatenate([o_hg, o_rg], axis=-1) @ w_out[l]
        x = x + g2[:, None, :] * y

        h = modulate(rms_norm(x, ffn2_norm[l]), sh3, sc3)
        x = x + 0.5 * g3[:, None, :] * swiglu(h, ffn2_w1[l], ffn2_w3[l], ffn2_w2[l])
    return rms_norm(x, final_norm)


_drawn_inputs = setup_inputs


def setup_inputs(seed=0):
    import zlib

    import numpy as np

    out = dict(_drawn_inputs(seed))
    spreads = {}
    factors = {'ffn1_norm': 2.912,
     'hg_lb_fwd': 8.0,
     'hg_lb_bwd': 8.0,
     'hg_out_norm': 7.455,
     'rg_conv_b': 4.27,
     'rg_ba_fwd': 64.0,
     'rg_bx_fwd': 44.125,
     'rg_ba_bwd': 64.0,
     'rg_bx_bwd': 38.383,
     'ffn2_norm': 6.084}
    for name, (base, spread) in spreads.items():
        noise = np.random.default_rng([zlib.crc32(name.encode()), seed]).standard_normal(out[name].shape)
        drawn = base * np.exp(spread * noise) if base else spread * noise
        out[name] = __import__('jax').numpy.asarray(drawn.astype(out[name].dtype))
    for name, factor in factors.items():
        out[name] = (out[name] * factor).astype(out[name].dtype)
    return out
```

```python
from contextlib import ExitStack

import numpy as np
import concourse.bass as bass
from concourse import mybir

F32 = mybir.dt.float32
F32R = mybir.dt.float32r
U8 = mybir.dt.uint8
ALU = mybir.AluOpType
ACT = mybir.ActivationFunctionType

P = 128
T = 512
D = 1024
FF = 2816
KD = D // P
KF = FF // P
TC = T // P
HEADS = 4
RT = 4
N_MOD = 9
EPS = 1e-6
UNIT = KD * P
HALF_UNITS = KF // 2
LEVELS = (64, 32, 16, 8, 4, 2, 1)

U_FFN1 = 0
U_MIX = U_FFN1 + 3 * KF
N_Z = 28
U_OUT = U_MIX + N_Z
U_FFN2 = U_OUT + 8
N_UNITS = U_FFN2 + 3 * KF
Z_UNITS = ([("v", i) for i in range(4)] + [("rx", i) for i in range(4)] + [("g", 0), ("g", 1)]
           + [(w, 0) for w in "qfb"] + [(w, 1) for w in "qfb"] + [("g", 2), ("g", 3)]
           + [(w, 2) for w in "qfb"] + [("gate", 0), ("gate", 1)]
           + [(w, 3) for w in "qfb"] + [("gate", 2), ("gate", 3)])
Z_COLUMN = {"q": 0, "f": 512, "b": 1024, "v": 1536, "g": 2048, "rx": 2560, "gate": 3072}
MODS = ("sc1", "sh1", "g1", "sh2", "sc2", "g2", "sh3", "sc3", "g3")
MOD_AT = {"sh1": 0, "sc1": 1, "g1": 2, "sh2": 3, "sc2": 4, "g2": 5, "sh3": 6, "sc3": 7, "g3": 8}
VEC = {}
_at = 0
for _name, _n in (("c", 8), ("b_ada", 72), ("norm0", 8), ("norm1", 8), ("norm2", 8), ("norm3", 8),
                  ("lb", 16), ("hg_norm", 1), ("conv_w", 16), ("conv_b", 4), ("ba", 8), ("bx", 8), ("lam", 8)):
    VEC[_name] = _at
    _at += _n
N_VEC = _at


def build(nc, xt, wu, wada, vecs_in, bd_in, consts_in, out):
    with ExitStack() as ctx:
        place = [nc.sbuf_base + (-nc.sbuf_base) % 64]

        def at(name, shape, dt, offset):
            n = int(np.prod(shape[1:])) * (1 if dt == U8 else 4)
            return nc.alloc_sbuf_tensor_at(name, shape, dt, offset=offset), offset + (n + 63) // 64 * 64

        def sb(name, shape, dt=F32):
            t, place[0] = at(name, shape, dt, place[0])
            return t

        def sem(name):
            return ctx.enter_context(nc.semaphore(name))

        x = sb("x", [P, KD, T])
        h_at = place[0]
        hhi = sb("hhi", [P, KD, T], F32R)
        hlo = sb("hlo", [P, KD, T], F32R)
        raw = sb("raw", [P, 2, UNIT])
        whi = sb("whi", [P, 2, UNIT], F32R)
        wlo = sb("wlo", [P, 2, UNIT], F32R)
        vecs = sb("vecs", [P, N_VEC])
        ident = sb("ident", [P, P])
        ones = sb("ones", [P, P])
        epst = sb("epst", [P, 1])
        cs = sb("cs", [P, KD])
        mods = sb("mods", [P, N_MOD * KD])
        scale = sb("scale", [P, 3 * KD])
        gates = sb("gates", [P, 3 * KD])
        rms = sb("rms", [P, TC])
        rinv = sb("rinv", [P, TC])
        diag = sb("diag", [P, TC, P])
        tmp = sb("tmp", [P, 2, T])
        small = sb("small", [P, 136])
        sp, nsp = small[:, 0:8], small[:, 8:16]
        lbt, oml = small[:, 16:24], small[:, 24:32]
        arena = place[0]
        off = arena
        ghi, off = at("ghi", [P, KF, T], F32R, off)
        glo, off = at("glo", [P, KF, T], F32R, off)
        sq, off = at("sq", [P, 4, T], F32, off)
        silu_sb, off = at("silu_sb", [P, T], F32, off)
        g32, off = at("g32", [P, T], F32, off)
        ada, off = at("ada", [P, 4, D], F32, off)
        acc, off = at("acc", [P, D], F32, off)
        fin, off = at("fin", [P, D], F32, off)
        outt, _ = at("outt", [P, KD, T], F32, arena)
        yhi, _ = at("yhi", [P, KD, T], F32R, h_at)
        ylo, _ = at("ylo", [P, KD, T], F32R, h_at + KD * T * 4)
        off = arena
        vn, off = at("vn", [P, TC, T], F32, off)
        pt, off = at("pt", [P, TC * TC, P], F32, off)
        w3, off = at("w3", [P, 2, 3, T], F32, off)
        cum, off = at("cum", [P, 2, 2, T], F32, off)
        dif, off = at("dif", [P, 2, 2, T], F32, off)
        dec, off = at("dec", [P, 2, 2, T], F32, off)
        qk, off = at("qk", [P, 2, 2, T], F32, off)
        lg, off = at("lg", [P, 2 * 517], F32, off)
        far, off = at("far", [P, 4, P], F32, off)
        tot, off = at("tot", [P, 2, TC], F32, off)
        etot, off = at("etot", [P, 2, 2, TC], F32, off)
        lgend, off = at("lgend", [P, TC], F32, off)
        masks, off = at("masks", [P, 7, P], U8, off)
        resets, off = at("resets", [P, T], F32, off)
        osb, osq = tmp[:, 0, :], tmp[:, 1, :]
        sg, off = at("sg", [P, HEADS, T], F32, off)
        xc, off = at("xc", [P, RT, T], F32, off)
        rxp, off = at("rxp", [P, RT, T + 4], F32, off)
        hr, _ = at("hr", [P, RT, T], F32, off - RT * (T + 4) * 4)
        gg, _ = at("gg", [P, RT, T], F32, off)
        ra, off = at("ra", [P, RT, T], F32, off)
        on, _ = at("on", [P, HEADS, T], F32, off)
        rt, off = at("rt", [P, RT, T], F32, off)
        ri, off = at("ri", [P, RT, T], F32, off)
        mask_f = dif[:].rearrange("p a l t -> p (a l t)")[:, 0:7 * P]
        a2 = qk[:, 1]
        bd, off = at("bd", [P, 4, RT, P], F32, off)

        psum = ctx.enter_context(nc.psum_tensor("psum", [P, 8, T], F32))
        bank = [psum[:, b, :] for b in range(8)]
        sums, modp, rb = psum[:, 6, 0:TC], psum[:, 6, 16:24], psum[:, 7, :]

        vecs_loaded, x_loaded, mix_loaded = sem("vecs_loaded"), sem("x_loaded"), sem("mix_loaded")
        ada_loaded = [sem(f"ada_loaded{i}") for i in range(4)]
        raw_loaded = [sem(f"raw_loaded{i}") for i in range(2)]
        hi_done, lo_done, unit_used = sem("hi_done"), sem("lo_done"), sem("unit_used")
        ones_set, cs_done, small_done = sem("ones_set"), sem("cs_done"), sem("small_done")
        ada_added, mod_summed, mod_ready = sem("ada_added"), sem("mod_summed"), sem("mod_ready")
        cols_ready = sem("cols_ready")
        sq_done, sq_used, rms_done, rinv_done = sem("sq_done"), sem("sq_used"), sem("rms_done"), sem("rinv_done")
        diag_done, rb_done, htmp_done = sem("diag_done"), sem("rb_done"), sem("htmp_done")
        hhi_done, hlo_done = sem("hhi_done"), sem("hlo_done")
        silu_done, gate_prod, ghi_done, glo_done = sem("silu_done"), sem("gate_prod"), sem("ghi_done"), sem("glo_done")
        x_ready, out_ready, stored = sem("x_ready"), sem("out_ready"), sem("stored")
        masks_set = sem("masks_set")
        v_copied, z_evac, rxp_zero = sem("v_copied"), sem("z_evac"), sem("rxp_zero")
        conv_step, xc_ready = sem("conv_step"), sem("xc_ready")
        gates_summed, gate_evac, tanh_done, a_done = sem("gates_summed"), sem("gate_evac"), sem("tanh_done"), sem("a_done")
        a2_done, one_a2, root_done = sem("a2_done"), sem("one_a2"), sem("root_done")
        rg_step, rg_scanned = sem("rg_step"), sem("rg_scanned")
        k_done, ln_done = sem("k_done"), sem("ln_done")
        cum_step, cum_ready, tot_ready, etot_done = sem("cum_step"), sem("cum_ready"), sem("tot_ready"), sem("etot_done")
        dif_done, dec_done, qk_done, far_done = sem("dif_done"), sem("dec_done"), sem("qk_done"), sem("far_done")
        scored, blk_copied, blk_masked = sem("scored"), sem("blk_copied"), sem("blk_masked")
        pv_done, osb_done, osq_done, osum_done = sem("pv_done"), sem("osb_done"), sem("osq_done"), sem("osum_done")
        orms_done, orinv_done, odiag_done, orb_done = sem("orms_done"), sem("orinv_done"), sem("odiag_done"), sem("orb_done")
        on_step, on_done, yrg_done, yhi_done, y_ready = (sem("on_step"), sem("on_done"), sem("yrg_done"),
                                                         sem("yhi_done"), sem("y_ready"))

        def vec(name, i=0, n=1):
            return vecs[:, VEC[name] + i:VEC[name] + i + n]

        def mod(name, i=0, n=1):
            m = MODS.index(name) * KD + i
            return mods[:, m:m + n]

        SHIFT = ("sh1", "sh2", "sh3")
        STEPS = 4 + len(LEVELS)

        def evac_wait(eng, h, s):
            if s < 4:
                eng.wait_ge(blk_copied, 4 * h + s + 1)
            else:
                eng.wait_ge(blk_masked, (STEPS - 4) * h + s - 3)

        def step_before(h, s, n):
            g = STEPS * h + s - n
            return (g // STEPS, g % STEPS) if g >= 0 else None

        block = ctx.enter_context(nc.Block())

        @block.sync
        def _(sp_):
            sp_.dma_start(vecs[:], vecs_in).then_inc(vecs_loaded, 16)
            sp_.dma_start(ident[:], consts_in[:, 0:P]).then_inc(vecs_loaded, 16)
            for i in range(2):
                n = KD // 2
                sp_.dma_start(x[:, n * i:n * i + n, :], xt[T * i:T * i + T].rearrange("(d p) t -> p d t", p=P)
                              ).then_inc(x_loaded, 16)
            for u in range(2):
                sp_.dma_start(raw[:, u, :], wu[u]).then_inc(raw_loaded[u], 16)
            with sp_.Fori(1, N_UNITS // 2) as j:
                for s in range(2):
                    sp_.wait_ge(lo_done, 2 * j + (s - 1))
                    sp_.dma_start(raw[:, s, :], wu[bass.ds(2 * j + s, 1)].rearrange("a p n -> p (a n)")
                                  ).then_inc(raw_loaded[s], 16)
            for d in range(KD):
                sp_.wait_ge(out_ready, d + 1)
                sp_.dma_start(out[d * P:(d + 1) * P, :], outt[:, d, :]).then_inc(stored, 16)
            sp_.wait_ge(stored, 16 * KD)

        @block.gpsimd
        def _(pool):
            for k in range(4):
                pool.dma_start(ada[:, k, :], wada[k]).then_inc(ada_loaded[k], 16)
            for k in range(4, 8):
                pool.wait_ge(ada_added, k - 3)
                pool.dma_start(ada[:, k % 4, :], wada[k]).then_inc(ada_loaded[k % 4], 16)
            with pool.Fori(1, N_MOD) as j:
                for k in range(8):
                    pool.wait_ge(ada_added, 8 * j + (k - 3))
                    pool.dma_start(ada[:, k % 4, :], wada[bass.ds(8 * j + k, 1)].rearrange("a p n -> p (a n)")
                                   ).then_inc(ada_loaded[k % 4], 16)
            pool.wait_ge(unit_used, U_MIX)
            pool.wait_ge(sq_used, 2 * KD)
            pool.dma_start(bd[:], bd_in).then_inc(mix_loaded, 16)
            pool.dma_start(mask_f, consts_in[:, P + T:P + T + 7 * P]).then_inc(mix_loaded, 16)
            pool.dma_start(resets[:], consts_in[:, P:P + T]).then_inc(mix_loaded, 16)
            pool.wait_ge(masks_set, 1)
            for h in range(HEADS):
                p = h % 2
                pool.wait_ge(tot_ready, 2 * (h + 1))
                if h:
                    pool.wait_ge(dec_done, 9 * h)
                nc.gpsimd.tensor_tensor(dif[:, 1].rearrange("p l (c t) -> p l c t", c=TC),
                                        tot[:].unsqueeze(3).broadcast_to([P, 2, TC, P]),
                                        cum[:, p].rearrange("p l (c t) -> p l c t", c=TC),
                                        ALU.subtract).then_inc(dif_done, 1)
                for i, hw in enumerate(LEVELS):
                    e = i + 2
                    if e > 2:
                        pool.wait_ge(dec_done, 9 * h + e - 1)
                    c5 = cum[:, p].rearrange("p l (n two w) -> p l n two w", two=2, w=hw)
                    d5 = dif[:, e % 2].rearrange("p l (n two w) -> p l n two w", two=2, w=hw)
                    ref = c5[:, :, :, 1, 0:1].broadcast_to([P, 2, T // (2 * hw), hw])
                    nc.gpsimd.tensor_tensor(d5[:, :, :, 1, :], c5[:, :, :, 1, :], ref, ALU.subtract)
                    nc.gpsimd.tensor_tensor(d5[:, :, :, 0, :], ref, c5[:, :, :, 0, :],
                                            ALU.subtract).then_inc(dif_done, 1)

        @block.scalar
        def _(act):
            def hi(j, slot):
                act.wait_ge(raw_loaded[slot], 16 * (j + 1))
                if not (isinstance(j, int) and j == 0):
                    act.wait_ge(unit_used, 2 * j + (slot - 1))
                nc.scalar.activation(whi[:, slot, :], raw[:, slot, :], ACT.Copy).then_inc(hi_done, 1)

            def hi_u(u):
                if u < N_UNITS:
                    hi(u // 2, u % 2)

            def square(n, d):
                if n == 0:
                    act.wait_ge(x_loaded, 16 * 2)
                else:
                    act.wait_ge(x_ready, KD * (n - 1) + d + 1)
                if KD * n + d >= 4:
                    act.wait_ge(sq_used, KD * n + d - 3)
                nc.scalar.activation(sq[:, d % 4, :], x[:, d, :], ACT.Square).then_inc(sq_done, 1)

            def root(n):
                act.wait_ge(sq_used, KD * (n + 1))
                nc.scalar.activation(rms[:], sums, ACT.Sqrt, bias=epst[:], scale=1.0 / D).then_inc(rms_done, 1)

            def h_upper(n):
                for d in range(KD):
                    act.wait_ge(htmp_done, KD * n + d + 1)
                    nc.scalar.activation(hhi[:, d, :], tmp[:, d % 2, :], ACT.Identity,
                                         bias=mod(SHIFT[n], d)).then_inc(hhi_done, 1)

            def up_step(n, f, fp, i):
                j = (U_FFN1, U_FFN2)[n] // 2 + 2 * i + fp
                hi(j + 1, 0)
                act.wait_ge(unit_used, 2 * j + 1)
                if not (isinstance(f, int) and KF * n + f == 0):
                    act.wait_ge(gate_prod, f + KF * n)
                nc.scalar.activation(silu_sb[:], bank[fp], ACT.Silu).then_inc(silu_done, 1)
                hi(j + 1, 1)
                act.wait_ge(gate_prod, f + (KF * n + 1))
                nc.scalar.activation(ghi[:, bass.ds(f, 1), :].rearrange("p a t -> p (a t)"), g32[:],
                                     ACT.Copy).then_inc(ghi_done, 1)

            def ffn_up(n):
                for fp in range(2):
                    up_step(n, fp, fp, 0)
                nc.scalar.preload_act_table(ACT.Silu)
                with act.Fori(1, KF // 2) as i:
                    for fp in range(2):
                        up_step(n, 2 * i + fp, fp, i)

            def ffn_down(n):
                norm = (1, 3)[n]
                u0 = (U_FFN1, U_FFN2)[n] + 2 * KF
                for half in range(2):
                    u = u0 + HALF_UNITS * half
                    hi_u(u + 2)
                    if half:
                        for d in range(4):
                            square(norm, d)
                    last = n == 1 and half == 1
                    with act.Fori(0, (HALF_UNITS - 1) // 2 - last) as i:
                        for s in range(2):
                            v = u + 3 + s
                            hi(i + v // 2, v % 2)
                nc.scalar.preload_act_table(ACT.Sqrt)
                for d in range(4, KD):
                    square(norm, d)
                root(norm)

            act.wait_ge(vecs_loaded, 32)
            nc.scalar.activation(cs[:], vec("c", 0, 8), ACT.Silu).then_inc(cs_done, 1)
            act.wait_ge(small_done, 1)
            nc.scalar.activation(small[:, 32:40], small[:, 32:40], ACT.Exp).then_inc(cs_done, 1)
            nc.scalar.activation(small[:, 40:56], small[:, 40:56], ACT.Exp).then_inc(cs_done, 1)
            for d in range(KD):
                square(0, d)
            act.wait_ge(ones_set, 2)
            root(0)
            hi(0, 0)
            hi(0, 1)
            h_upper(0)
            ffn_up(0)
            ffn_down(0)
            h_upper(1)

            zi = {u: m for m, u in enumerate(Z_UNITS)}

            def z_bank(m):
                act.wait_ge(unit_used, U_MIX + m + 1)
                return bank[m % 2]

            def z_post(m):
                what, i = Z_UNITS[m]
                hi_u(U_MIX + m + 2)
                if what == "v":
                    if i == 3:
                        act.wait_ge(unit_used, U_MIX + 4)
                        for c in range(TC):
                            nc.scalar.activation(vn[:, c, :], bank[2 + c], ACT.Copy).then_inc(v_copied, 1)
                    return
                src = z_bank(m)
                if what == "rx":
                    nc.scalar.activation(rxp[:, i, 2:2 + T], src, ACT.Copy).then_inc(z_evac, 1)
                elif what == "g":
                    nc.scalar.activation(sg[:, i, :], src, ACT.Silu).then_inc(z_evac, 1)
                elif what == "gate":
                    act.wait_ge(rg_scanned, 2 * RT)
                    nc.scalar.activation(gg[:, i, :], src, ACT.Gelu_apprx_tanh).then_inc(z_evac, 1)
                else:
                    if what == "q" and i >= 2:
                        act.wait_ge(qk_done, 10 * (i - 1))
                        act.wait_ge(scored, STEPS * (i - 1))
                    slot = {"f": 0, "q": 1, "b": 2}[what]
                    nc.scalar.activation(w3[:, i % 2, slot, :], src, ACT.Silu if what == "q" else ACT.Sigmoid
                                         ).then_inc(z_evac, 1)

            def logs(h):
                for lane in range(2):
                    act.wait_ge(k_done, 4 * h + 2 * lane + 2)
                    v = lg[:, 517 * lane:517 * lane + T]
                    nc.scalar.activation(v, v, ACT.Ln).then_inc(ln_done, 1)

            def gate_post(dr, ct):
                gi = RT * dr + ct
                act.wait_ge(gates_summed, gi + 1)
                if dr:
                    act.wait_ge(rg_scanned, ct + 1)
                nc.scalar.activation(ra[:, ct, :], bank[2], ACT.Sigmoid, bias=vec("ba", gi)).then_inc(gate_evac, 1)
                nc.scalar.activation(ri[:, ct, :], bank[3], ACT.Sigmoid, bias=vec("bx", gi)).then_inc(gate_evac, 1)
                act.wait_ge(gate_evac, 2 * gi + 1)
                nc.scalar.activation(rt[:, ct, :], ra[:, ct, :], ACT.Tanh, scale=sp[:, gi:gi + 1]).then_inc(tanh_done, 1)

            def rg_exp(dr):
                for ct in range(RT):
                    gi = RT * dr + ct
                    act.wait_ge(tanh_done, gi + 1)
                    nc.scalar.activation(ra[:, ct, :], ra[:, ct, :], ACT.Exp, scale=nsp[:, gi:gi + 1]).then_inc(a_done, 1)
                    act.wait_ge(a_done, gi + 1)
                    if gi >= 2:
                        act.wait_ge(one_a2, gi - 1)
                    nc.scalar.activation(a2[:, ct % 2, :], ra[:, ct, :], ACT.Square).then_inc(a2_done, 1)

            def rg_root(dr):
                for ct in range(RT):
                    act.wait_ge(one_a2, RT * dr + ct + 1)
                    nc.scalar.activation(rt[:, ct, :], rt[:, ct, :], ACT.Sqrt).then_inc(root_done, 1)

            def decay(h, e):
                if e >= 2:
                    act.wait_ge(qk_done, 10 * h + e - 1)
                elif h:
                    act.wait_ge(qk_done, 10 * (h - 1) + 9)
                if e == 0:
                    act.wait_ge(tot_ready, 2 * (h + 1))
                    if h:
                        act.wait_ge(far_done, h)
                    nc.scalar.activation(etot[:, h % 2], tot[:], ACT.Exp).then_inc(etot_done, 1)
                    nc.scalar.activation(dec[:, 0], cum[:, h % 2], ACT.Exp).then_inc(dec_done, 1)
                else:
                    act.wait_ge(dif_done, 8 * h + e)
                    nc.scalar.activation(dec[:, e % 2], dif[:, e % 2], ACT.Exp).then_inc(dec_done, 1)

            def block_copy(h, s):
                act.wait_ge(scored, STEPS * h + s + 1)
                if s == 0 and h:
                    act.wait_ge(pv_done, h)
                src = bank[4 + (STEPS * h + s) % 2]
                if s == 0:
                    nc.scalar.activation(pt[:, 1:5:3, :], src[:, 0:256].rearrange("p (b t) -> p b t", b=2), ACT.Copy)
                    nc.scalar.activation(pt[:, 11:15:3, :], src[:, 256:512].rearrange("p (b t) -> p b t", b=2),
                                         ACT.Copy).then_inc(blk_copied, 1)
                else:
                    p4 = pt[:].rearrange("p (a b) t -> p a b t", a=TC)
                    dst = {1: p4[:, 0:2, 2:4, :], 2: p4[:, 2:4, 0:2, :], 3: pt[:, 0:16:5, :]}[s]
                    src = (src.rearrange("p (b t) -> p b t", b=4) if s == 3
                           else src.rearrange("p (a b t) -> p a b t", a=2, b=2))
                    nc.scalar.activation(dst, src, ACT.Copy).then_inc(blk_copied, 1)

            def o_copy(h):
                act.wait_ge(pv_done, h + 1)
                if h:
                    act.wait_ge(on_done, h)
                    act.wait_ge(osum_done, h)
                nc.scalar.activation(osb, bank[6], ACT.Copy).then_inc(osb_done, 1)
                nc.scalar.activation(osq, bank[6], ACT.Square).then_inc(osq_done, 1)

            def o_root(h):
                act.wait_ge(osum_done, h + 1)
                nc.scalar.activation(rms[:], psum[:, 7, 0:TC], ACT.Sqrt, bias=epst[:],
                                     scale=1.0 / P).then_inc(orms_done, 1)

            def y_upper(k):
                if k < RT:
                    act.wait_ge(yrg_done, k + 1)
                else:
                    act.wait_ge(on_done, k - 3)
                act.wait_ge(unit_used, U_OUT)
                src = hr[:, k, :] if k < RT else on[:, k - RT, :]
                nc.scalar.activation(yhi[:, k, :], src, ACT.Copy).then_inc(yhi_done, 1)

            for m in range(9):
                z_post(m)
            act.wait_ge(small_done, 2)
            gate_post(0, 0)
            gate_post(0, 1)
            z_post(9)
            gate_post(0, 2)
            gate_post(0, 3)
            rg_exp(0)
            z_post(10)
            rg_root(0)
            z_post(11)
            z_post(12)
            logs(0)
            for ct in range(RT):
                gate_post(1, ct)
            rg_exp(1)
            for r in range(HEADS):
                first = zi[("q", r + 1)] if r < 3 else None
                gaps = 10 if r < 3 else 6
                decay(r, 0)
                decay(r, 1)
                if r == 0:
                    rg_root(1)
                if r == 3:
                    for k in range(RT):
                        y_upper(k)
                s = 0
                for g in range(gaps):
                    for _ in range(2 if (r == 3 and g < 5) or (r < 3 and g == 0) else 1):
                        if 2 <= s <= 8:
                            decay(r, s)
                        if s < 4:
                            block_copy(r, s)
                        s += 1
                    if g == 0 and r:
                        o_copy(r - 1)
                    if g == 3 and r:
                        o_root(r - 1)
                    if g % 2 and r < 3:
                        z_post(first + g // 2)
                        if g // 2 == 2:
                            logs(r + 1)
                    if r == 3:
                        if g % 2:
                            hi_u(U_OUT + g // 2 + 2)
                        if g == 2:
                            y_upper(4)
                            y_upper(5)
                        if g == 5:
                            y_upper(6)
            nc.scalar.preload_act_table(ACT.Sqrt)
            o_copy(3)
            o_root(3)
            y_upper(7)
            for m in range(3, 8):
                hi_u(U_OUT + m + 2)
                if m == 4:
                    for d in range(4):
                        square(2, d)
            for d in range(4, KD):
                square(2, d)
            root(2)
            h_upper(2)
            ffn_up(1)
            ffn_down(1)

        @block.vector
        def _(dve):
            def lo(j, slot):
                dve.wait_ge(hi_done, 2 * j + (slot + 1))
                nc.vector.tensor_tensor(wlo[:, slot, :], raw[:, slot, :], whi[:, slot, :],
                                        ALU.subtract).then_inc(lo_done, 1)

            def lo_u(u):
                if u < N_UNITS:
                    lo(u // 2, u % 2)

            def ada_add(j, k):
                dve.wait_ge(ada_loaded[k % 4], 32 * j + 16 * (k // 4 + 1))
                if not (isinstance(j, int) and j == 0 and k == 0):
                    dve.wait_ge(ada_added, 8 * j + k)
                dst = acc
                if k == 7:
                    dst = fin
                    if not (isinstance(j, int) and j == 0):
                        dve.wait_ge(mod_summed, 1 * j)
                if k == 0:
                    nc.vector.tensor_scalar(dst[:], ada[:, k % 4, :], cs[:, k:k + 1], None,
                                            ALU.mult).then_inc(ada_added, 1)
                else:
                    nc.vector.scalar_tensor_tensor(dst[:], ada[:, k % 4, :], cs[:, k:k + 1], acc[:], ALU.mult,
                                                   ALU.add).then_inc(ada_added, 1)

            def mod_bias(j):
                dve.wait_ge(mod_summed, j + 1)
                nc.vector.tensor_tensor(mods[:, bass.ds(8 * j, 8)], modp, vecs[:, bass.ds(8 * j + VEC["b_ada"], 8)],
                                        ALU.add).then_inc(mod_ready, 1)

            def rms_inverse(n, done, r_done, d_done):
                dve.wait_ge(done, n + 1)
                nc.vector.reciprocal(rinv[:], rms[:]).then_inc(r_done, 1)
                dve.wait_ge(r_done, n + 1)
                nc.vector.tensor_tensor(diag[:], ident[:].unsqueeze(1).broadcast_to([P, TC, P]),
                                        rinv[:].unsqueeze(2).broadcast_to([P, TC, P]), ALU.mult).then_inc(d_done, 1)

            def h_split(n):
                dve.wait_ge(rb_done, n + 1)
                dve.wait_ge(cols_ready, 2 * n + 1)
                for d in range(KD + 1):
                    if d < KD:
                        if d >= 2:
                            dve.wait_ge(hlo_done, KD * n + d - 1)
                        nc.vector.scalar_tensor_tensor(tmp[:, d % 2, :], x[:, d, :], scale[:, KD * n + d:KD * n + d + 1],
                                                       rb, ALU.mult, ALU.mult).then_inc(htmp_done, 1)
                    if d:
                        dve.wait_ge(hhi_done, KD * n + d)
                        nc.vector.scalar_tensor_tensor(hlo[:, d - 1, :], tmp[:, (d - 1) % 2, :], mod(SHIFT[n], d - 1),
                                                       hhi[:, d - 1, :], ALU.add, ALU.subtract).then_inc(hlo_done, 1)

            def up_step(n, f, fp, i, mod_j=None):
                j = (U_FFN1, U_FFN2)[n] // 2 + 2 * i + fp
                ks = range(4 * fp, 4 * fp + 4) if mod_j is not None else ()
                lo(j + 1, 0)
                for k in ks[0:2]:
                    ada_add(mod_j, k)
                dve.wait_ge(unit_used, 2 * j + 2)
                dve.wait_ge(silu_done, f + (KF * n + 1))
                if not (isinstance(f, int) and KF * n + f == 0):
                    dve.wait_ge(glo_done, f + KF * n)
                nc.vector.tensor_tensor(g32[:], silu_sb[:], bank[2 + fp], ALU.mult).then_inc(gate_prod, 1)
                lo(j + 1, 1)
                dve.wait_ge(ghi_done, f + (KF * n + 1))
                nc.vector.tensor_tensor(glo[:, bass.ds(f, 1), :].rearrange("p a t -> p (a t)"), g32[:],
                                        ghi[:, bass.ds(f, 1), :].rearrange("p a t -> p (a t)"),
                                        ALU.subtract).then_inc(glo_done, 1)
                for k in ks[2:4]:
                    ada_add(mod_j, k)

            def update(n, d, src):
                dve.wait_ge(unit_used, (U_FFN1 + 2 * KF, U_OUT, U_FFN2 + 2 * KF)[n]
                            + (HALF_UNITS, 4, HALF_UNITS)[n] * (1 + d // 4))
                nc.vector.scalar_tensor_tensor(x[:, d, :], src, gates[:, KD * n + d:KD * n + d + 1], x[:, d, :],
                                               ALU.mult, ALU.add).then_inc(x_ready, 1)

            def columns(n):
                g, sc = ("g1", "g2", "g3")[n], ("sc2", "sc3")[n] if n < 2 else None
                dve.wait_ge(mod_ready, N_MOD)
                nc.vector.tensor_scalar(gates[:, KD * n:KD * n + KD], mod(g, 0, KD), (0.5, 1.0, 0.5)[n], None,
                                        ALU.mult).then_inc(cols_ready, 1)
                if sc:
                    nc.vector.scalar_tensor_tensor(scale[:, KD * (n + 1):KD * (n + 2)], mod(sc, 0, KD), 1.0,
                                                   vec(f"norm{n + 1}", 0, KD), ALU.add, ALU.mult).then_inc(cols_ready, 1)

            def ffn_down(n):
                branch, u0 = (0, 2)[n], (U_FFN1, U_FFN2)[n] + 2 * KF
                columns(branch)
                dve.wait_ge(cols_ready, (3, 6)[n])
                for half in range(2):
                    u = u0 + HALF_UNITS * half
                    lo_u(u + 2)
                    if half:
                        for d in range(4):
                            update(branch, d, bank[4 + d])
                    last = n == 1 and half == 1
                    with dve.Fori(0, (HALF_UNITS - 1) // 2 - last) as i:
                        for s in range(2):
                            v = u + 3 + s
                            lo(i + v // 2, v % 2)
                for d in range(4, KD):
                    update(branch, d, bank[d - 4])

            nc.vector.memset(ones[:], 1.0).then_inc(ones_set, 1)
            nc.vector.memset(epst[:], EPS).then_inc(ones_set, 1)
            dve.wait_ge(vecs_loaded, 32)
            chain = [0]

            def step(ins):
                chain[0] += 1
                ins.then_inc(cum_step, 1)
                dve.wait_ge(cum_step, chain[0])

            lam, y_, ym, s_, s2, q_ = (small[:, 8 * i:8 * i + 8] for i in (10, 4, 11, 12, 13, 14))
            lb_e, t8, t9 = small[:, 40:56], small[:, 120:128], small[:, 128:136]
            step(nc.vector.tensor_scalar(lam, vec("lam", 0, 8), -1.0, None, ALU.mult))
            step(nc.vector.tensor_tensor(y_, lam, vec("lam", 0, 8), ALU.min))
            lb0, lb1 = vec("lb", 0, 8), vec("lb", 8, 8)
            step(nc.vector.tensor_tensor(t8, lb0, lb1, ALU.max))
            step(nc.vector.tensor_tensor(lb_e[:, 0:8], lb0, t8, ALU.subtract))
            nc.vector.tensor_tensor(lb_e[:, 8:16], lb1, t8, ALU.subtract).then_inc(small_done, 1)
            dve.wait_ge(cs_done, 3)
            step(nc.vector.tensor_scalar(ym, y_, 2.0, None, ALU.add))
            step(nc.vector.reciprocal(s_, ym))
            step(nc.vector.tensor_tensor(s_, s_, y_, ALU.mult))
            step(nc.vector.tensor_tensor(s2, s_, s_, ALU.mult))
            step(nc.vector.tensor_scalar(q_, s2, 1.0 / 17, None, ALU.mult))
            for o in (15, 13, 11, 9, 7, 5, 3):
                step(nc.vector.scalar_tensor_tensor(q_, q_, 1.0 / o, s2, ALU.add, ALU.mult))
            step(nc.vector.scalar_tensor_tensor(q_, q_, 1.0, s_, ALU.add, ALU.mult))
            step(nc.vector.tensor_scalar(lam, lam, 0.0, None, ALU.max))
            step(nc.vector.scalar_tensor_tensor(q_, q_, 2.0, lam, ALU.mult, ALU.add))
            step(nc.vector.tensor_scalar(nsp, q_, -8.0, None, ALU.mult))
            step(nc.vector.tensor_scalar(sp, q_, 8.0, None, ALU.mult))
            step(nc.vector.tensor_tensor(t8, lb_e[:, 0:8], lb_e[:, 8:16], ALU.add))
            step(nc.vector.reciprocal(t8, t8))
            step(nc.vector.tensor_tensor(lb_e[:, 0:8], lb_e[:, 0:8], t8, ALU.mult))
            step(nc.vector.tensor_tensor(lb_e[:, 8:16], lb_e[:, 8:16], t8, ALU.mult))
            step(nc.vector.tensor_tensor(t9, lb_e[:, 0:8], lb_e[:, 8:16], ALU.add))
            step(nc.vector.tensor_tensor(t9, t9, lb_e[:, 0:8], ALU.subtract))
            step(nc.vector.tensor_scalar(oml, t9, -1.0, 1.0, ALU.mult, ALU.add))
            step(nc.vector.tensor_scalar(lbt, t9, 1e-18, None, ALU.max))
            nc.vector.tensor_copy(t8, lbt).then_inc(small_done, 1)
            dve.wait_ge(cs_done, 1)
            for k in range(4):
                ada_add(0, k)
            rms_inverse(0, rms_done, rinv_done, diag_done)
            for k in range(4, 8):
                ada_add(0, k)
            for k in range(8):
                ada_add(1, k)
                if k == 3:
                    mod_bias(0)
            dve.wait_ge(mod_ready, 1)
            nc.vector.scalar_tensor_tensor(scale[:, 0:KD], mod("sc1", 0, KD), 1.0, vec("norm0", 0, KD), ALU.add,
                                           ALU.mult).then_inc(cols_ready, 1)
            mod_bias(1)
            lo(0, 0)
            lo(0, 1)
            dve.wait_ge(mod_ready, 2)
            h_split(0)
            for fp in range(2):
                up_step(0, fp, fp, 0, 2)
            with dve.Fori(1, 7) as i:
                for fp in range(2):
                    up_step(0, 2 * i + fp, fp, i, i + 2)
                mod_bias(i + 1)
            for fp in range(2):
                up_step(0, 14 + fp, fp, 7)
            mod_bias(8)
            with dve.Fori(8, KF // 2) as i:
                for fp in range(2):
                    up_step(0, 2 * i + fp, fp, i)
            ffn_down(0)
            rms_inverse(1, rms_done, rinv_done, diag_done)
            h_split(1)

            zi = {u: m for m, u in enumerate(Z_UNITS)}
            nc.vector.memset(rxp[:, :, 0:2], 0.0).then_inc(rxp_zero, 1)
            nc.vector.memset(rxp[:, :, 2 + T:4 + T], 0.0).then_inc(rxp_zero, 1)

            conv = [0]

            def convolve(ct):
                dve.wait_ge(z_evac, ct + 1)
                dve.wait_ge(rxp_zero, 2)
                for j in range(4):
                    tap = vec("conv_w", 4 * j + ct)
                    src = rxp[:, ct, j:j + T]
                    if j == 0:
                        ins = nc.vector.tensor_scalar(xc[:, ct, :], src, tap, vec("conv_b", ct), ALU.mult, ALU.add)
                    else:
                        ins = nc.vector.scalar_tensor_tensor(xc[:, ct, :], src, tap, xc[:, ct, :], ALU.mult, ALU.add)
                    if j < 3:
                        conv[0] += 1
                        ins.then_inc(conv_step, 1)
                        dve.wait_ge(conv_step, conv[0])
                ins.then_inc(xc_ready, 1)

            def one_minus_a2(dr, ct):
                dve.wait_ge(a2_done, RT * dr + ct + 1)
                nc.vector.scalar_tensor_tensor(rt[:, ct, :], a2[:, ct % 2, :], 1.0, rt[:, ct, :], ALU.add,
                                               ALU.mult).then_inc(one_a2, 1)

            rg = [0]

            def recur(dr, ct):
                def rstep(ins):
                    rg[0] += 1
                    ins.then_inc(rg_step, 1)
                    dve.wait_ge(rg_step, rg[0])
                rstep(nc.vector.tensor_tensor(ri[:, ct, :], ri[:, ct, :], xc[:, ct, :], ALU.mult))
                dve.wait_ge(root_done, RT * dr + ct + 1)
                rstep(nc.vector.tensor_tensor(ri[:, ct, :], ri[:, ct, :], rt[:, ct, :], ALU.mult))
                if dr == 0:
                    nc.vector.tensor_tensor_scan(hr[:, ct, :], ra[:, ct, :], ri[:, ct, :], 0.0, ALU.mult,
                                                 ALU.add).then_inc(rg_scanned, 1)
                else:
                    rstep(nc.vector.tensor_tensor_scan(rt[:, ct, ::-1], ra[:, ct, ::-1], ri[:, ct, ::-1], 0.0, ALU.mult,
                                                       ALU.add))
                    nc.vector.tensor_tensor(hr[:, ct, :], hr[:, ct, :], rt[:, ct, :], ALU.add).then_inc(rg_scanned, 1)

            def z_post(m):
                what, i = Z_UNITS[m]
                lo_u(U_MIX + m + 2)
                if what in "fb":
                    lane = "fb".index(what)
                    slot = 2 * lane
                    dve.wait_ge(z_evac, m - 3)
                    if i:
                        dve.wait_ge(cum_ready, 2 * i)
                    v = lg[:, 517 * lane:517 * lane + T]
                    c = 4 * lane + i
                    nc.vector.tensor_scalar(v, w3[:, i % 2, slot, :], oml[:, c:c + 1], lbt[:, c:c + 1], ALU.mult,
                                            ALU.add).then_inc(k_done, 1)
                    dve.wait_ge(k_done, 4 * i + 2 * lane + 1)
                    nc.vector.tensor_scalar(w3[:, i % 2, slot, :], v, -1.0, 1.0, ALU.mult, ALU.add).then_inc(k_done, 1)

            def sum_logs(h):
                p = h % 2
                dve.wait_ge(ln_done, 2 * h + 2)
                if h >= 1:
                    dve.wait_ge(dif_done, 8 * (h - 1) + 1)
                    dve.wait_ge(etot_done, h)
                if h >= 2:
                    dve.wait_ge(dec_done, 9 * (h - 1))
                late = lg[:, 516:516 + T + 1]
                step(nc.vector.tensor_copy(lgend[:], late[:, P:T + 1:P]))
                step(nc.vector.memset(late[:, 0:T:P], 0.0))
                nc.vector.tensor_tensor_scan(cum[:, p, 0, :], resets[:], lg[:, 0:T], 0.0, ALU.mult,
                                             ALU.add).then_inc(cum_ready, 1)
                nc.vector.tensor_tensor_scan(cum[:, p, 1, :], resets[:], late[:, 0:T], 0.0, ALU.mult,
                                             ALU.add).then_inc(cum_ready, 1)
                dve.wait_ge(cum_ready, 2 * h + 2)
                nc.vector.tensor_copy(tot[:, 0, :], cum[:, p, 0, P - 1:T:P]).then_inc(tot_ready, 1)
                nc.vector.tensor_tensor(tot[:, 1, :], cum[:, p, 1, P - 1:T:P], lgend[:], ALU.add).then_inc(tot_ready, 1)

            def decayed(h, e):
                p = h % 2
                if e == 1 and h == 0:
                    dve.wait_ge(one_a2, 2 * RT)
                if e in (0, 1) and h:
                    dve.wait_ge(scored, STEPS * (h - 1) + 10 + e)
                elif e in (2, 3):
                    dve.wait_ge(scored, STEPS * h + 3)
                elif e >= 4:
                    dve.wait_ge(scored, STEPS * h + e)
                if e < 9:
                    dve.wait_ge(dec_done, 9 * h + e + 1)
                if e < 2:
                    if e == 0:
                        dve.wait_ge(k_done, 4 * h + 4)
                    nc.vector.tensor_tensor(qk[:, e], dec[:, e], w3[:, p, 1 - e:3 - e, :], ALU.mult).then_inc(qk_done, 1)
                elif e < 9:
                    hw = LEVELS[e - 2]
                    q5 = qk[:, e % 2].rearrange("p l (n two w) -> p l n two w", two=2, w=hw)
                    d5 = dec[:, e % 2].rearrange("p l (n two w) -> p l n two w", two=2, w=hw)
                    w5 = w3[:, p].rearrange("p l (n two w) -> p l n two w", two=2, w=hw)
                    nc.vector.tensor_tensor(q5[:, :, :, 1, :], d5[:, :, :, 1, :], w5[:, 1:3, :, 1, :], ALU.mult)
                    nc.vector.tensor_tensor(q5[:, ::-1, :, 0, :], d5[:, :, :, 0, :], w5[:, 0:2, :, 0, :],
                                            ALU.mult).then_inc(qk_done, 1)
                else:
                    nc.vector.tensor_tensor(qk[:, 1, 1, :], w3[:, p, 0, :], w3[:, p, 2, :], ALU.add).then_inc(qk_done, 1)

            def decay_far(h):
                dve.wait_ge(qk_done, 10 * h + 2)
                dve.wait_ge(etot_done, h + 1)
                for i, (e, lane, c, by) in enumerate(((0, 0, 3, 2), (1, 0, 0, 1), (1, 1, 0, 1), (0, 1, 3, 2))):
                    ins = nc.vector.tensor_scalar(far[:, i, :], qk[:, e, lane, c * P:(c + 1) * P],
                                                  etot[:, h % 2, lane, by:by + 1], None, ALU.mult)
                ins.then_inc(far_done, 1)

            def mask_in_block(h, s):
                dve.wait_ge(scored, STEPS * h + s + 1)
                if s == 4:
                    dve.wait_ge(blk_copied, 4 * h + 4)
                else:
                    dve.wait_ge(blk_masked, 7 * h + s - 4)
                nc.vector.copy_predicated(pt[:, 0:16:5, :], masks[:, s - 4:s - 3, :].broadcast_to([P, TC, P]),
                                          bank[4 + (STEPS * h + s) % 2].rearrange("p (b t) -> p b t", b=TC)
                                          ).then_inc(blk_masked, 1)

            def o_norm(h):
                dve.wait_ge(orb_done, h + 1)
                dve.wait_ge(osb_done, h + 1)
                nc.vector.scalar_tensor_tensor(on[:, h, :], osb, vec("hg_norm"), rb, ALU.mult,
                                               ALU.mult).then_inc(on_step, 1)
                dve.wait_ge(on_step, h + 1)
                nc.vector.tensor_tensor(on[:, h, :], on[:, h, :], sg[:, h, :], ALU.mult).then_inc(on_done, 1)

            def y_lower(k):
                dve.wait_ge(yhi_done, k + 1)
                src = hr[:, k, :] if k < RT else on[:, k - RT, :]
                nc.vector.tensor_tensor(ylo[:, k, :], src, yhi[:, k, :], ALU.subtract).then_inc(y_ready, 1)

            for m in range(4):
                z_post(m)
            for m in range(4, 8):
                z_post(m)
                convolve(m - 4)
            z_post(8)
            z_post(9)
            dve.wait_ge(mix_loaded, 48)
            nc.vector.tensor_copy(masks[:].rearrange("p a t -> p (a t)"), mask_f).then_inc(masks_set, 1)
            for ct in range(RT):
                one_minus_a2(0, ct)
            z_post(10)
            for ct in range(2):
                recur(0, ct)
            z_post(11)
            for ct in range(2, 4):
                recur(0, ct)
            z_post(12)
            sum_logs(0)
            for ct in range(RT):
                one_minus_a2(1, ct)
            for r in range(HEADS):
                first = zi[("q", r + 1)] if r < 3 else None
                gaps = 10 if r < 3 else 6
                decayed(r, 0)
                decayed(r, 1)
                decay_far(r)
                s = 0
                for g in range(gaps):
                    for _ in range(2 if (r == 3 and g < 5) or (r < 3 and g == 0) else 1):
                        if 3 <= s:
                            decayed(r, s - 1)
                        if s >= 5:
                            mask_in_block(r, s - 1)
                        s += 1
                    if g == 4 and r:
                        rms_inverse(r - 1, orms_done, orinv_done, odiag_done)
                    if g == (4 if r == 3 else 6) and r:
                        o_norm(r - 1)
                    if g % 2 and r < 3:
                        z_post(first + g // 2)
                        if g // 2 == 2:
                            sum_logs(r + 1)
                    if r == 0 and g in (2, 4, 6, 8):
                        recur(1, g // 2 - 1)
                    if r == 3:
                        if g == 0:
                            for k in range(RT):
                                dve.wait_ge(z_evac, N_Z - 4)
                                dve.wait_ge(rg_scanned, RT + k + 1)
                                nc.vector.tensor_tensor(hr[:, k, :], hr[:, k, :], gg[:, k, :],
                                                        ALU.mult).then_inc(yrg_done, 1)
                            for k in range(RT):
                                y_lower(k)
                        if g % 2:
                            lo_u(U_OUT + g // 2 + 2)
                        if g == 2:
                            y_lower(4)
                            y_lower(5)
                        if g == 5:
                            y_lower(6)
                mask_in_block(r, STEPS - 1)
            rms_inverse(3, orms_done, orinv_done, odiag_done)
            o_norm(3)
            y_lower(7)
            columns(1)
            dve.wait_ge(cols_ready, 5)
            for m in range(3, 8):
                lo_u(U_OUT + m + 2)
                if m == 4:
                    for d in range(4):
                        update(1, d, bank[d])
            for d in range(4, KD):
                update(1, d, bank[d])
            rms_inverse(2, rms_done, rinv_done, diag_done)
            h_split(2)
            for fp in range(2):
                up_step(1, fp, fp, 0)
            with dve.Fori(1, KF // 2) as i:
                for fp in range(2):
                    up_step(1, 2 * i + fp, fp, i)
            ffn_down(1)
            rms_inverse(3, rms_done, rinv_done, diag_done)
            dve.wait_ge(rb_done, 4)
            for d in range(KD):
                nc.vector.scalar_tensor_tensor(outt[:, d, :], x[:, d, :], vec("norm3", d), rb, ALU.mult,
                                               ALU.mult).then_inc(out_ready, 1)

        @block.tensor
        def _(pe):
            def three(dst, slot, col, rhi, rlo, start, stop):
                a, b = whi[:, slot, col:col + P], wlo[:, slot, col:col + P]
                nc.tensor.matmul(dst, a, rhi, start=start, stop=False)
                nc.tensor.matmul(dst, a, rlo, start=False, stop=False)
                return nc.tensor.matmul(dst, b, rhi, start=False, stop=stop)

            def up_step(n, f, fp, i):
                j = (U_FFN1, U_FFN2)[n] // 2 + 2 * i + fp
                first = isinstance(f, int) and f == 0
                for s in range(2):
                    pe.wait_ge(lo_done, 2 * j + (s + 1))
                    if not (isinstance(f, int) and f < 2) or n:
                        pe.wait_ge((silu_done, gate_prod)[s], f + (KF * n - 1))
                    for k in range(KD):
                        if first and s == 0:
                            pe.wait_ge(hlo_done, KD * (0, 2)[n] + k + 1)
                        ins = three(bank[2 * s + fp], s, k * P, hhi[:, k, :], hlo[:, k, :], k == 0, k == KD - 1)
                    ins.then_inc(unit_used, 1)

            def mod_sum(j):
                pe.wait_ge(ada_added, 8 * j + 8)
                if not (isinstance(j, int) and j == 0):
                    pe.wait_ge(mod_ready, 1 * j)
                for t in range(KD):
                    ins = nc.tensor.matmul(modp[:, t:t + 1], fin[:, t * P:(t + 1) * P], ones[:, 0:1], start=True,
                                           stop=True)
                ins.then_inc(mod_summed, 1)

            def down_unit(half, slot, rhs, first, last, wait_for):
                wait_for()
                for t in range(2):
                    rhi, rlo = rhs(t)
                    for d in range(4):
                        ins = three(bank[(4, 0)[half] + d], slot, (4 * t + d) * P, rhi, rlo, first and t == 0,
                                    last and t == 1)
                ins.then_inc(unit_used, 1)

            def ffn_down(n):
                u0 = (U_FFN1, U_FFN2)[n] + 2 * KF
                for half in range(2):
                    u = u0 + HALF_UNITS * half

                    def rhs_of(k):
                        return lambda t: tuple(g[:, bass.ds(k + t, 1), :].rearrange("p a t -> p (a t)")
                                               for g in (ghi, glo))

                    def wait_for(u=u, half=half):
                        pe.wait_ge(lo_done, u + 1)
                        if half == 0:
                            pe.wait_ge(glo_done, KF * n + 2)
                            pe.wait_ge(mod_ready, N_MOD)
                        else:
                            pe.wait_ge(glo_done, KF * n + KF)

                    down_unit(half, u % 2, rhs_of(0), True, False, wait_for)
                    with pe.Fori(0, (HALF_UNITS - 1) // 2 - 1) as i:
                        for s in range(2):
                            v = u + 1 + s

                            def wait_in(v=v, s=s, half=half):
                                pe.wait_ge(lo_done, 2 * i + (v + 1))
                                if half == 0:
                                    pe.wait_ge(glo_done, 4 * i + (KF * n + 4 + 2 * s))
                            down_unit(half, v % 2, rhs_of(4 * i + (2 + 2 * s)), False, False, wait_in)
                    for s in range(2):
                        v = u + HALF_UNITS - 2 + s

                        def wait_last(v=v, s=s, half=half):
                            pe.wait_ge(lo_done, v + 1)
                            if half == 0:
                                pe.wait_ge(glo_done, KF * n + KF - 2 + 2 * s)
                        down_unit(half, v % 2, rhs_of(KF - 4 + 2 * s), False, s == 1, wait_last)

            def norm(n):
                for d in range(KD):
                    pe.wait_ge(sq_done, KD * n + d + 1)
                    if d == 0 and n == 0:
                        pe.wait_ge(ones_set, 2)
                    if d == 0 and n:
                        pe.wait_ge(x_ready, KD * (n - 1) + 4)
                        if n == 2:
                            pe.wait_ge(x_ready, KD * n)
                    for c in range(TC):
                        ins = nc.tensor.matmul(sums[:, c:c + 1], sq[:, d % 4, c * P:(c + 1) * P], ones[:, 0:1],
                                               start=(d == 0 and c == 0), stop=(d == KD - 1), skip_group_check=True)
                    ins.then_inc(sq_used, 1)
                pe.wait_ge(diag_done, n + 1)
                nc.tensor.matmul(rb, ones[:], diag[:].rearrange("p c t -> p (c t)"), start=True,
                                 stop=True).then_inc(rb_done, 1)

            norm(0)
            mod_sum(0)
            mod_sum(1)
            for fp in range(2):
                up_step(0, fp, fp, 0)
            with pe.Fori(1, 8) as i:
                up_step(0, 2 * i, 0, i)
                mod_sum(i + 1)
                up_step(0, 2 * i + 1, 1, i)
            with pe.Fori(8, KF // 2) as i:
                for fp in range(2):
                    up_step(0, 2 * i + fp, fp, i)
            ffn_down(0)
            norm(1)

            zi = {u: m for m, u in enumerate(Z_UNITS)}

            def z_half(m, part):
                u = U_MIX + m
                what, i = Z_UNITS[m]
                if part == 0:
                    pe.wait_ge(lo_done, u + 1)
                if what == "v":
                    k = 2 * i + part
                    if i == 0:
                        pe.wait_ge(hlo_done, KD + k + 1)
                    elif part == 0:
                        pe.wait_ge(hlo_done, KD + 2 * i + 2)
                    a, b = (w[:, u % 2, part * T:(part + 1) * T] for w in (whi, wlo))
                    for c in range(TC):
                        dst, cc = bank[2 + c], slice(c * P, (c + 1) * P)
                        nc.tensor.matmul(dst, hhi[:, k, cc], a, start=(k == 0), stop=False)
                        nc.tensor.matmul(dst, hhi[:, k, cc], b, start=False, stop=False)
                        ins = nc.tensor.matmul(dst, hlo[:, k, cc], a, start=False, stop=(k == KD - 1))
                else:
                    if part == 0 and m >= 6:
                        pe.wait_ge(z_evac, m - 5)
                    for k in range(4 * part, 4 * part + 4):
                        ins = three(bank[m % 2], u % 2, k * P, hhi[:, k, :], hlo[:, k, :], k == 0, k == KD - 1)
                if part == 1:
                    ins.then_inc(unit_used, 1)

            def z_unit(m):
                z_half(m, 0)
                z_half(m, 1)

            def gate_sums(dr, ct):
                gi = RT * dr + ct
                pe.wait_ge(xc_ready, ct + 1)
                pe.wait_ge(mix_loaded, 48)
                if gi:
                    pe.wait_ge(gate_evac, 2 * gi)
                else:
                    pe.wait_ge(v_copied, 2)
                for w in range(2):
                    ins = nc.tensor.matmul(bank[2 + w], bd[:, 2 * dr + w, ct, :], xc[:, ct, :], start=True, stop=True)
                ins.then_inc(gates_summed, 1)

            def scores(h, s):
                before = step_before(h, s, 2)
                if before is None:
                    pe.wait_ge(v_copied, TC)
                else:
                    evac_wait(pe, *before)
                dst = bank[4 + (STEPS * h + s) % 2]
                QF, KB, KF_, QB = qk[:, 0, 0, :], qk[:, 0, 1, :], qk[:, 1, 0, :], qk[:, 1, 1, :]

                def c(a, i):
                    return a[:, i * P:(i + 1) * P]
                if s == 0:
                    pe.wait_ge(qk_done, 10 * h + 2)
                    pairs = [(c(KF_, 0), c(QF, 1)), (c(KB, 1), c(QB, 0)), (c(KF_, 2), c(QF, 3)), (c(KB, 3), c(QB, 2))]
                elif s == 1:
                    pe.wait_ge(far_done, h + 1)
                    pairs = [(k, q) for k in (far[:, 1, :], c(KF_, 1)) for q in (c(QF, 2), far[:, 0, :])]
                elif s == 2:
                    pairs = [(k, q) for k in (c(KB, 2), far[:, 3, :]) for q in (far[:, 2, :], c(QB, 1))]
                else:
                    pe.wait_ge(qk_done, 10 * h + s)
                    e = s - 1
                    q = qk[:, e % 2, 0, :] if s < STEPS - 1 else w3[:, h % 2, 1, :]
                    pairs = [(c(qk[:, e % 2, 1, :], i), c(q, i)) for i in range(TC)]
                for i, (k, q) in enumerate(pairs):
                    ins = nc.tensor.matmul(dst[:, i * P:(i + 1) * P], k, q, start=True, stop=True)
                ins.then_inc(scored, 1)

            def pv(h):
                pe.wait_ge(blk_copied, 4 * h + 4)
                pe.wait_ge(blk_masked, 7 * h + 7)
                if h:
                    pe.wait_ge(osb_done, h)
                    pe.wait_ge(osq_done, h)
                for c in range(TC):
                    ins = nc.tensor.matmul(bank[6], vn[:, c, h * P:(h + 1) * P],
                                           pt[:, 4 * c:4 * c + 4, :].rearrange("p b t -> p (b t)"), start=(c == 0),
                                           stop=(c == TC - 1))
                ins.then_inc(pv_done, 1)

            def o_sums(h):
                pe.wait_ge(osq_done, h + 1)
                if h:
                    pe.wait_ge(on_done, h)
                for c in range(TC):
                    ins = nc.tensor.matmul(psum[:, 7, c:c + 1], osq[:, c * P:(c + 1) * P], ones[:, 0:1], start=True,
                                           stop=True)
                ins.then_inc(osum_done, 1)

            def o_rb(h):
                pe.wait_ge(odiag_done, h + 1)
                nc.tensor.matmul(rb, ones[:], diag[:].rearrange("p c t -> p (c t)"), start=True,
                                 stop=True).then_inc(orb_done, 1)

            def out_half(m, part):
                half, kk = m // 4, m % 4
                u = U_OUT + m
                if part == 0:
                    pe.wait_ge(lo_done, u + 1)
                    if m == 0:
                        pe.wait_ge(z_evac, N_Z - 4)
                        pe.wait_ge(gate_evac, 16)
                    if m == 4:
                        pe.wait_ge(on_done, HEADS)
                k = 2 * kk + part
                if half == 0:
                    pe.wait_ge(y_ready, k + 1)
                for d in range(4):
                    ins = three(bank[4 * half + d], u % 2, (4 * part + d) * P, yhi[:, k, :], ylo[:, k, :], k == 0,
                                k == KD - 1)
                if part == 1:
                    ins.then_inc(unit_used, 1)

            for m in range(9):
                z_unit(m)
            gate_sums(0, 0)
            gate_sums(0, 1)
            z_unit(9)
            gate_sums(0, 2)
            gate_sums(0, 3)
            for m in range(10, 13):
                z_unit(m)
            for ct in range(RT):
                gate_sums(1, ct)
            for r in range(HEADS):
                first = zi[("q", r + 1)] if r < 3 else None
                gaps = 10 if r < 3 else 6
                s = 0
                for g in range(gaps):
                    if r < 3:
                        z_half(first + g // 2, g % 2)
                    else:
                        out_half(g // 2, g % 2)
                    for _ in range(2 if (r == 3 and g < 5) or (r < 3 and g == 0) else 1):
                        scores(r, s)
                        s += 1
                    if g == 2 and r:
                        o_sums(r - 1)
                    if g == (4 if r == 3 else 5) and r:
                        o_rb(r - 1)
                pv(r)
            o_sums(3)
            o_rb(3)
            for m in range(3, 8):
                out_half(m, 0)
                out_half(m, 1)
            norm(2)
            for fp in range(2):
                up_step(1, fp, fp, 0)
            with pe.Fori(1, KF // 2) as i:
                for fp in range(2):
                    up_step(1, 2 * i + fp, fp, i)
            ffn_down(1)
            norm(3)


def _down_units(w):
    n = w.shape[0] // 256
    return w.reshape(n, 2, P, 2, 4, P).transpose(3, 0, 2, 1, 4, 5).reshape(2 * n, P, UNIT)


def _col_units(w):
    n = w.shape[1] // P
    return w.reshape(KD, P, n, P).transpose(2, 1, 0, 3).reshape(n, P, UNIT)


def _cols(v):
    return np.ascontiguousarray(v).reshape(-1, P).T


def layout(inputs):
    i = {k: np.asarray(v) for k, v in inputs.items()}
    units = []

    def ffn(w1, w3, w2):
        units.append(np.stack([_col_units(w1), _col_units(w3)], axis=1).reshape(2 * KF, P, UNIT))
        units.append(_down_units(w2))

    ffn(i["ffn1_w1"][0], i["ffn1_w3"][0], i["ffn1_w2"][0])
    w_in = i["w_in"][0]
    v = w_in[:, Z_COLUMN["v"]:Z_COLUMN["v"] + T].reshape(4, 2, P, T).transpose(0, 2, 1, 3).reshape(4, P, UNIT)
    z = _col_units(w_in)
    units.append(np.stack([v[t] if what == "v" else z[Z_COLUMN[what] // P + t] for what, t in Z_UNITS]))
    w_out = i["w_out"][0]
    units.append(_down_units(np.concatenate([w_out[T:], w_out[:T]])))
    ffn(i["ffn2_w1"][0], i["ffn2_w3"][0], i["ffn2_w2"][0])
    order = [MOD_AT[m] for m in MODS]
    wada = i["w_ada"][0].reshape(KD, P, N_MOD, D).transpose(2, 0, 1, 3)[order].reshape(N_MOD * KD, P, D)
    vecs = [_cols(i["c"][0]), _cols(i["b_ada"][0].reshape(N_MOD, D)[order].reshape(-1)),
            _cols(i["ffn1_norm"][0]), _cols(i["mix_norm"][0]), _cols(i["ffn2_norm"][0]), _cols(i["final_norm"]),
            _cols(i["hg_lb_fwd"][0]), _cols(i["hg_lb_bwd"][0]), _cols(i["hg_lb_fwd"][1]), _cols(i["hg_lb_bwd"][1]),
            _cols(i["hg_out_norm"][0]), _cols(i["rg_conv_w"][0].reshape(-1)), _cols(i["rg_conv_b"][0])]
    for a, b in (("rg_ba_fwd", "rg_ba_bwd"), ("rg_bx_fwd", "rg_bx_bwd"), ("rg_lam_fwd", "rg_lam_bwd")):
        vecs += [_cols(i[a][0]), _cols(i[b][0])]
    bd = np.zeros((P, 4, RT, P), np.float32)
    for w, name in enumerate(("rg_wa_fwd", "rg_wx_fwd", "rg_wa_bwd", "rg_wx_bwd")):
        for n in range(8):
            o = 64 * (n % 2)
            bd[o:o + 64, w, n // 2, o:o + 64] = i[name][0, n]
    xor = np.arange(P)[:, None] ^ np.arange(P)[None, :]
    mask = np.stack([xor < w for w in (64, 32, 16, 8, 4, 2, 1)], axis=1).astype(np.float32)
    resets = np.ones((P, T), np.float32)
    resets[:, ::P] = 0.0
    return {
        "xt": np.ascontiguousarray(i["x"][0].T), "wu": np.ascontiguousarray(np.concatenate(units)),
        "wada": np.ascontiguousarray(wada), "vecs": np.ascontiguousarray(np.concatenate(vecs, axis=1)),
        "bd": bd, "consts": np.concatenate([np.eye(P, dtype=np.float32), resets, mask.reshape(P, 7 * P)], axis=1),
    }


def kernel(**inputs):
    import concourse.bacc as bacc
    from concourse.bass_utils import run_bass_kernel_spmd

    nc = bacc.Bacc("TRN2", target_bir_lowering=False, num_devices=1)
    arrays = layout(inputs)
    aps = [nc.dram_tensor(n, a.shape, mybir.dt.from_np(a.dtype), kind="ExternalInput").ap() for n, a in arrays.items()]
    out = nc.dram_tensor("out", (D, T), F32, kind="ExternalOutput").ap()
    build(nc, *aps, out)
    r = run_bass_kernel_spmd(nc, [arrays], core_ids=[0])
    return np.ascontiguousarray(r.results[0]["out"].T)[None]
```

```python
from contextlib import ExitStack

import numpy as np
import concourse.bass as bass
from concourse import mybir

F32 = mybir.dt.float32
F32R = mybir.dt.float32r
U8 = mybir.dt.uint8
ALU = mybir.AluOpType
ACT = mybir.ActivationFunctionType

P = 128
T = 512
D = 1024
FF = 2816
KD = D // P
KF = FF // P
TC = T // P
HEADS = 4
RT = 4
N_MOD = 9
EPS = 1e-6
UNIT = KD * P
HALF_UNITS = KF // 2
LEVELS = (64, 32, 16, 8, 4, 2, 1)

U_FFN1 = 0
U_MIX = U_FFN1 + 3 * KF
N_Z = 28
U_OUT = U_MIX + N_Z
U_FFN2 = U_OUT + 8
N_UNITS = U_FFN2 + 3 * KF
Z_UNITS = ([("v", i) for i in range(4)] + [("rx", i) for i in range(4)]
           + [(w, 0) for w in "qfb"] + [("g", 0), ("g", 1)] + [(w, 1) for w in "qfb"] + [("g", 2), ("g", 3)]
           + [(w, 2) for w in "qfb"] + [("gate", 0), ("gate", 1)]
           + [(w, 3) for w in "qfb"] + [("gate", 2), ("gate", 3)])
Z_COLUMN = {"q": 0, "f": 512, "b": 1024, "v": 1536, "g": 2048, "rx": 2560, "gate": 3072}
MODS = ("sc1", "sh1", "g1", "sh2", "sc2", "g2", "sh3", "sc3", "g3")
MOD_AT = {"sh1": 0, "sc1": 1, "g1": 2, "sh2": 3, "sc2": 4, "g2": 5, "sh3": 6, "sc3": 7, "g3": 8}
VEC = {}
_at = 0
for _name, _n in (("c", 8), ("b_ada", 72), ("norm0", 8), ("norm1", 8), ("norm2", 8), ("norm3", 8),
                  ("lb", 16), ("hg_norm", 1), ("conv_w", 16), ("conv_b", 4), ("ba", 8), ("bx", 8), ("lam", 8)):
    VEC[_name] = _at
    _at += _n
N_VEC = _at


def build(nc, xt, wu, wada, vecs_in, bd_in, consts_in, out):
    with ExitStack() as ctx:
        place = [nc.sbuf_base + (-nc.sbuf_base) % 64]

        def at(name, shape, dt, offset):
            n = int(np.prod(shape[1:])) * (1 if dt == U8 else 4)
            return nc.alloc_sbuf_tensor_at(name, shape, dt, offset=offset), offset + (n + 63) // 64 * 64

        def sb(name, shape, dt=F32):
            t, place[0] = at(name, shape, dt, place[0])
            return t

        def sem(name):
            return ctx.enter_context(nc.semaphore(name))

        x = sb("x", [P, KD, T])
        h_at = place[0]
        hhi = sb("hhi", [P, KD, T], F32R)
        hlo = sb("hlo", [P, KD, T], F32R)
        raw = sb("raw", [P, 2, UNIT])
        whi = sb("whi", [P, 2, UNIT], F32R)
        wlo = sb("wlo", [P, 2, UNIT], F32R)
        vecs = sb("vecs", [P, N_VEC])
        ident = sb("ident", [P, P])
        ones = sb("ones", [P, P])
        epst = sb("epst", [P, 1])
        cs = sb("cs", [P, KD])
        mods = sb("mods", [P, N_MOD * KD])
        scale = sb("scale", [P, 3 * KD])
        gates = sb("gates", [P, 3 * KD])
        rms = sb("rms", [P, TC])
        rinv = sb("rinv", [P, TC])
        diag = sb("diag", [P, TC, P])
        tmp = sb("tmp", [P, 2, T])
        small = sb("small", [P, 136])
        sp4, nsp4 = small[:, 0:8], small[:, 8:16]
        lbm, omh = small[:, 16:24], small[:, 24:32]
        half_b, half_gain = small[:, 56:72], small[:, 72:73]
        arena = place[0]
        off = arena
        ghi, off = at("ghi", [P, KF, T], F32R, off)
        glo, off = at("glo", [P, KF, T], F32R, off)
        sq, off = at("sq", [P, 4, T], F32, off)
        silu_sb, off = at("silu_sb", [P, T], F32, off)
        g32, off = at("g32", [P, T], F32, off)
        ada, off = at("ada", [P, 4, D], F32, off)
        acc, off = at("acc", [P, D], F32, off)
        fin, off = at("fin", [P, D], F32, off)
        outt, _ = at("outt", [P, KD, T], F32, arena)
        yhi, _ = at("yhi", [P, KD, T], F32R, h_at)
        ylo, _ = at("ylo", [P, KD, T], F32R, h_at + KD * T * 4)
        off = arena
        vn, off = at("vn", [P, TC, T], F32, off)
        pt, off = at("pt", [P, TC * TC, P], F32, off)
        w3, off = at("w3", [P, 2, 3, T], F32, off)
        cum, off = at("cum", [P, 2, 2, T], F32, off)
        dif, off = at("dif", [P, 2, 2, T], F32, off)
        dec, off = at("dec", [P, 2, 2, T], F32, off)
        qk, off = at("qk", [P, 2, 2, T], F32, off)
        lg, off = at("lg", [P, 2 * 517], F32, off)
        far, off = at("far", [P, 4, P], F32, off)
        tot, off = at("tot", [P, 2, TC], F32, off)
        etot, off = at("etot", [P, 2, 2, TC], F32, off)
        lgend, off = at("lgend", [P, TC], F32, off)
        masks, off = at("masks", [P, 7, P], U8, off)
        resets, off = at("resets", [P, T], F32, off)
        osb, osq = tmp[:, 0, :], tmp[:, 1, :]
        sg, off = at("sg", [P, HEADS, T], F32, off)
        xc, off = at("xc", [P, RT, T], F32, off)
        rxp, off = at("rxp", [P, RT, T + 4], F32, off)
        hr, _ = at("hr", [P, RT, T], F32, off - RT * (T + 4) * 4)
        gg, _ = at("gg", [P, RT, T], F32, off)
        ra, off = at("ra", [P, RT, T], F32, off)
        on, _ = at("on", [P, HEADS, T], F32, off)
        rt, off = at("rt", [P, RT, T], F32, off)
        ri, off = at("ri", [P, RT, T], F32, off)
        mask_f = dif[:].rearrange("p a l t -> p (a l t)")[:, 0:7 * P]
        a2 = tmp
        bd, off = at("bd", [P, 4, RT, P], F32, off)

        psum = ctx.enter_context(nc.psum_tensor("psum", [P, 8, T], F32))
        bank = [psum[:, b, :] for b in range(8)]
        modp = psum[:, 5, 0:8]

        def sums(n):
            return bank[(6, 6, 0, 6, 7)[n]][:, 0:TC]

        def rb(n):
            return bank[(7, 7, 1, 7, 7)[n]]

        vecs_loaded, x_loaded, mix_loaded = sem("vecs_loaded"), sem("x_loaded"), sem("mix_loaded")
        ada_first = [sem(f"ada_first{i}") for i in range(4)]
        ada_loaded = [sem(f"ada_loaded{i}") for i in range(4)]
        raw_loaded = [sem(f"raw_loaded{i}") for i in range(2)]
        hi_done, lo_done, unit_used = sem("hi_done"), sem("lo_done"), sem("unit_used")
        ones_set, cs_done, small_done = sem("ones_set"), sem("cs_done"), sem("small_done")
        ada_added, mod_summed, mod_ready = sem("ada_added"), sem("mod_summed"), sem("mod_ready")
        cols_ready = sem("cols_ready")
        sq_done, sq_added, sq_used, rms_done, rinv_done = sem("sq_done"), sem("sq_added"), sem("sq_used"), sem("rms_done"), sem("rinv_done")
        diag_done, rb_done, htmp_done = sem("diag_done"), sem("rb_done"), sem("htmp_done")
        hhi_done, hlo_done = sem("hhi_done"), sem("hlo_done")
        tile_done, zq_done, gelu_done = sem("tile_done"), sem("zq_done"), sem("gelu_done")
        silu_done, gate_prod, ghi_done, glo_done = sem("silu_done"), sem("gate_prod"), sem("ghi_done"), sem("glo_done")
        x_ready, out_ready, stored = sem("x_ready"), sem("out_ready"), sem("stored")
        masks_set = sem("masks_set")
        v_copied, z_evac, rxp_zero = sem("v_copied"), sem("z_evac"), sem("rxp_zero")
        conv_step, xc_ready = sem("conv_step"), sem("xc_ready")
        gates_summed, gate_evac, tanh_done, a_done = sem("gates_summed"), sem("gate_evac"), sem("tanh_done"), sem("a_done")
        a2_done, one_a2, root_done = sem("a2_done"), sem("one_a2"), sem("root_done")
        rg_step, rg_scanned = sem("rg_step"), sem("rg_scanned")
        k_done, ln_done = sem("k_done"), sem("ln_done")
        cum_step, cum_ready, tot_ready, etot_done = sem("cum_step"), sem("cum_ready"), sem("tot_ready"), sem("etot_done")
        dif_done, dec_done, qk_done, far_done = sem("dif_done"), sem("dec_done"), sem("qk_done"), sem("far_done")
        scored, blk_copied, blk_masked = sem("scored"), sem("blk_copied"), sem("blk_masked")
        pv_done, osb_done, osq_done, osum_done = sem("pv_done"), sem("osb_done"), sem("osq_done"), sem("osum_done")
        orms_done, orinv_done, odiag_done, orb_done = sem("orms_done"), sem("orinv_done"), sem("odiag_done"), sem("orb_done")
        on_step, on_done, yrg_done, yhi_done, y_ready = (sem("on_step"), sem("on_done"), sem("yrg_done"),
                                                         sem("yhi_done"), sem("y_ready"))

        def vec(name, i=0, n=1):
            return vecs[:, VEC[name] + i:VEC[name] + i + n]

        def mod(name, i=0, n=1):
            m = MODS.index(name) * KD + i
            return mods[:, m:m + n]

        SHIFT = ("sh1", "sh2", "sh3")
        STEPS = 4 + len(LEVELS)
        STEPS_AT = ([[0], [1, 2]] + [[g + 1] for g in range(2, 10)],
                    [[0], [1, 2], [3, 4], [5, 6], [7, 8], [9, 10]])

        QG_COUNT = {z: 1 + sum(w in "qg" for w, _ in Z_UNITS[:m]) for m, z in enumerate(Z_UNITS) if z[0] in "qg"}

        def evac_wait(eng, h, s):
            if s < 4:
                eng.wait_ge(blk_copied, 4 * h + s + 1)
            else:
                eng.wait_ge(blk_masked, (STEPS - 4) * h + s - 3)

        def step_before(h, s, n):
            g = STEPS * h + s - n
            return (g // STEPS, g % STEPS) if g >= 0 else None

        block = ctx.enter_context(nc.Block())

        @block.sync
        def _(sp_):
            sp_.dma_start(vecs[:], vecs_in).then_inc(vecs_loaded, 16)
            sp_.dma_start(ident[:], consts_in[:, 0:P]).then_inc(vecs_loaded, 16)
            for k in range(4):
                sp_.dma_start(ada[:, k, :], wada[k]).then_inc(ada_first[k], 16)
            for i in range(2):
                n = KD // 2
                sp_.dma_start(x[:, n * i:n * i + n, :], xt[T * i:T * i + T].rearrange("(d p) t -> p d t", p=P)
                              ).then_inc(x_loaded, 16)
            for k in range(4, 16):
                sp_.wait_ge(ada_added, k - 3)
                sp_.dma_start(ada[:, k % 4, :], wada[k]).then_inc(ada_first[k % 4], 16)
            for u in range(2):
                sp_.dma_start(raw[:, u, :], wu[u]).then_inc(raw_loaded[u], 16)
            with sp_.Fori(1, N_UNITS // 2) as j:
                for s in range(2):
                    sp_.wait_ge(lo_done, 2 * j + (s - 1))
                    sp_.dma_start(raw[:, s, :], wu[bass.ds(2 * j + s, 1)].rearrange("a p n -> p (a n)")
                                  ).then_inc(raw_loaded[s], 16)
            for d in range(KD):
                sp_.wait_ge(out_ready, d + 1)
                sp_.dma_start(out[d * P:(d + 1) * P, :], outt[:, d, :]).then_inc(stored, 16)
            sp_.wait_ge(stored, 16 * KD)

        @block.gpsimd
        def _(pool):
            def add_squares(n, part):
                if part == 0:
                    pool.wait_ge(sq_done, KD * n + 4)
                    nc.gpsimd.tensor_tensor(sq[:, 0:2, :], sq[:, 0:2, :], sq[:, 2:4, :], ALU.add).then_inc(sq_added, 1)
                    pool.wait_ge(sq_added, 3 * n + 1)
                else:
                    pool.wait_ge(sq_done, KD * n + 6)
                nc.gpsimd.tensor_tensor(sq[:, 0, :], sq[:, 0, :], sq[:, 1, :], ALU.add).then_inc(sq_added, 1)

            add_squares(0, 0)
            add_squares(0, 1)
            with pool.Fori(2, N_MOD) as j:
                for k in range(8):
                    pool.wait_ge(ada_added, 8 * j + (k - 3))
                    pool.dma_start(ada[:, k % 4, :], wada[bass.ds(8 * j + k, 1)].rearrange("a p n -> p (a n)")
                                   ).then_inc(ada_loaded[k % 4], 16)
            add_squares(1, 0)
            add_squares(1, 1)
            pool.wait_ge(unit_used, U_MIX)
            pool.wait_ge(sq_used, 4 * 2)
            pool.dma_start(bd[:], bd_in).then_inc(mix_loaded, 16)
            pool.dma_start(mask_f, consts_in[:, P + T:P + T + 7 * P]).then_inc(mix_loaded, 16)
            pool.dma_start(resets[:], consts_in[:, P:P + T]).then_inc(mix_loaded, 16)
            pool.wait_ge(masks_set, 1)
            for h in range(HEADS):
                p = h % 2
                pool.wait_ge(tot_ready, 2 * (h + 1))
                if h:
                    pool.wait_ge(dec_done, 9 * h)
                nc.gpsimd.tensor_tensor(dif[:, 1].rearrange("p l (c t) -> p l c t", c=TC),
                                        tot[:].unsqueeze(3).broadcast_to([P, 2, TC, P]),
                                        cum[:, p].rearrange("p l (c t) -> p l c t", c=TC),
                                        ALU.subtract).then_inc(dif_done, 1)
                for i, hw in enumerate(LEVELS):
                    e = i + 2
                    if e > 2:
                        pool.wait_ge(dec_done, 9 * h + e - 1)
                    c5 = cum[:, p].rearrange("p l (n two w) -> p l n two w", two=2, w=hw)
                    d5 = dif[:, e % 2].rearrange("p l (n two w) -> p l n two w", two=2, w=hw)
                    ref = c5[:, :, :, 1, 0:1].broadcast_to([P, 2, T // (2 * hw), hw])
                    nc.gpsimd.tensor_tensor(d5[:, :, :, 1, :], c5[:, :, :, 1, :], ref, ALU.subtract)
                    nc.gpsimd.tensor_tensor(d5[:, :, :, 0, :], ref, c5[:, :, :, 0, :],
                                            ALU.subtract).then_inc(dif_done, 1)
            for n in (2, 3):
                add_squares(n, 0)
                add_squares(n, 1)

        @block.scalar
        def _(act):
            def hi(j, slot):
                act.wait_ge(raw_loaded[slot], 16 * (j + 1))
                if not (isinstance(j, int) and j == 0):
                    act.wait_ge(unit_used, 2 * j + (slot - 1))
                nc.scalar.activation(whi[:, slot, :], raw[:, slot, :], ACT.Copy).then_inc(hi_done, 1)

            def hi_u(u):
                if u < N_UNITS:
                    hi(u // 2, u % 2)

            def square(n, d):
                if n == 0:
                    act.wait_ge(x_loaded, 16 * 2)
                else:
                    act.wait_ge(x_ready, KD * (n - 1) + d + 1)
                if d >= 4:
                    act.wait_ge(sq_used, 4 * n + 1)
                elif n:
                    act.wait_ge(sq_used, 4 * n)
                nc.scalar.activation(sq[:, d % 4, :], x[:, d, :], ACT.Square).then_inc(sq_done, 1)

            def root(n):
                act.wait_ge(sq_used, 4 * (n + 1))
                nc.scalar.activation(rms[:], sums(n), ACT.Sqrt, bias=epst[:], scale=1.0 / D).then_inc(rms_done, 1)

            def h_upper(n):
                if n == 0:
                    act.wait_ge(mod_ready, 2)
                for d in range(KD):
                    act.wait_ge(htmp_done, KD * n + d + 1)
                    nc.scalar.activation(hhi[:, d, :], tmp[:, d % 2, :], ACT.Identity,
                                         bias=mod(SHIFT[n], d)).then_inc(hhi_done, 1)

            def up_step(n, f, fp, i):
                j = (U_FFN1, U_FFN2)[n] // 2 + 2 * i + fp
                hi(j + 1, 0)
                act.wait_ge(unit_used, 2 * j + 1)
                if not (isinstance(f, int) and KF * n + f == 0):
                    act.wait_ge(gate_prod, f + KF * n)
                nc.scalar.activation(silu_sb[:], bank[fp], ACT.Silu).then_inc(silu_done, 1)
                hi(j + 1, 1)
                act.wait_ge(gate_prod, f + (KF * n + 1))
                nc.scalar.activation(ghi[:, bass.ds(f, 1), :].rearrange("p a t -> p (a t)"), g32[:],
                                     ACT.Copy).then_inc(ghi_done, 1)

            def ffn_up(n):
                for fp in range(2):
                    up_step(n, fp, fp, 0)
                nc.scalar.preload_act_table(ACT.Silu)
                with act.Fori(1, KF // 2) as i:
                    for fp in range(2):
                        up_step(n, 2 * i + fp, fp, i)

            def ffn_down(n):
                norm = (1, 3)[n]
                u0 = (U_FFN1, U_FFN2)[n] + 2 * KF
                nc.scalar.preload_act_table(ACT.Sqrt)
                for half in range(2):
                    u = u0 + HALF_UNITS * half
                    hi_u(u + 2)
                    if half:
                        for d in range(4):
                            square(norm, d)
                    with act.Fori(0, (HALF_UNITS - 1) // 2 - half) as i:
                        for s in range(2):
                            v = u + 3 + s
                            hi(i + v // 2, v % 2)
                hi_u(u + HALF_UNITS)
                for d in range(4, KD):
                    square(norm, d)
                root(norm)
                hi_u(u + HALF_UNITS + 1)

            act.wait_ge(vecs_loaded, 32)
            nc.scalar.activation(cs[:], vec("c", 0, 8), ACT.Silu).then_inc(cs_done, 1)
            act.wait_ge(small_done, 1)
            nc.scalar.activation(small[:, 32:40], small[:, 32:40], ACT.Exp).then_inc(cs_done, 1)
            nc.scalar.activation(small[:, 40:56], small[:, 40:56], ACT.Exp).then_inc(cs_done, 1)
            nc.scalar.preload_act_table(ACT.Sqrt)
            for d in range(KD):
                square(0, d)
            act.wait_ge(ones_set, 2)
            root(0)
            hi(0, 0)
            hi(0, 1)
            h_upper(0)
            ffn_up(0)
            ffn_down(0)
            h_upper(1)

            zi = {u: m for m, u in enumerate(Z_UNITS)}

            def z_bank(m):
                act.wait_ge(unit_used, U_MIX + m + 1)
                return bank[m % 2]

            def z_post(m):
                what, i = Z_UNITS[m]
                hi_u(U_MIX + m + 2)
                if what == "v":
                    if i == 3:
                        act.wait_ge(unit_used, U_MIX + 4)
                        for c in range(TC):
                            nc.scalar.activation(vn[:, c, :], bank[2 + c], ACT.Copy, scale=0.5).then_inc(v_copied, 1)
                    return
                src = z_bank(m)
                if what == "rx":
                    nc.scalar.activation(rxp[:, i, 2:2 + T], src, ACT.Copy).then_inc(z_evac, 1)
                elif what == "g":
                    nc.scalar.activation(sg[:, i, :], src, ACT.Tanh, scale=0.5).then_inc(z_evac, 1)
                elif what == "gate":
                    act.wait_ge(rg_scanned, 2 * RT)
                    nc.scalar.activation(gg[:, i, :], src, ACT.Copy).then_inc(z_evac, 1)
                else:
                    if what == "q" and i >= 2:
                        act.wait_ge(qk_done, 10 * (i - 1))
                        act.wait_ge(scored, STEPS * (i - 1))
                    slot = {"f": 0, "q": 1, "b": 2}[what]
                    nc.scalar.activation(w3[:, i % 2, slot, :], src, ACT.Tanh, scale=0.5).then_inc(z_evac, 1)

            def logs(h):
                for lane in range(2):
                    act.wait_ge(k_done, 6 * h + 3 * lane + 3)
                    v = lg[:, 517 * lane:517 * lane + T]
                    nc.scalar.activation(v, v, ACT.Ln).then_inc(ln_done, 1)

            def gate_post(dr, ct):
                gi = RT * dr + ct
                act.wait_ge(gates_summed, gi + 1)
                if dr:
                    act.wait_ge(rg_scanned, ct + 1)
                nc.scalar.activation(ra[:, ct, :], bank[2], ACT.Tanh, bias=half_b[:, gi:gi + 1],
                                     scale=0.5).then_inc(gate_evac, 1)
                nc.scalar.activation(ri[:, ct, :], bank[3], ACT.Tanh, bias=half_b[:, 8 + gi:9 + gi],
                                     scale=0.5).then_inc(gate_evac, 1)
                act.wait_ge(gate_evac, 2 * gi + 1)
                nc.scalar.activation(rt[:, ct, :], ra[:, ct, :], ACT.Tanh, bias=sp4[:, gi:gi + 1],
                                     scale=sp4[:, gi:gi + 1]).then_inc(tanh_done, 1)

            def rg_exp(dr, ct):
                gi = RT * dr + ct
                act.wait_ge(tanh_done, gi + 1)
                nc.scalar.activation(ra[:, ct, :], ra[:, ct, :], ACT.Exp, bias=nsp4[:, gi:gi + 1],
                                     scale=nsp4[:, gi:gi + 1]).then_inc(a_done, 1)
                act.wait_ge(a_done, gi + 1)
                if gi >= 2:
                    act.wait_ge(one_a2, gi - 1)
                nc.scalar.activation(a2[:, ct % 2, :], ra[:, ct, :], ACT.Square).then_inc(a2_done, 1)

            def rg_root(dr):
                for ct in range(RT):
                    act.wait_ge(one_a2, RT * dr + ct + 1)
                    nc.scalar.activation(rt[:, ct, :], rt[:, ct, :], ACT.Sqrt).then_inc(root_done, 1)

            def decay(h, e):
                if e >= 2:
                    act.wait_ge(qk_done, 10 * h + e - 1)
                elif h:
                    act.wait_ge(qk_done, 10 * (h - 1) + 9)
                if e == 0:
                    act.wait_ge(tot_ready, 2 * (h + 1))
                    if h:
                        act.wait_ge(far_done, h)
                    nc.scalar.activation(etot[:, h % 2], tot[:], ACT.Exp).then_inc(etot_done, 1)
                    nc.scalar.activation(dec[:, 0], cum[:, h % 2], ACT.Exp).then_inc(dec_done, 1)
                else:
                    act.wait_ge(dif_done, 8 * h + e)
                    nc.scalar.activation(dec[:, e % 2], dif[:, e % 2], ACT.Exp).then_inc(dec_done, 1)

            def block_copy(h, s):
                act.wait_ge(scored, STEPS * h + s + 1)
                if s == 0 and h:
                    act.wait_ge(pv_done, h)
                src = bank[4 + (STEPS * h + s) % 2]
                if s == 0:
                    nc.scalar.activation(pt[:, 1:5:3, :], src[:, 0:256].rearrange("p (b t) -> p b t", b=2), ACT.Copy)
                    nc.scalar.activation(pt[:, 11:15:3, :], src[:, 256:512].rearrange("p (b t) -> p b t", b=2),
                                         ACT.Copy).then_inc(blk_copied, 1)
                else:
                    p4 = pt[:].rearrange("p (a b) t -> p a b t", a=TC)
                    dst = {1: p4[:, 0:2, 2:4, :], 2: p4[:, 2:4, 0:2, :], 3: pt[:, 0:16:5, :]}[s]
                    src = (src.rearrange("p (b t) -> p b t", b=4) if s == 3
                           else src.rearrange("p (a b t) -> p a b t", a=2, b=2))
                    nc.scalar.activation(dst, src, ACT.Copy).then_inc(blk_copied, 1)

            def o_copy(h):
                act.wait_ge(pv_done, h + 1)
                if h == 0:
                    act.wait_ge(one_a2, 2 * RT)
                if h:
                    act.wait_ge(on_done, h)
                    act.wait_ge(osum_done, h)
                nc.scalar.activation(osb, bank[6], ACT.Copy).then_inc(osb_done, 1)
                nc.scalar.activation(osq, bank[6], ACT.Square).then_inc(osq_done, 1)

            def o_root(h):
                act.wait_ge(osum_done, h + 1)
                nc.scalar.activation(rms[:], sums(4), ACT.Sqrt, bias=epst[:],
                                     scale=1.0 / P).then_inc(orms_done, 1)

            def y_upper(k):
                if k < RT:
                    act.wait_ge(yrg_done, k + 1)
                else:
                    act.wait_ge(on_done, k - 3)
                act.wait_ge(unit_used, U_OUT)
                src = hr[:, k, :] if k < RT else on[:, k - RT, :]
                nc.scalar.activation(yhi[:, k, :], src, ACT.Copy).then_inc(yhi_done, 1)

            for m in range(9):
                z_post(m)
            act.wait_ge(small_done, 2)
            gate_post(0, 0)
            gate_post(0, 1)
            z_post(9)
            gate_post(0, 2)
            gate_post(0, 3)
            for ct in range(RT):
                rg_exp(0, ct)
            z_post(10)
            logs(0)
            rg_root(0)
            z_post(11)
            decay(0, 0)
            decay(0, 1)
            z_post(12)
            for r in range(HEADS):
                first = zi[("q", r + 1)] if r < 3 else None
                decay(r, 2)
                if r == 3:
                    for k in range(RT):
                        act.wait_ge(z_evac, N_Z - 4)
                        nc.scalar.activation(gg[:, k, :], gg[:, k, :], ACT.Gelu_apprx_tanh).then_inc(gelu_done, 1)
                    for k in range(RT):
                        y_upper(k)
                for g, steps in enumerate(STEPS_AT[r == 3]):
                    for s in steps:
                        if 3 <= s + 1 <= 8:
                            decay(r, s + 1)
                        if s < 4:
                            block_copy(r, s)
                    if r and g == 0:
                        o_copy(r - 1)
                    if r and g == (2 if r == 3 else 4):
                        o_root(r - 1)
                    if r == 1 and g == 1:
                        rg_root(1)
                    if r < 3:
                        if g == 9:
                            decay(r + 1, 0)
                            decay(r + 1, 1)
                        if g % 2:
                            z_post(first + g // 2)
                        if g == 6:
                            logs(r + 1)
                    if r == 0 and 4 <= g < 8:
                        gate_post(1, g - 4)
                        rg_exp(1, g - 4)
                    if r == 3:
                        if g % 2:
                            hi_u(U_OUT + g // 2 + 2)
                        if g == 2:
                            y_upper(4)
                            y_upper(5)
                        if g == 5:
                            y_upper(6)
            nc.scalar.preload_act_table(ACT.Sqrt)
            o_copy(3)
            o_root(3)
            y_upper(7)
            for m in range(3, 7):
                hi_u(U_OUT + m + 2)
                if m == 4:
                    for d in range(4):
                        square(2, d)
            for d in range(4, KD):
                square(2, d)
            root(2)
            hi_u(U_OUT + 9)
            h_upper(2)
            ffn_up(1)
            ffn_down(1)

        @block.vector
        def _(dve):
            def lo(j, slot):
                dve.wait_ge(hi_done, 2 * j + (slot + 1))
                nc.vector.tensor_tensor(wlo[:, slot, :], raw[:, slot, :], whi[:, slot, :],
                                        ALU.subtract).then_inc(lo_done, 1)

            def lo_u(u):
                if u < N_UNITS:
                    lo(u // 2, u % 2)

            def ada_add(j, k):
                if isinstance(j, int) and j < 2:
                    dve.wait_ge(ada_first[k % 4], 32 * j + 16 * (k // 4 + 1))
                else:
                    dve.wait_ge(ada_loaded[k % 4], 32 * j + (16 * (k // 4 + 1) - 64))
                if not (isinstance(j, int) and j == 0 and k == 0):
                    dve.wait_ge(ada_added, 8 * j + k)
                dst = acc
                if k == 7:
                    dst = fin
                    if not (isinstance(j, int) and j == 0):
                        dve.wait_ge(mod_summed, 1 * j)
                if k == 0:
                    nc.vector.tensor_scalar(dst[:], ada[:, k % 4, :], cs[:, k:k + 1], None,
                                            ALU.mult).then_inc(ada_added, 1)
                else:
                    nc.vector.scalar_tensor_tensor(dst[:], ada[:, k % 4, :], cs[:, k:k + 1], acc[:], ALU.mult,
                                                   ALU.add).then_inc(ada_added, 1)

            def mod_bias(j):
                dve.wait_ge(mod_summed, j + 1)
                nc.vector.tensor_tensor(mods[:, bass.ds(8 * j, 8)], modp, vecs[:, bass.ds(8 * j + VEC["b_ada"], 8)],
                                        ALU.add).then_inc(mod_ready, 1)

            def rms_inverse(n, done, r_done, d_done):
                dve.wait_ge(done, n + 1)
                nc.vector.reciprocal(rinv[:], rms[:]).then_inc(r_done, 1)
                dve.wait_ge(r_done, n + 1)
                nc.vector.tensor_tensor(diag[:], ident[:].unsqueeze(1).broadcast_to([P, TC, P]),
                                        rinv[:].unsqueeze(2).broadcast_to([P, TC, P]), ALU.mult).then_inc(d_done, 1)

            def h_split(n):
                dve.wait_ge(rb_done, n + 1)
                dve.wait_ge(cols_ready, 2 * n + 1)
                for d in range(KD + 1):
                    if n == 0 and d == 1:
                        mod_bias(1)
                        lo(0, 1)
                        dve.wait_ge(mod_ready, 2)
                    if d < KD:
                        if d >= 2:
                            dve.wait_ge(hlo_done, KD * n + d - 1)
                        nc.vector.scalar_tensor_tensor(tmp[:, d % 2, :], x[:, d, :], scale[:, KD * n + d:KD * n + d + 1],
                                                       rb(n), ALU.mult, ALU.mult).then_inc(htmp_done, 1)
                    if d:
                        dve.wait_ge(hhi_done, KD * n + d)
                        nc.vector.scalar_tensor_tensor(hlo[:, d - 1, :], tmp[:, (d - 1) % 2, :], mod(SHIFT[n], d - 1),
                                                       hhi[:, d - 1, :], ALU.add, ALU.subtract).then_inc(hlo_done, 1)

            def up_step(n, f, fp, i, mod_j=None):
                j = (U_FFN1, U_FFN2)[n] // 2 + 2 * i + fp
                ks = range(4 * fp, 4 * fp + 4) if mod_j is not None else ()
                lo(j + 1, 0)
                for k in ks[0:2]:
                    ada_add(mod_j, k)
                dve.wait_ge(unit_used, 2 * j + 2)
                dve.wait_ge(silu_done, f + (KF * n + 1))
                if not (isinstance(f, int) and KF * n + f == 0):
                    dve.wait_ge(glo_done, f + KF * n)
                nc.vector.tensor_tensor(g32[:], silu_sb[:], bank[2 + fp], ALU.mult).then_inc(gate_prod, 1)
                lo(j + 1, 1)
                dve.wait_ge(ghi_done, f + (KF * n + 1))
                nc.vector.tensor_tensor(glo[:, bass.ds(f, 1), :].rearrange("p a t -> p (a t)"), g32[:],
                                        ghi[:, bass.ds(f, 1), :].rearrange("p a t -> p (a t)"),
                                        ALU.subtract).then_inc(glo_done, 1)
                for k in ks[2:4]:
                    ada_add(mod_j, k)

            def update(n, d, src):
                if d in (4, 5, 6):
                    dve.wait_ge(tile_done, 3 * n + d - 3)
                else:
                    dve.wait_ge(unit_used, (U_FFN1 + 2 * KF, U_OUT, U_FFN2 + 2 * KF)[n]
                                + (HALF_UNITS, 4, HALF_UNITS)[n] * (1 + d // 4))
                nc.vector.scalar_tensor_tensor(x[:, d, :], src, gates[:, KD * n + d:KD * n + d + 1], x[:, d, :],
                                               ALU.mult, ALU.add).then_inc(x_ready, 1)

            def columns(n):
                g, sc = ("g1", "g2", "g3")[n], ("sc2", "sc3")[n] if n < 2 else None
                dve.wait_ge(mod_ready, N_MOD)
                nc.vector.tensor_scalar(gates[:, KD * n:KD * n + KD], mod(g, 0, KD), (0.5, 1.0, 0.5)[n], None,
                                        ALU.mult).then_inc(cols_ready, 1)
                if sc:
                    nc.vector.scalar_tensor_tensor(scale[:, KD * (n + 1):KD * (n + 2)], mod(sc, 0, KD), 1.0,
                                                   vec(f"norm{n + 1}", 0, KD), ALU.add, ALU.mult).then_inc(cols_ready, 1)

            def ffn_down(n):
                branch, u0 = (0, 2)[n], (U_FFN1, U_FFN2)[n] + 2 * KF
                columns(branch)
                dve.wait_ge(cols_ready, (3, 6)[n])
                for half in range(2):
                    u = u0 + HALF_UNITS * half
                    lo_u(u + 2)
                    if half:
                        for d in range(4):
                            update(branch, d, bank[4 + d])
                    with dve.Fori(0, (HALF_UNITS - 1) // 2 - half) as i:
                        for s in range(2):
                            v = u + 3 + s
                            lo(i + v // 2, v % 2)
                lo_u(u + HALF_UNITS)
                for d in range(4, KD):
                    update(branch, d, bank[d - 4])
                rms_inverse((1, 3)[n], rms_done, rinv_done, diag_done)
                lo_u(u + HALF_UNITS + 1)

            nc.vector.memset(ones[:], 1.0).then_inc(ones_set, 1)
            nc.vector.memset(epst[:], EPS).then_inc(ones_set, 1)
            dve.wait_ge(vecs_loaded, 32)
            chain = [0]

            def step(ins):
                chain[0] += 1
                ins.then_inc(cum_step, 1)
                dve.wait_ge(cum_step, chain[0])

            lam, y_, ym, s_, s2, q_ = (small[:, 8 * i:8 * i + 8] for i in (10, 4, 11, 12, 13, 14))
            lb_e, t8, t9 = small[:, 40:56], small[:, 120:128], small[:, 128:136]
            step(nc.vector.tensor_scalar(lam, vec("lam", 0, 8), -1.0, None, ALU.mult))
            step(nc.vector.tensor_tensor(y_, lam, vec("lam", 0, 8), ALU.min))
            lb0, lb1 = vec("lb", 0, 8), vec("lb", 8, 8)
            step(nc.vector.tensor_tensor(t8, lb0, lb1, ALU.max))
            step(nc.vector.tensor_tensor(lb_e[:, 0:8], lb0, t8, ALU.subtract))
            nc.vector.tensor_tensor(lb_e[:, 8:16], lb1, t8, ALU.subtract).then_inc(small_done, 1)
            dve.wait_ge(cs_done, 3)
            step(nc.vector.tensor_scalar(ym, y_, 2.0, None, ALU.add))
            step(nc.vector.reciprocal(s_, ym))
            step(nc.vector.tensor_tensor(s_, s_, y_, ALU.mult))
            step(nc.vector.tensor_tensor(s2, s_, s_, ALU.mult))
            step(nc.vector.tensor_scalar(q_, s2, 1.0 / 17, None, ALU.mult))
            for o in (15, 13, 11, 9, 7, 5, 3):
                step(nc.vector.scalar_tensor_tensor(q_, q_, 1.0 / o, s2, ALU.add, ALU.mult))
            step(nc.vector.scalar_tensor_tensor(q_, q_, 1.0, s_, ALU.add, ALU.mult))
            step(nc.vector.tensor_scalar(lam, lam, 0.0, None, ALU.max))
            step(nc.vector.scalar_tensor_tensor(q_, q_, 2.0, lam, ALU.mult, ALU.add))
            step(nc.vector.tensor_scalar(nsp4, q_, -4.0, None, ALU.mult))
            step(nc.vector.tensor_scalar(sp4, q_, 4.0, None, ALU.mult))
            step(nc.vector.tensor_scalar(half_b, vec("ba", 0, 16), 0.5, None, ALU.mult))
            step(nc.vector.tensor_scalar(half_gain, vec("hg_norm"), 0.5, None, ALU.mult))
            step(nc.vector.tensor_tensor(t8, lb_e[:, 0:8], lb_e[:, 8:16], ALU.add))
            step(nc.vector.reciprocal(t8, t8))
            step(nc.vector.tensor_tensor(lb_e[:, 0:8], lb_e[:, 0:8], t8, ALU.mult))
            step(nc.vector.tensor_tensor(lb_e[:, 8:16], lb_e[:, 8:16], t8, ALU.mult))
            step(nc.vector.tensor_tensor(t9, lb_e[:, 0:8], lb_e[:, 8:16], ALU.add))
            step(nc.vector.tensor_tensor(t9, t9, lb_e[:, 0:8], ALU.subtract))
            step(nc.vector.tensor_scalar(omh, t9, -0.5, 0.5, ALU.mult, ALU.add))
            nc.vector.tensor_tensor(lbm, t9, omh, ALU.add).then_inc(small_done, 1)
            dve.wait_ge(cs_done, 1)
            for k in range(8):
                ada_add(0, k)
            for k in range(8):
                ada_add(1, k)
                if k == 5:
                    mod_bias(0)
                if k == 6:
                    rms_inverse(0, rms_done, rinv_done, diag_done)
            dve.wait_ge(mod_ready, 1)
            nc.vector.scalar_tensor_tensor(scale[:, 0:KD], mod("sc1", 0, KD), 1.0, vec("norm0", 0, KD), ALU.add,
                                           ALU.mult).then_inc(cols_ready, 1)
            lo(0, 0)
            h_split(0)
            for fp in range(2):
                up_step(0, fp, fp, 0, 2)
            with dve.Fori(1, 7) as i:
                for fp in range(2):
                    up_step(0, 2 * i + fp, fp, i, i + 2)
                mod_bias(i + 1)
            for fp in range(2):
                up_step(0, 14 + fp, fp, 7)
            mod_bias(8)
            with dve.Fori(8, KF // 2) as i:
                for fp in range(2):
                    up_step(0, 2 * i + fp, fp, i)
            ffn_down(0)
            h_split(1)

            zi = {u: m for m, u in enumerate(Z_UNITS)}
            nc.vector.memset(rxp[:, :, 0:2], 0.0).then_inc(rxp_zero, 1)
            nc.vector.memset(rxp[:, :, 2 + T:4 + T], 0.0).then_inc(rxp_zero, 1)

            conv = [0]

            def convolve(ct):
                dve.wait_ge(z_evac, ct + 1)
                dve.wait_ge(rxp_zero, 2)
                for j in range(4):
                    tap = vec("conv_w", 4 * j + ct)
                    src = rxp[:, ct, j:j + T]
                    if j == 0:
                        ins = nc.vector.tensor_scalar(xc[:, ct, :], src, tap, vec("conv_b", ct), ALU.mult, ALU.add)
                    else:
                        ins = nc.vector.scalar_tensor_tensor(xc[:, ct, :], src, tap, xc[:, ct, :], ALU.mult, ALU.add)
                    if j < 3:
                        conv[0] += 1
                        ins.then_inc(conv_step, 1)
                        dve.wait_ge(conv_step, conv[0])
                ins.then_inc(xc_ready, 1)

            def one_minus_a2(dr, ct):
                dve.wait_ge(a2_done, RT * dr + ct + 1)
                nc.vector.scalar_tensor_tensor(rt[:, ct, :], a2[:, ct % 2, :], 1.0, rt[:, ct, :], ALU.add,
                                               ALU.mult).then_inc(one_a2, 1)

            rg = [0]

            def recur(dr, ct):
                def rstep(ins):
                    rg[0] += 1
                    ins.then_inc(rg_step, 1)
                    dve.wait_ge(rg_step, rg[0])
                rstep(nc.vector.scalar_tensor_tensor(ri[:, ct, :], ri[:, ct, :], 1.0, xc[:, ct, :], ALU.add, ALU.mult))
                dve.wait_ge(root_done, RT * dr + ct + 1)
                rstep(nc.vector.tensor_tensor(ri[:, ct, :], ri[:, ct, :], rt[:, ct, :], ALU.mult))
                if dr == 0:
                    nc.vector.tensor_tensor_scan(hr[:, ct, :], ra[:, ct, :], ri[:, ct, :], 0.0, ALU.mult,
                                                 ALU.add).then_inc(rg_scanned, 1)
                else:
                    rstep(nc.vector.tensor_tensor_scan(rt[:, ct, ::-1], ra[:, ct, ::-1], ri[:, ct, ::-1], 0.0, ALU.mult,
                                                       ALU.add))
                    nc.vector.tensor_tensor(hr[:, ct, :], hr[:, ct, :], rt[:, ct, :], ALU.add).then_inc(rg_scanned, 1)

            def z_post(m):
                what, i = Z_UNITS[m]
                lo_u(U_MIX + m + 2)
                if what in "qg":
                    dst = w3[:, i % 2, 1, :] if what == "q" else sg[:, i, :]
                    dve.wait_ge(z_evac, m - 3)
                    nc.vector.scalar_tensor_tensor(dst, dst, 1.0, bank[m % 2], ALU.add, ALU.mult).then_inc(zq_done, 1)
                if what in "fb":
                    lane = "fb".index(what)
                    slot = 2 * lane
                    dve.wait_ge(z_evac, m - 3)
                    if i:
                        dve.wait_ge(cum_ready, 2 * i)
                    v = lg[:, 517 * lane:517 * lane + T]
                    c = 4 * lane + i
                    nc.vector.tensor_scalar(v, w3[:, i % 2, slot, :], omh[:, c:c + 1], lbm[:, c:c + 1], ALU.mult,
                                            ALU.add).then_inc(k_done, 1)
                    dve.wait_ge(k_done, 6 * i + 3 * lane + 1)
                    nc.vector.tensor_scalar(w3[:, i % 2, slot, :], v, -1.0, 1.0, ALU.mult, ALU.add).then_inc(k_done, 1)
                    dve.wait_ge(k_done, 6 * i + 3 * lane + 2)
                    nc.vector.tensor_scalar(v, v, 1e-18, None, ALU.max).then_inc(k_done, 1)

            def sum_logs(h):
                p = h % 2
                dve.wait_ge(ln_done, 2 * h + 2)
                if h >= 1:
                    dve.wait_ge(dif_done, 8 * (h - 1) + 1)
                    dve.wait_ge(etot_done, h)
                if h >= 2:
                    dve.wait_ge(dec_done, 9 * (h - 1))
                late = lg[:, 516:516 + T + 1]
                step(nc.vector.tensor_copy(lgend[:], late[:, P:T + 1:P]))
                step(nc.vector.memset(late[:, 0:T:P], 0.0))
                nc.vector.tensor_tensor_scan(cum[:, p, 0, :], resets[:], lg[:, 0:T], 0.0, ALU.mult,
                                             ALU.add).then_inc(cum_ready, 1)
                nc.vector.tensor_tensor_scan(cum[:, p, 1, :], resets[:], late[:, 0:T], 0.0, ALU.mult,
                                             ALU.add).then_inc(cum_ready, 1)
                dve.wait_ge(cum_ready, 2 * h + 2)
                nc.vector.tensor_copy(tot[:, 0, :], cum[:, p, 0, P - 1:T:P]).then_inc(tot_ready, 1)
                nc.vector.tensor_tensor(tot[:, 1, :], cum[:, p, 1, P - 1:T:P], lgend[:], ALU.add).then_inc(tot_ready, 1)

            def decayed(h, e):
                p = h % 2
                if e in (0, 1) and h:
                    dve.wait_ge(scored, STEPS * (h - 1) + 10 + e)
                elif e in (2, 3):
                    dve.wait_ge(scored, STEPS * h + 3)
                elif e >= 4:
                    dve.wait_ge(scored, STEPS * h + e)
                if e < 9:
                    dve.wait_ge(dec_done, 9 * h + e + 1)
                if e < 2:
                    if e == 0:
                        dve.wait_ge(k_done, 6 * h + 6)
                        dve.wait_ge(zq_done, QG_COUNT[("q", h)])
                    nc.vector.tensor_tensor(qk[:, e], dec[:, e], w3[:, p, 1 - e:3 - e, :], ALU.mult).then_inc(qk_done, 1)
                elif e < 9:
                    hw = LEVELS[e - 2]
                    q5 = qk[:, e % 2].rearrange("p l (n two w) -> p l n two w", two=2, w=hw)
                    d5 = dec[:, e % 2].rearrange("p l (n two w) -> p l n two w", two=2, w=hw)
                    w5 = w3[:, p].rearrange("p l (n two w) -> p l n two w", two=2, w=hw)
                    nc.vector.tensor_tensor(q5[:, :, :, 1, :], d5[:, :, :, 1, :], w5[:, 1:3, :, 1, :], ALU.mult)
                    nc.vector.tensor_tensor(q5[:, ::-1, :, 0, :], d5[:, :, :, 0, :], w5[:, 0:2, :, 0, :],
                                            ALU.mult).then_inc(qk_done, 1)
                else:
                    nc.vector.tensor_tensor(qk[:, 1, 1, :], w3[:, p, 0, :], w3[:, p, 2, :], ALU.add).then_inc(qk_done, 1)

            def decay_far(h):
                dve.wait_ge(qk_done, 10 * h + 2)
                dve.wait_ge(etot_done, h + 1)
                for i, (e, lane, c, by) in enumerate(((0, 0, 3, 2), (1, 0, 0, 1), (1, 1, 0, 1), (0, 1, 3, 2))):
                    ins = nc.vector.tensor_scalar(far[:, i, :], qk[:, e, lane, c * P:(c + 1) * P],
                                                  etot[:, h % 2, lane, by:by + 1], None, ALU.mult)
                ins.then_inc(far_done, 1)

            def mask_in_block(h, s):
                dve.wait_ge(scored, STEPS * h + s + 1)
                if s == 4:
                    dve.wait_ge(blk_copied, 4 * h + 4)
                else:
                    dve.wait_ge(blk_masked, 7 * h + s - 4)
                nc.vector.copy_predicated(pt[:, 0:16:5, :], masks[:, s - 4:s - 3, :].broadcast_to([P, TC, P]),
                                          bank[4 + (STEPS * h + s) % 2].rearrange("p (b t) -> p b t", b=TC)
                                          ).then_inc(blk_masked, 1)

            def o_norm(h):
                dve.wait_ge(orb_done, h + 1)
                dve.wait_ge(osb_done, h + 1)
                nc.vector.scalar_tensor_tensor(on[:, h, :], osb, half_gain, rb(4), ALU.mult,
                                               ALU.mult).then_inc(on_step, 1)
                dve.wait_ge(on_step, h + 1)
                nc.vector.tensor_tensor(on[:, h, :], on[:, h, :], sg[:, h, :], ALU.mult).then_inc(on_done, 1)

            def y_lower(k):
                dve.wait_ge(yhi_done, k + 1)
                src = hr[:, k, :] if k < RT else on[:, k - RT, :]
                nc.vector.tensor_tensor(ylo[:, k, :], src, yhi[:, k, :], ALU.subtract).then_inc(y_ready, 1)

            for m in range(4):
                z_post(m)
            for m in range(4, 8):
                z_post(m)
                convolve(m - 4)
            dve.wait_ge(mix_loaded, 48)
            nc.vector.tensor_copy(masks[:].rearrange("p a t -> p (a t)"), mask_f).then_inc(masks_set, 1)
            z_post(8)
            z_post(9)
            for ct in range(RT):
                one_minus_a2(0, ct)
            z_post(10)
            sum_logs(0)
            for ct in range(2):
                recur(0, ct)
            z_post(11)
            for ct in range(2, 4):
                recur(0, ct)
            z_post(12)
            for r in range(HEADS):
                first = zi[("q", r + 1)] if r < 3 else None
                gaps = STEPS_AT[r == 3]
                decayed(r, 0)
                decayed(r, 1)
                decay_far(r)
                if r == 3:
                    for k in range(RT):
                        dve.wait_ge(gelu_done, k + 1)
                        dve.wait_ge(rg_scanned, RT + k + 1)
                        nc.vector.scalar_tensor_tensor(hr[:, k, :], hr[:, k, :], 0.5, gg[:, k, :], ALU.mult,
                                                       ALU.mult).then_inc(yrg_done, 1)
                    for k in range(RT):
                        y_lower(k)
                for g, steps in enumerate(gaps):
                    for s in steps:
                        if s >= 2 and s < STEPS - 1:
                            decayed(r, s)
                        if s >= 5:
                            mask_in_block(r, s - 1)
                    if g and g % 2 == 0:
                        if r < 3:
                            z_post(first + g // 2 - 1)
                        else:
                            lo_u(U_OUT + g // 2 + 1)
                    if r < 3 and g == 7:
                        sum_logs(r + 1)
                    if r and g == (2 if r == 3 else 5):
                        rms_inverse(r - 1, orms_done, orinv_done, odiag_done)
                    if r and g == (4 if r == 3 else 7):
                        o_norm(r - 1)
                    if r == 0 and 5 <= g < 9:
                        one_minus_a2(1, g - 5)
                    if r == 1 and 2 <= g < 6:
                        recur(1, g - 2)
                    if r == 3 and g == 3:
                        y_lower(4)
                        y_lower(5)
                    if r == 3 and g == 5:
                        y_lower(6)
                mask_in_block(r, STEPS - 1)
                if r < 3:
                    z_post(first + 4)
                else:
                    lo_u(U_OUT + 4)
            rms_inverse(3, orms_done, orinv_done, odiag_done)
            o_norm(3)
            y_lower(7)
            columns(1)
            dve.wait_ge(cols_ready, 5)
            for m in range(3, 7):
                lo_u(U_OUT + m + 2)
                if m == 4:
                    for d in range(4):
                        update(1, d, bank[d])
            for d in range(4, KD):
                update(1, d, bank[d])
            rms_inverse(2, rms_done, rinv_done, diag_done)
            lo_u(U_OUT + 9)
            h_split(2)
            for fp in range(2):
                up_step(1, fp, fp, 0)
            with dve.Fori(1, KF // 2) as i:
                for fp in range(2):
                    up_step(1, 2 * i + fp, fp, i)
            ffn_down(1)
            dve.wait_ge(rb_done, 4)
            for d in range(KD):
                nc.vector.scalar_tensor_tensor(outt[:, d, :], x[:, d, :], vec("norm3", d), rb(3), ALU.mult,
                                               ALU.mult).then_inc(out_ready, 1)

        @block.tensor
        def _(pe):
            def three(dst, slot, col, rhi, rlo, start, stop):
                a, b = whi[:, slot, col:col + P], wlo[:, slot, col:col + P]
                nc.tensor.matmul(dst, a, rhi, start=start, stop=False)
                nc.tensor.matmul(dst, a, rlo, start=False, stop=False)
                return nc.tensor.matmul(dst, b, rhi, start=False, stop=stop)

            def up_step(n, f, fp, i):
                j = (U_FFN1, U_FFN2)[n] // 2 + 2 * i + fp
                if isinstance(f, int) and f == 0:
                    pe.wait_ge(lo_done, 2 * j + 2)
                    for k in range(KD):
                        pe.wait_ge(hlo_done, KD * (0, 2)[n] + k + 1)
                        for s in range(2):
                            ins = three(bank[2 * s], s, k * P, hhi[:, k, :], hlo[:, k, :], k == 0, k == KD - 1)
                            if k == KD - 1:
                                ins.then_inc(unit_used, 1)
                    return
                for s in range(2):
                    pe.wait_ge(lo_done, 2 * j + (s + 1))
                    if not (isinstance(f, int) and f < 2) or n:
                        pe.wait_ge((silu_done, gate_prod)[s], f + (KF * n - 1))
                    for k in range(KD):
                        ins = three(bank[2 * s + fp], s, k * P, hhi[:, k, :], hlo[:, k, :], k == 0, k == KD - 1)
                    ins.then_inc(unit_used, 1)

            def mod_sum(j):
                pe.wait_ge(ada_added, 8 * j + 8)
                if not (isinstance(j, int) and j == 0):
                    pe.wait_ge(mod_ready, 1 * j)
                for t in range(KD):
                    ins = nc.tensor.matmul(modp[:, t:t + 1], fin[:, t * P:(t + 1) * P], ones[:, 0:1], start=True,
                                           stop=True)
                ins.then_inc(mod_summed, 1)

            def last_unit(slot, b0, rhs):
                for d in range(4):
                    for t in range(2):
                        rhi, rlo = rhs(t)
                        ins = three(bank[b0 + d], slot, (4 * t + d) * P, rhi, rlo, False, t == 1)
                    ins.then_inc(unit_used if d == 3 else tile_done, 1)

            def down_unit(half, slot, rhs, first, last, wait_for):
                wait_for()
                for t in range(2):
                    rhi, rlo = rhs(t)
                    for d in range(4):
                        ins = three(bank[(4, 0)[half] + d], slot, (4 * t + d) * P, rhi, rlo, first and t == 0,
                                    last and t == 1)
                ins.then_inc(unit_used, 1)

            def ffn_down(n):
                u0 = (U_FFN1, U_FFN2)[n] + 2 * KF
                for half in range(2):
                    u = u0 + HALF_UNITS * half

                    def rhs_of(k):
                        return lambda t: tuple(g[:, bass.ds(k + t, 1), :].rearrange("p a t -> p (a t)")
                                               for g in (ghi, glo))

                    def wait_for(u=u, half=half):
                        pe.wait_ge(lo_done, u + 1)
                        if half == 0:
                            pe.wait_ge(glo_done, KF * n + 2)
                            pe.wait_ge(mod_ready, N_MOD)
                        else:
                            pe.wait_ge(glo_done, KF * n + KF)

                    down_unit(half, u % 2, rhs_of(0), True, False, wait_for)
                    with pe.Fori(0, (HALF_UNITS - 1) // 2 - 1) as i:
                        for s in range(2):
                            v = u + 1 + s

                            def wait_in(v=v, s=s, half=half):
                                pe.wait_ge(lo_done, 2 * i + (v + 1))
                                if half == 0:
                                    pe.wait_ge(glo_done, 4 * i + (KF * n + 4 + 2 * s))
                            down_unit(half, v % 2, rhs_of(4 * i + (2 + 2 * s)), False, False, wait_in)
                    if half:
                        norm_sums((1, 3)[n], 0)
                    for s in range(2):
                        v = u + HALF_UNITS - 2 + s

                        def wait_last(v=v, s=s, half=half):
                            pe.wait_ge(lo_done, v + 1)
                            if half == 0:
                                pe.wait_ge(glo_done, KF * n + KF - 2 + 2 * s)
                        if half and s:
                            wait_last()
                            last_unit(v % 2, 0, rhs_of(KF - 2))
                        else:
                            down_unit(half, v % 2, rhs_of(KF - 4 + 2 * s), False, s == 1, wait_last)

            def norm_sums(n, part):
                if part == 0:
                    if n == 0:
                        pe.wait_ge(ones_set, 2)
                    else:
                        pe.wait_ge(x_ready, KD * (n - 1) + 4)
                for i, slot in (((0, 0),), ((1, 0), (2, 2), (3, 3)))[part]:
                    if i < 2:
                        pe.wait_ge(sq_added, 3 * n + 2 + i)
                    else:
                        pe.wait_ge(sq_done, KD * n + 5 + i)
                    for c in range(TC):
                        ins = nc.tensor.matmul(sums(n)[:, c:c + 1], sq[:, slot, c * P:(c + 1) * P], ones[:, 0:1],
                                               start=(i == 0 and c == 0), stop=(i == 3), skip_group_check=True)
                    ins.then_inc(sq_used, 1)

            def keep_busy(b, n):
                for _ in range(n):
                    nc.tensor.matmul(bank[b][:, 0:P], ident[:], ones[:], start=True, stop=True)

            def norm_turn(n, b):
                keep_busy(b, 2)
                norm_sums(n, 1)
                keep_busy(b, 3)
                norm_rb(n)
                keep_busy(b, 11)

            def norm_rb(n):
                pe.wait_ge(diag_done, n + 1)
                nc.tensor.matmul(rb(n), ones[:], diag[:].rearrange("p c t -> p (c t)"), start=True,
                                 stop=True).then_inc(rb_done, 1)

            norm_sums(0, 0)
            mod_sum(0)
            norm_sums(0, 1)
            keep_busy(4, 4)
            norm_rb(0)
            mod_sum(1)
            keep_busy(4, 7)
            for fp in range(2):
                up_step(0, fp, fp, 0)
            with pe.Fori(1, 8) as i:
                up_step(0, 2 * i, 0, i)
                mod_sum(i + 1)
                up_step(0, 2 * i + 1, 1, i)
            with pe.Fori(8, KF // 2) as i:
                for fp in range(2):
                    up_step(0, 2 * i + fp, fp, i)
            ffn_down(0)
            norm_turn(1, 5)

            zi = {u: m for m, u in enumerate(Z_UNITS)}

            def z_half(m, part):
                u = U_MIX + m
                what, i = Z_UNITS[m]
                if part == 0:
                    pe.wait_ge(lo_done, u + 1)
                if what == "v":
                    k = 2 * i + part
                    if i == 0:
                        pe.wait_ge(hlo_done, KD + k + 1)
                    elif part == 0:
                        pe.wait_ge(hlo_done, KD + 2 * i + 2)
                    a, b = (w[:, u % 2, part * T:(part + 1) * T] for w in (whi, wlo))
                    for c in range(TC):
                        dst, cc = bank[2 + c], slice(c * P, (c + 1) * P)
                        nc.tensor.matmul(dst, hhi[:, k, cc], a, start=(k == 0), stop=False)
                        nc.tensor.matmul(dst, hhi[:, k, cc], b, start=False, stop=False)
                        ins = nc.tensor.matmul(dst, hlo[:, k, cc], a, start=False, stop=(k == KD - 1))
                else:
                    if part == 0 and m >= 6:
                        pe.wait_ge(z_evac, m - 5)
                        if Z_UNITS[m - 2] in QG_COUNT:
                            pe.wait_ge(zq_done, QG_COUNT[Z_UNITS[m - 2]])
                    for k in range(4 * part, 4 * part + 4):
                        ins = three(bank[m % 2], u % 2, k * P, hhi[:, k, :], hlo[:, k, :], k == 0, k == KD - 1)
                if part == 1:
                    ins.then_inc(unit_used, 1)

            def z_unit(m):
                z_half(m, 0)
                z_half(m, 1)

            def gate_sums(dr, ct):
                gi = RT * dr + ct
                pe.wait_ge(xc_ready, ct + 1)
                pe.wait_ge(mix_loaded, 48)
                if gi:
                    pe.wait_ge(gate_evac, 2 * gi)
                else:
                    pe.wait_ge(v_copied, 2)
                for w in range(2):
                    ins = nc.tensor.matmul(bank[2 + w], bd[:, 2 * dr + w, ct, :], xc[:, ct, :], start=True, stop=True)
                ins.then_inc(gates_summed, 1)

            def scores(h, s):
                before = step_before(h, s, 2)
                if before is None:
                    pe.wait_ge(v_copied, TC)
                else:
                    evac_wait(pe, *before)
                dst = bank[4 + (STEPS * h + s) % 2]
                QF, KB, KF_, QB = qk[:, 0, 0, :], qk[:, 0, 1, :], qk[:, 1, 0, :], qk[:, 1, 1, :]

                def c(a, i):
                    return a[:, i * P:(i + 1) * P]
                if s == 0:
                    pe.wait_ge(qk_done, 10 * h + 2)
                    pairs = [(c(KF_, 0), c(QF, 1)), (c(KB, 1), c(QB, 0)), (c(KF_, 2), c(QF, 3)), (c(KB, 3), c(QB, 2))]
                elif s == 1:
                    pe.wait_ge(far_done, h + 1)
                    pairs = [(k, q) for k in (far[:, 1, :], c(KF_, 1)) for q in (c(QF, 2), far[:, 0, :])]
                elif s == 2:
                    pairs = [(k, q) for k in (c(KB, 2), far[:, 3, :]) for q in (far[:, 2, :], c(QB, 1))]
                else:
                    pe.wait_ge(qk_done, 10 * h + s)
                    e = s - 1
                    q = qk[:, e % 2, 0, :] if s < STEPS - 1 else w3[:, h % 2, 1, :]
                    pairs = [(c(qk[:, e % 2, 1, :], i), c(q, i)) for i in range(TC)]
                for i, (k, q) in enumerate(pairs):
                    ins = nc.tensor.matmul(dst[:, i * P:(i + 1) * P], k, q, start=True, stop=True)
                ins.then_inc(scored, 1)

            def pv(h):
                pe.wait_ge(blk_copied, 4 * h + 4)
                pe.wait_ge(blk_masked, 7 * h + 7)
                if h:
                    pe.wait_ge(osb_done, h)
                    pe.wait_ge(osq_done, h)
                for c in range(TC):
                    ins = nc.tensor.matmul(bank[6], vn[:, c, h * P:(h + 1) * P],
                                           pt[:, 4 * c:4 * c + 4, :].rearrange("p b t -> p (b t)"), start=(c == 0),
                                           stop=(c == TC - 1))
                ins.then_inc(pv_done, 1)

            def o_sums(h):
                pe.wait_ge(osq_done, h + 1)
                if h:
                    pe.wait_ge(on_done, h)
                for c in range(TC):
                    ins = nc.tensor.matmul(sums(4)[:, c:c + 1], osq[:, c * P:(c + 1) * P], ones[:, 0:1], start=True,
                                           stop=True)
                ins.then_inc(osum_done, 1)

            def o_rb(h):
                pe.wait_ge(odiag_done, h + 1)
                nc.tensor.matmul(rb(4), ones[:], diag[:].rearrange("p c t -> p (c t)"), start=True,
                                 stop=True).then_inc(orb_done, 1)

            def out_half(m, part):
                half, kk = m // 4, m % 4
                u = U_OUT + m
                if part == 0:
                    pe.wait_ge(lo_done, u + 1)
                    if m == 0:
                        pe.wait_ge(z_evac, N_Z - 4)
                        pe.wait_ge(gate_evac, 16)
                    if m == 4:
                        pe.wait_ge(on_done, HEADS)
                k = 2 * kk + part
                if half == 0:
                    pe.wait_ge(y_ready, k + 1)
                for d in range(4):
                    ins = three(bank[4 * half + d], u % 2, (4 * part + d) * P, yhi[:, k, :], ylo[:, k, :], k == 0,
                                k == KD - 1)
                if part == 1:
                    ins.then_inc(unit_used, 1)

            for m in range(9):
                z_unit(m)
            gate_sums(0, 0)
            gate_sums(0, 1)
            z_unit(9)
            gate_sums(0, 2)
            gate_sums(0, 3)
            for m in range(10, 13):
                z_unit(m)
            for r in range(HEADS):
                first = zi[("q", r + 1)] if r < 3 else None
                for g, steps in enumerate(STEPS_AT[r == 3]):
                    if r < 3:
                        z_half(first + g // 2, g % 2)
                    else:
                        out_half(g // 2, g % 2)
                    if r and g == 0:
                        pv(r - 1)
                    for s in steps:
                        scores(r, s)
                    if r and g == (1 if r == 3 else 3):
                        o_sums(r - 1)
                    if r and g == (3 if r == 3 else 6):
                        o_rb(r - 1)
                    if r == 0 and 3 <= g < 7:
                        gate_sums(1, g - 3)
            pv(3)
            o_sums(3)
            out_half(3, 0)
            o_rb(3)
            out_half(3, 1)
            for m in range(4, 7):
                out_half(m, 0)
                out_half(m, 1)
            norm_sums(2, 0)
            pe.wait_ge(lo_done, U_OUT + 8)
            last_unit((U_OUT + 7) % 2, 4, lambda t: (yhi[:, 6 + t, :], ylo[:, 6 + t, :]))
            norm_turn(2, 2)
            for fp in range(2):
                up_step(1, fp, fp, 0)
            with pe.Fori(1, KF // 2) as i:
                for fp in range(2):
                    up_step(1, 2 * i + fp, fp, i)
            ffn_down(1)
            norm_sums(3, 1)
            norm_rb(3)


def _down_units(w):
    n = w.shape[0] // 256
    return w.reshape(n, 2, P, 2, 4, P).transpose(3, 0, 2, 1, 4, 5).reshape(2 * n, P, UNIT)


def _col_units(w):
    n = w.shape[1] // P
    return w.reshape(KD, P, n, P).transpose(2, 1, 0, 3).reshape(n, P, UNIT)


def _cols(v):
    return np.ascontiguousarray(v).reshape(-1, P).T


def layout(inputs):
    i = {k: np.asarray(v) for k, v in inputs.items()}
    units = []

    def ffn(w1, w3, w2):
        units.append(np.stack([_col_units(w1), _col_units(w3)], axis=1).reshape(2 * KF, P, UNIT))
        units.append(_down_units(w2))

    ffn(i["ffn1_w1"][0], i["ffn1_w3"][0], i["ffn1_w2"][0])
    w_in = i["w_in"][0]
    v = w_in[:, Z_COLUMN["v"]:Z_COLUMN["v"] + T].reshape(4, 2, P, T).transpose(0, 2, 1, 3).reshape(4, P, UNIT)
    z = _col_units(w_in)
    units.append(np.stack([v[t] if what == "v" else z[Z_COLUMN[what] // P + t] for what, t in Z_UNITS]))
    w_out = i["w_out"][0]
    units.append(_down_units(np.concatenate([w_out[T:], w_out[:T]])))
    ffn(i["ffn2_w1"][0], i["ffn2_w3"][0], i["ffn2_w2"][0])
    order = [MOD_AT[m] for m in MODS]
    wada = i["w_ada"][0].reshape(KD, P, N_MOD, D).transpose(2, 0, 1, 3)[order].reshape(N_MOD * KD, P, D)
    vecs = [_cols(i["c"][0]), _cols(i["b_ada"][0].reshape(N_MOD, D)[order].reshape(-1)),
            _cols(i["ffn1_norm"][0]), _cols(i["mix_norm"][0]), _cols(i["ffn2_norm"][0]), _cols(i["final_norm"]),
            _cols(i["hg_lb_fwd"][0]), _cols(i["hg_lb_bwd"][0]), _cols(i["hg_lb_fwd"][1]), _cols(i["hg_lb_bwd"][1]),
            _cols(i["hg_out_norm"][0]), _cols(i["rg_conv_w"][0].reshape(-1)), _cols(i["rg_conv_b"][0])]
    for a, b in (("rg_ba_fwd", "rg_ba_bwd"), ("rg_bx_fwd", "rg_bx_bwd"), ("rg_lam_fwd", "rg_lam_bwd")):
        vecs += [_cols(i[a][0]), _cols(i[b][0])]
    bd = np.zeros((P, 4, RT, P), np.float32)
    for w, name in enumerate(("rg_wa_fwd", "rg_wx_fwd", "rg_wa_bwd", "rg_wx_bwd")):
        for n in range(8):
            o = 64 * (n % 2)
            bd[o:o + 64, w, n // 2, o:o + 64] = i[name][0, n]
    xor = np.arange(P)[:, None] ^ np.arange(P)[None, :]
    mask = np.stack([xor < w for w in (64, 32, 16, 8, 4, 2, 1)], axis=1).astype(np.float32)
    resets = np.ones((P, T), np.float32)
    resets[:, ::P] = 0.0
    return {
        "xt": np.ascontiguousarray(i["x"][0].T), "wu": np.ascontiguousarray(np.concatenate(units)),
        "wada": np.ascontiguousarray(wada), "vecs": np.ascontiguousarray(np.concatenate(vecs, axis=1)),
        "bd": bd, "consts": np.concatenate([np.eye(P, dtype=np.float32), resets, mask.reshape(P, 7 * P)], axis=1),
    }


def kernel(**inputs):
    import concourse.bacc as bacc
    from concourse.bass_utils import run_bass_kernel_spmd

    nc = bacc.Bacc("TRN2", target_bir_lowering=False, num_devices=1)
    arrays = layout(inputs)
    aps = [nc.dram_tensor(n, a.shape, mybir.dt.from_np(a.dtype), kind="ExternalInput").ap() for n, a in arrays.items()]
    out = nc.dram_tensor("out", (D, T), F32, kind="ExternalOutput").ap()
    build(nc, *aps, out)
    r = run_bass_kernel_spmd(nc, [arrays], core_ids=[0])
    return np.ascontiguousarray(r.results[0]["out"].T)[None]
```

```python
from contextlib import ExitStack

import numpy as np
import concourse.bass as bass
from concourse import mybir

F32 = mybir.dt.float32
F32R = mybir.dt.float32r
U8 = mybir.dt.uint8
ALU = mybir.AluOpType
ACT = mybir.ActivationFunctionType

P = 128
T = 512
D = 1024
FF = 2816
KD = D // P
KF = FF // P
TC = T // P
HEADS = 4
RT = 4
N_MOD = 9
EPS = 1e-6
UNIT = KD * P
HALF_UNITS = KF // 2
PAIR_UNITS = HALF_UNITS - 4
LEVELS = (64, 32, 16, 8, 4, 2, 1)

U_FFN1 = 0
U_MIX = U_FFN1 + 3 * KF
N_Z = 28
U_OUT = U_MIX + N_Z
U_FFN2 = U_OUT + 8
N_UNITS = U_FFN2 + 3 * KF
Z_UNITS = ([("v", 0), ("v", 1)] + [("rx", i) for i in range(4)] + [("v", 2), ("v", 3)]
           + [(w, 0) for w in "qfb"] + [("g", 0), ("g", 1)] + [(w, 1) for w in "qfb"] + [("g", 2), ("g", 3)]
           + [(w, 2) for w in "qfb"] + [("gate", 0), ("gate", 1)]
           + [(w, 3) for w in "qfb"] + [("gate", 2), ("gate", 3)])
EVACS = [sum(w != "v" for w, _ in Z_UNITS[:m + 1]) for m in range(len(Z_UNITS))]
TANH_MIN = -1.0 + 2.0 ** -24
OUT_BLOCKS = ([(k, o) for k in range(6) for o in range(4)] + [(k, o) for k in range(5) for o in (4, 5)]
              + [(k, o) for k in (6, 7) for o in range(4)] + [(k, o) for k in (5, 6, 7) for o in (4, 5)]
              + [(k, o) for o in (6, 7) for k in range(KD)])
Z_COLUMN = {"q": 0, "f": 512, "b": 1024, "v": 1536, "g": 2048, "rx": 2560, "gate": 3072}
MODS = ("sc1", "sh1", "g1", "sh2", "sc2", "g2", "sh3", "sc3", "g3")
MOD_AT = {"sh1": 0, "sc1": 1, "g1": 2, "sh2": 3, "sc2": 4, "g2": 5, "sh3": 6, "sc3": 7, "g3": 8}
VEC = {}
_at = 0
for _name, _n in (("c", 8), ("b_ada", 72), ("norm0", 8), ("norm1", 8), ("norm2", 8), ("norm3", 8),
                  ("lb", 16), ("hg_norm", 1), ("conv_w", 16), ("conv_b", 4), ("ba", 8), ("bx", 8), ("lam", 8)):
    VEC[_name] = _at
    _at += _n
N_VEC = _at


def build(nc, xt, wu, wada, vecs_in, bd_in, consts_in, out):
    with ExitStack() as ctx:
        place = [nc.sbuf_base + (-nc.sbuf_base) % 64]

        def at(name, shape, dt, offset):
            n = int(np.prod(shape[1:])) * (1 if dt == U8 else 4)
            return nc.alloc_sbuf_tensor_at(name, shape, dt, offset=offset), offset + (n + 63) // 64 * 64

        def sb(name, shape, dt=F32):
            t, place[0] = at(name, shape, dt, place[0])
            return t

        def sem(name):
            return ctx.enter_context(nc.semaphore(name))

        x = sb("x", [P, KD, T])
        h_at = place[0]
        hhi = sb("hhi", [P, KD, T], F32R)
        hlo = sb("hlo", [P, KD, T], F32R)
        raw = sb("raw", [P, 2, UNIT])
        whi = sb("whi", [P, 2, UNIT], F32R)
        wlo = sb("wlo", [P, 2, UNIT], F32R)
        vecs = sb("vecs", [P, N_VEC])
        ident = sb("ident", [P, P])
        ones = sb("ones", [P, P])
        epst = sb("epst", [P, 1])
        cs = sb("cs", [P, KD])
        mods = sb("mods", [P, N_MOD * KD])
        scale = sb("scale", [P, 3 * KD])
        gates = sb("gates", [P, 3 * KD])
        rms = sb("rms", [P, TC])
        rinv = sb("rinv", [P, TC])
        diag = sb("diag", [P, TC, P])
        tmp = sb("tmp", [P, 2, T])
        small = sb("small", [P, 136])
        sp4, nsp4 = small[:, 0:8], small[:, 8:16]
        lbm, omh = small[:, 16:24], small[:, 24:32]
        nomh, omk = small[:, 120:128], small[:, 128:136]
        half_b, half_gain = small[:, 56:72], small[:, 72:73]
        arena = place[0]
        off = arena
        ghi, off = at("ghi", [P, KF, T], F32R, off)
        glo, off = at("glo", [P, KF, T], F32R, off)
        sq, off = at("sq", [P, 4, T], F32, off)
        silu_sb, off = at("silu_sb", [P, T], F32, off)
        g32, off = at("g32", [P, T], F32, off)
        ada, off = at("ada", [P, 4, D], F32, off)
        acc, off = at("acc", [P, D], F32, off)
        fin, off = at("fin", [P, D], F32, off)
        outt, _ = at("outt", [P, KD, T], F32, arena)
        yhi, _ = at("yhi", [P, KD, T], F32R, h_at)
        ylo, _ = at("ylo", [P, KD, T], F32R, h_at + KD * T * 4)
        off = arena
        vn, off = at("vn", [P, TC, T], F32, off)
        pt, off = at("pt", [P, TC * TC, P], F32, off)
        w3, off = at("w3", [P, 2, 3, T], F32, off)
        cum, off = at("cum", [P, 2, 2, T], F32, off)
        dif, off = at("dif", [P, 2, 2, T], F32, off)
        dec, off = at("dec", [P, 2, 2, T], F32, off)
        qk, off = at("qk", [P, 2, 2, T], F32, off)
        lg, off = at("lg", [P, 2 * 517], F32, off)
        far, off = at("far", [P, 4, P], F32, off)
        tot, off = at("tot", [P, 2, TC], F32, off)
        etot, off = at("etot", [P, 2, 2, TC], F32, off)
        lgend, off = at("lgend", [P, TC], F32, off)
        masks, off = at("masks", [P, 7, P], U8, off)
        resets, off = at("resets", [P, T], F32, off)
        osb, osq = tmp[:, 0, :], tmp[:, 1, :]
        sg, off = at("sg", [P, HEADS, T], F32, off)
        xc, off = at("xc", [P, RT, T], F32, off)
        rxp, off = at("rxp", [P, RT, T + 4], F32, off)
        hr, _ = at("hr", [P, RT, T], F32, off - RT * (T + 4) * 4)
        gg, _ = at("gg", [P, RT, T], F32, off)
        ra, off = at("ra", [P, RT, T], F32, off)
        on, _ = at("on", [P, HEADS, T], F32, off)
        rt, off = at("rt", [P, RT, T], F32, off)
        ri, off = at("ri", [P, RT, T], F32, off)
        mask_f = dif[:].rearrange("p a l t -> p (a l t)")[:, 0:7 * P]
        a2 = tmp
        bd, off = at("bd", [P, 4, RT, P], F32, off)

        psum = ctx.enter_context(nc.psum_tensor("psum", [P, 8, T], F32))
        bank = [psum[:, b, :] for b in range(8)]
        modp = psum[:, 5, 0:8]

        def sums(n):
            return bank[(6, 6, 0, 6, 7)[n]][:, 0:TC]

        def rb(n):
            return bank[(7, 7, 1, 7, 7)[n]]

        vecs_loaded, x_loaded, mix_loaded = sem("vecs_loaded"), sem("x_loaded"), sem("mix_loaded")
        ada_first = [sem(f"ada_first{i}") for i in range(4)]
        ada_loaded = [sem(f"ada_loaded{i}") for i in range(4)]
        raw_loaded = [sem(f"raw_loaded{i}") for i in range(2)]
        hi_done, lo_done, unit_used = sem("hi_done"), sem("lo_done"), sem("unit_used")
        ones_set, cs_done, small_done = sem("ones_set"), sem("cs_done"), sem("small_done")
        ada_added, mod_summed, mod_ready = sem("ada_added"), sem("mod_summed"), sem("mod_ready")
        cols_ready = sem("cols_ready")
        sq_done, sq_added, sq_used = sem("sq_done"), sem("sq_added"), sem("sq_used")
        rms_done, rinv_done = sem("rms_done"), sem("rinv_done")
        diag_done, rb_done, htmp_done = sem("diag_done"), sem("rb_done"), sem("htmp_done")
        hhi_done, hlo_done = sem("hhi_done"), sem("hlo_done")
        zq_done, gelu_done = sem("zq_done"), sem("gelu_done")
        silu_done, gate_prod, ghi_done, glo_done = sem("silu_done"), sem("gate_prod"), sem("ghi_done"), sem("glo_done")
        x_ready, out_ready, stored = sem("x_ready"), sem("out_ready"), sem("stored")
        masks_set = sem("masks_set")
        v_copied, z_evac, rxp_zero = sem("v_copied"), sem("z_evac"), sem("rxp_zero")
        conv_step, xc_ready = sem("conv_step"), sem("xc_ready")
        gates_summed, gate_evac, tanh_done, a_done = sem("gates_summed"), sem("gate_evac"), sem("tanh_done"), sem("a_done")
        a2_done, one_a2, root_done = sem("a2_done"), sem("one_a2"), sem("root_done")
        rg_step, rg_scanned = sem("rg_step"), sem("rg_scanned")
        clamped, k_done, ln_done = sem("clamped"), sem("k_done"), sem("ln_done")
        cum_step, cum_ready, tot_ready, etot_done = sem("cum_step"), sem("cum_ready"), sem("tot_ready"), sem("etot_done")
        dif_done, dec_done, qk_done, far_done = sem("dif_done"), sem("dec_done"), sem("qk_done"), sem("far_done")
        scored, blk_copied, blk_masked = sem("scored"), sem("blk_copied"), sem("blk_masked")
        pv_done, osb_done, osq_done, osum_done = sem("pv_done"), sem("osb_done"), sem("osq_done"), sem("osum_done")
        orms_done, orinv_done, odiag_done, orb_done = sem("orms_done"), sem("orinv_done"), sem("odiag_done"), sem("orb_done")
        on_step, on_done, yrg_done, yhi_done, y_ready = (sem("on_step"), sem("on_done"), sem("yrg_done"),
                                                         sem("yhi_done"), sem("y_ready"))

        def vec(name, i=0, n=1):
            return vecs[:, VEC[name] + i:VEC[name] + i + n]

        def mod(name, i=0, n=1):
            m = MODS.index(name) * KD + i
            return mods[:, m:m + n]

        SHIFT = ("sh1", "sh2", "sh3")
        STEPS = 4 + len(LEVELS)
        STEPS_AT = ([[0], [1, 2]] + [[g + 1] for g in range(2, 10)],
                    [[0, 1], [2], [3, 4], [5, 6], [7], [8, 9], [10]])

        QG_COUNT = {z: 1 + sum(w in "qg" for w, _ in Z_UNITS[:m]) for m, z in enumerate(Z_UNITS) if z[0] in "qg"}

        def gate_bank(dr, ct):
            return 6 - 4 * (dr and ct % 2)

        def evac_wait(eng, h, s):
            if s < 4:
                eng.wait_ge(blk_copied, 4 * h + s + 1)
            else:
                eng.wait_ge(blk_masked, (STEPS - 4) * h + s - 3)

        def step_before(h, s, n):
            g = STEPS * h + s - n
            return (g // STEPS, g % STEPS) if g >= 0 else None

        block = ctx.enter_context(nc.Block())

        @block.sync
        def _(sp_):
            sp_.dma_start(vecs[:], vecs_in).then_inc(vecs_loaded, 16)
            sp_.dma_start(ident[:], consts_in[:, 0:P]).then_inc(vecs_loaded, 16)
            for k in range(4):
                sp_.dma_start(ada[:, k, :], wada[k]).then_inc(ada_first[k], 16)
            for i in range(2):
                n = KD // 2
                sp_.dma_start(x[:, n * i:n * i + n, :], xt[T * i:T * i + T].rearrange("(d p) t -> p d t", p=P)
                              ).then_inc(x_loaded, 16)
            for k in range(4, 16):
                sp_.wait_ge(ada_added, k - 3)
                sp_.dma_start(ada[:, k % 4, :], wada[k]).then_inc(ada_first[k % 4], 16)
            for u in range(2):
                sp_.dma_start(raw[:, u, :], wu[u]).then_inc(raw_loaded[u], 16)
            with sp_.Fori(1, N_UNITS // 2) as j:
                for s in range(2):
                    sp_.wait_ge(lo_done, 2 * j + (s - 1))
                    sp_.dma_start(raw[:, s, :], wu[bass.ds(2 * j + s, 1)].rearrange("a p n -> p (a n)")
                                  ).then_inc(raw_loaded[s], 16)
            for d in range(KD):
                sp_.wait_ge(out_ready, d + 1)
                sp_.dma_start(out[d * P:(d + 1) * P, :], outt[:, d, :]).then_inc(stored, 16)
            sp_.wait_ge(stored, 16 * KD)

        @block.gpsimd
        def _(pool):
            def add_squares(n, part):
                if part == 0:
                    pool.wait_ge(sq_done, KD * n + 4)
                    nc.gpsimd.tensor_tensor(sq[:, 0:2, :], sq[:, 0:2, :], sq[:, 2:4, :], ALU.add).then_inc(sq_added, 1)
                    pool.wait_ge(sq_added, 4 * n + 1)
                    nc.gpsimd.tensor_tensor(sq[:, 0, :], sq[:, 0, :], sq[:, 1, :], ALU.add).then_inc(sq_added, 1)
                else:
                    pool.wait_ge(sq_done, KD * n + 6)
                    nc.gpsimd.tensor_tensor(sq[:, 0, :], sq[:, 0, :], sq[:, 1, :], ALU.add).then_inc(sq_added, 1)
                    pool.wait_ge(sq_done, KD * n + 7)
                    pool.wait_ge(sq_added, 4 * n + 3)
                    nc.gpsimd.tensor_tensor(sq[:, 0, :], sq[:, 0, :], sq[:, 2, :], ALU.add).then_inc(sq_added, 1)

            add_squares(0, 0)
            add_squares(0, 1)
            for k in range(8):
                pool.wait_ge(ada_added, 13 + k)
                pool.dma_start(ada[:, k % 4, :], wada[16 + k]).then_inc(ada_loaded[k % 4], 16)
                if k == 3:
                    for u in range(2):
                        pool.wait_ge(hi_done, u + 1)
                        nc.gpsimd.tensor_tensor(wlo[:, u, :], raw[:, u, :], whi[:, u, :], ALU.subtract
                                                ).then_inc(lo_done, 1)
            with pool.Fori(3, N_MOD) as j:
                for k in range(8):
                    pool.wait_ge(ada_added, 8 * j + (k - 3))
                    pool.dma_start(ada[:, k % 4, :], wada[bass.ds(8 * j + k, 1)].rearrange("a p n -> p (a n)")
                                   ).then_inc(ada_loaded[k % 4], 16)
            add_squares(1, 0)
            add_squares(1, 1)
            pool.wait_ge(unit_used, U_MIX)
            pool.wait_ge(sq_used, 3 * 2)
            pool.dma_start(bd[:], bd_in).then_inc(mix_loaded, 16)
            pool.dma_start(mask_f, consts_in[:, P + T:P + T + 7 * P]).then_inc(mix_loaded, 16)
            pool.dma_start(resets[:], consts_in[:, P:P + T]).then_inc(mix_loaded, 16)

            def square_a(dr, ct):
                gi = RT * dr + ct
                pool.wait_ge(a_done, gi + 1)
                if gi >= 2:
                    pool.wait_ge(one_a2, gi - 1)
                nc.gpsimd.tensor_tensor(a2[:, ct % 2, :], ra[:, ct, :], ra[:, ct, :], ALU.mult).then_inc(a2_done, 1)

            for ct in range(RT):
                square_a(0, ct)
            pool.wait_ge(masks_set, 1)
            for h in range(HEADS):
                p = h % 2
                pool.wait_ge(tot_ready, 2 * (h + 1))
                if h:
                    pool.wait_ge(dec_done, 9 * h)
                nc.gpsimd.tensor_tensor(dif[:, 1].rearrange("p l (c t) -> p l c t", c=TC),
                                        tot[:].unsqueeze(3).broadcast_to([P, 2, TC, P]),
                                        cum[:, p].rearrange("p l (c t) -> p l c t", c=TC),
                                        ALU.subtract).then_inc(dif_done, 1)
                for i, hw in enumerate(LEVELS):
                    e = i + 2
                    if e > 2:
                        pool.wait_ge(dec_done, 9 * h + e - 1)
                    c5 = cum[:, p].rearrange("p l (n two w) -> p l n two w", two=2, w=hw)
                    d5 = dif[:, e % 2].rearrange("p l (n two w) -> p l n two w", two=2, w=hw)
                    ref = c5[:, :, :, 1, 0:1].broadcast_to([P, 2, T // (2 * hw), hw])
                    nc.gpsimd.tensor_tensor(d5[:, :, :, 1, :], c5[:, :, :, 1, :], ref, ALU.subtract)
                    nc.gpsimd.tensor_tensor(d5[:, :, :, 0, :], ref, c5[:, :, :, 0, :],
                                            ALU.subtract).then_inc(dif_done, 1)
                    if h == 0 and e >= 7:
                        square_a(1, e - 7)
                if h == 0:
                    square_a(1, 2)
                    square_a(1, 3)
            for n in (2, 3):
                add_squares(n, 0)
                add_squares(n, 1)

        @block.scalar
        def _(act):
            def hi(j, slot):
                act.wait_ge(raw_loaded[slot], 16 * (j + 1))
                if not (isinstance(j, int) and j == 0):
                    act.wait_ge(unit_used, 2 * j + (slot - 1))
                nc.scalar.activation(whi[:, slot, :], raw[:, slot, :], ACT.Copy).then_inc(hi_done, 1)

            def hi_u(u):
                if u < N_UNITS:
                    hi(u // 2, u % 2)

            def square(n, d):
                if n == 0:
                    act.wait_ge(x_loaded, 16 * 2)
                else:
                    act.wait_ge(x_ready, KD * (n - 1) + d + 1)
                if d >= 4:
                    act.wait_ge(sq_used, 3 * n + 1)
                elif n:
                    act.wait_ge(sq_used, 3 * n)
                nc.scalar.activation(sq[:, d % 4, :], x[:, d, :], ACT.Square).then_inc(sq_done, 1)

            def root(n):
                act.wait_ge(sq_used, 3 * (n + 1))
                nc.scalar.activation(rms[:], sums(n), ACT.Sqrt, bias=epst[:], scale=1.0 / D).then_inc(rms_done, 1)

            def h_upper(n):
                if n == 0:
                    act.wait_ge(mod_ready, 2)
                for d in range(KD):
                    act.wait_ge(htmp_done, KD * n + d + 1)
                    nc.scalar.activation(hhi[:, d, :], tmp[:, d % 2, :], ACT.Identity,
                                         bias=mod(SHIFT[n], d)).then_inc(hhi_done, 1)

            def up_step(n, f, fp, i):
                j = (U_FFN1, U_FFN2)[n] // 2 + 2 * i + fp
                hi(j + 1, 0)
                act.wait_ge(unit_used, 2 * j + 1)
                if not (isinstance(f, int) and KF * n + f == 0):
                    act.wait_ge(gate_prod, f + KF * n)
                nc.scalar.activation(silu_sb[:], bank[fp], ACT.Silu).then_inc(silu_done, 1)
                hi(j + 1, 1)
                act.wait_ge(gate_prod, f + (KF * n + 1))
                nc.scalar.activation(ghi[:, bass.ds(f, 1), :].rearrange("p a t -> p (a t)"), g32[:],
                                     ACT.Copy).then_inc(ghi_done, 1)

            def ffn_up(n):
                for fp in range(2):
                    up_step(n, fp, fp, 0)
                nc.scalar.preload_act_table(ACT.Silu)
                with act.Fori(1, KF // 2) as i:
                    for fp in range(2):
                        up_step(n, 2 * i + fp, fp, i)

            def ffn_down(n):
                norm = (1, 3)[n]
                u0 = (U_FFN1, U_FFN2)[n] + 2 * KF
                nc.scalar.preload_act_table(ACT.Sqrt)
                for half in range(2):
                    u = u0 + HALF_UNITS * half
                    hi_u(u + 2)
                    if half:
                        for d in range(4):
                            square(norm, d)
                    with act.Fori(0, (PAIR_UNITS if half else HALF_UNITS - 1) // 2) as i:
                        for s in range(2):
                            v = u + 3 + s
                            hi(i + v // 2, v % 2)
                for d in range(4, KD):
                    if d < 7:
                        hi_u(u + PAIR_UNITS + d - 2)
                    square(norm, d)
                root(norm)
                hi_u(u + HALF_UNITS + 1)

            act.wait_ge(vecs_loaded, 32)
            nc.scalar.activation(cs[:], vec("c", 0, 8), ACT.Silu).then_inc(cs_done, 1)
            act.wait_ge(small_done, 1)
            nc.scalar.activation(small[:, 32:40], small[:, 32:40], ACT.Exp).then_inc(cs_done, 1)
            nc.scalar.activation(small[:, 40:56], small[:, 40:56], ACT.Exp).then_inc(cs_done, 1)
            nc.scalar.preload_act_table(ACT.Sqrt)
            for d in range(KD):
                square(0, d)
            act.wait_ge(ones_set, 2)
            root(0)
            hi(0, 0)
            hi(0, 1)
            h_upper(0)
            ffn_up(0)
            ffn_down(0)
            h_upper(1)

            zi = {u: m for m, u in enumerate(Z_UNITS)}

            def z_bank(m):
                act.wait_ge(unit_used, U_MIX + m + 1)
                return bank[m % 2]

            def z_post(m):
                what, i = Z_UNITS[m]
                hi_u(U_MIX + m + 2)
                if what == "v":
                    if i == 3:
                        act.wait_ge(unit_used, U_MIX + m + 1)
                        for c in range(TC):
                            nc.scalar.activation(vn[:, c, :], bank[2 + c], ACT.Copy, scale=0.5).then_inc(v_copied, 1)
                    return
                src = z_bank(m)
                if what == "rx":
                    nc.scalar.activation(rxp[:, i, 2:2 + T], src, ACT.Copy).then_inc(z_evac, 1)
                elif what == "g":
                    nc.scalar.activation(sg[:, i, :], src, ACT.Tanh, scale=0.5).then_inc(z_evac, 1)
                elif what == "gate":
                    act.wait_ge(rg_scanned, RT + i + 1)
                    nc.scalar.activation(gg[:, i, :], src, ACT.Copy).then_inc(z_evac, 1)
                else:
                    if what == "q" and i >= 2:
                        act.wait_ge(qk_done, 10 * (i - 1))
                        act.wait_ge(scored, STEPS * (i - 1))
                    slot = {"f": 0, "q": 1, "b": 2}[what]
                    nc.scalar.activation(w3[:, i % 2, slot, :], src, ACT.Tanh, scale=0.5).then_inc(z_evac, 1)

            def logs(h):
                if h:
                    act.wait_ge(cum_ready, 2 * h)
                for lane in range(2):
                    c = 4 * lane + h
                    act.wait_ge(clamped, 2 * h + lane + 1)
                    nc.scalar.activation(lg[:, 517 * lane:517 * lane + T], w3[:, h % 2, 2 * lane, :], ACT.Ln,
                                         bias=lbm[:, c:c + 1], scale=omh[:, c:c + 1]).then_inc(ln_done, 1)
                for lane in range(2):
                    c = 4 * lane + h
                    act.wait_ge(ln_done, 2 * h + lane + 1)
                    k = w3[:, h % 2, 2 * lane, :]
                    nc.scalar.activation(k, k, ACT.Identity, bias=omk[:, c:c + 1],
                                         scale=nomh[:, c:c + 1]).then_inc(k_done, 1)

            def gate_post(dr, ct):
                gi = RT * dr + ct
                act.wait_ge(gates_summed, gi + 1)
                if dr:
                    act.wait_ge(rg_scanned, ct + 1)
                nc.scalar.activation(ra[:, ct, :], bank[gate_bank(dr, ct)], ACT.Tanh, bias=half_b[:, gi:gi + 1],
                                     scale=0.5).then_inc(gate_evac, 1)
                nc.scalar.activation(ri[:, ct, :], bank[gate_bank(dr, ct) + 1], ACT.Tanh, bias=half_b[:, 8 + gi:9 + gi],
                                     scale=0.5).then_inc(gate_evac, 1)
                act.wait_ge(gate_evac, 2 * gi + 1)
                nc.scalar.activation(rt[:, ct, :], ra[:, ct, :], ACT.Tanh, bias=sp4[:, gi:gi + 1],
                                     scale=sp4[:, gi:gi + 1]).then_inc(tanh_done, 1)

            def rg_exp(dr, ct):
                gi = RT * dr + ct
                act.wait_ge(tanh_done, gi + 1)
                nc.scalar.activation(ra[:, ct, :], ra[:, ct, :], ACT.Exp, bias=nsp4[:, gi:gi + 1],
                                     scale=nsp4[:, gi:gi + 1]).then_inc(a_done, 1)

            def rg_root(dr):
                for ct in range(RT):
                    act.wait_ge(one_a2, RT * dr + ct + 1)
                    nc.scalar.activation(rt[:, ct, :], rt[:, ct, :], ACT.Sqrt).then_inc(root_done, 1)

            def decay(h, e):
                if e >= 2:
                    act.wait_ge(qk_done, 10 * h + e - 1)
                elif h:
                    act.wait_ge(qk_done, 10 * (h - 1) + 9)
                if e == 0:
                    act.wait_ge(tot_ready, 2 * (h + 1))
                    if h:
                        act.wait_ge(far_done, h)
                    nc.scalar.activation(etot[:, h % 2], tot[:], ACT.Exp).then_inc(etot_done, 1)
                    nc.scalar.activation(dec[:, 0], cum[:, h % 2], ACT.Exp).then_inc(dec_done, 1)
                else:
                    act.wait_ge(dif_done, 8 * h + e)
                    nc.scalar.activation(dec[:, e % 2], dif[:, e % 2], ACT.Exp).then_inc(dec_done, 1)

            def block_copy(h, s):
                act.wait_ge(scored, STEPS * h + s + 1)
                if s == 0 and h:
                    act.wait_ge(pv_done, h)
                src = bank[4 + (STEPS * h + s) % 2]
                if s == 0:
                    nc.scalar.activation(pt[:, 1:5:3, :], src[:, 0:256].rearrange("p (b t) -> p b t", b=2), ACT.Copy)
                    nc.scalar.activation(pt[:, 11:15:3, :], src[:, 256:512].rearrange("p (b t) -> p b t", b=2),
                                         ACT.Copy).then_inc(blk_copied, 1)
                else:
                    p4 = pt[:].rearrange("p (a b) t -> p a b t", a=TC)
                    dst = {1: p4[:, 0:2, 2:4, :], 2: p4[:, 2:4, 0:2, :], 3: pt[:, 0:16:5, :]}[s]
                    src = (src.rearrange("p (b t) -> p b t", b=4) if s == 3
                           else src.rearrange("p (a b t) -> p a b t", a=2, b=2))
                    nc.scalar.activation(dst, src, ACT.Copy).then_inc(blk_copied, 1)

            def o_copy(h):
                act.wait_ge(pv_done, h + 1)
                if h == 0:
                    act.wait_ge(one_a2, 2 * RT)
                if h:
                    act.wait_ge(on_done, h)
                    act.wait_ge(osum_done, h)
                nc.scalar.activation(osb, bank[6], ACT.Copy).then_inc(osb_done, 1)
                nc.scalar.activation(osq, bank[6], ACT.Square).then_inc(osq_done, 1)

            def o_root(h):
                act.wait_ge(osum_done, h + 1)
                nc.scalar.activation(rms[:], sums(4), ACT.Sqrt, bias=epst[:],
                                     scale=1.0 / P).then_inc(orms_done, 1)

            def gelu(k):
                act.wait_ge(z_evac, EVACS[zi[("gate", k)]])
                nc.scalar.activation(gg[:, k, :], gg[:, k, :], ACT.Gelu_apprx_tanh).then_inc(gelu_done, 1)

            def y_upper(k):
                if k < RT:
                    act.wait_ge(yrg_done, k + 1)
                else:
                    act.wait_ge(on_done, k - 3)
                act.wait_ge(unit_used, U_OUT)
                src = hr[:, k, :] if k < RT else on[:, k - RT, :]
                nc.scalar.activation(yhi[:, k, :], src, ACT.Copy).then_inc(yhi_done, 1)

            for m in range(5):
                z_post(m)
            act.wait_ge(small_done, 2)
            gate_post(0, 0)
            for ct in range(1, RT):
                z_post(4 + ct)
                gate_post(0, ct)
                rg_exp(0, ct - 1)
            z_post(8)
            rg_exp(0, 3)
            rg_root(0)
            z_post(9)
            z_post(10)
            logs(0)
            z_post(11)
            decay(0, 0)
            decay(0, 1)
            z_post(12)
            for r in range(HEADS):
                first = zi[("q", r + 1)] if r < 3 else None
                if r == 3:
                    y_upper(0)
                    y_upper(1)
                decay(r, 2)
                if r == 3:
                    gelu(2)
                    gelu(3)
                for g, steps in enumerate(STEPS_AT[r == 3]):
                    for s in steps:
                        if 3 <= s + 1 <= 8:
                            decay(r, s + 1)
                        if s < 4:
                            block_copy(r, s)
                    if r and g == 0:
                        o_copy(r - 1)
                    if r == 3 and g == 5:
                        nc.scalar.preload_act_table(ACT.Sqrt)
                    if r and g == (5 if r == 3 else 4):
                        o_root(r - 1)
                    if r == 1 and g == 4:
                        rg_root(1)
                    if r == 2 and g == 1:
                        gelu(0)
                        gelu(1)
                    if r < 3:
                        if g == 9:
                            decay(r + 1, 0)
                            decay(r + 1, 1)
                        if g % 2:
                            z_post(first + g // 2)
                        if g == 6:
                            logs(r + 1)
                    if r == 0 and 4 <= g < 8:
                        gate_post(1, g - 4)
                        rg_exp(1, g - 4)
                    if r == 3:
                        if g and g % 2 == 0:
                            hi_u(U_OUT + g // 2 + 1)
                        if g == 1:
                            y_upper(2)
                            y_upper(3)
                        if g == 2:
                            y_upper(4)
                            y_upper(5)
            o_copy(3)
            y_upper(6)
            o_root(3)
            hi_u(U_OUT + 5)
            y_upper(7)
            for d in range(KD):
                if d in (0, 2, 4):
                    hi_u(U_OUT + 6 + d // 2)
                square(2, d)
            root(2)
            hi_u(U_OUT + 9)
            h_upper(2)
            ffn_up(1)
            ffn_down(1)

        @block.vector
        def _(dve):
            def lo(j, slot):
                dve.wait_ge(hi_done, 2 * j + (slot + 1))
                nc.vector.tensor_tensor(wlo[:, slot, :], raw[:, slot, :], whi[:, slot, :],
                                        ALU.subtract).then_inc(lo_done, 1)

            def lo_u(u):
                if u < N_UNITS:
                    lo(u // 2, u % 2)

            def ada_add(j, k):
                if isinstance(j, int) and j < 2:
                    dve.wait_ge(ada_first[k % 4], 32 * j + 16 * (k // 4 + 1))
                else:
                    dve.wait_ge(ada_loaded[k % 4], 32 * j + (16 * (k // 4 + 1) - 64))
                if not (isinstance(j, int) and j == 0 and k == 0):
                    dve.wait_ge(ada_added, 8 * j + k)
                dst = acc
                if k == 7:
                    dst = fin
                    if not (isinstance(j, int) and j == 0):
                        dve.wait_ge(mod_summed, 1 * j)
                if k == 0:
                    nc.vector.tensor_scalar(dst[:], ada[:, k % 4, :], cs[:, k:k + 1], None,
                                            ALU.mult).then_inc(ada_added, 1)
                else:
                    nc.vector.scalar_tensor_tensor(dst[:], ada[:, k % 4, :], cs[:, k:k + 1], acc[:], ALU.mult,
                                                   ALU.add).then_inc(ada_added, 1)

            def mod_bias(j):
                dve.wait_ge(mod_summed, j + 1)
                nc.vector.tensor_tensor(mods[:, bass.ds(8 * j, 8)], modp, vecs[:, bass.ds(8 * j + VEC["b_ada"], 8)],
                                        ALU.add).then_inc(mod_ready, 1)

            def rms_inverse(n, done, r_done, d_done):
                dve.wait_ge(done, n + 1)
                nc.vector.reciprocal(rinv[:], rms[:]).then_inc(r_done, 1)
                dve.wait_ge(r_done, n + 1)
                nc.vector.tensor_tensor(diag[:], ident[:].unsqueeze(1).broadcast_to([P, TC, P]),
                                        rinv[:].unsqueeze(2).broadcast_to([P, TC, P]), ALU.mult).then_inc(d_done, 1)

            def h_split(n):
                dve.wait_ge(rb_done, n + 1)
                dve.wait_ge(cols_ready, 2 * n + 1)
                for d in range(KD + 1):
                    if n == 0 and d == 1:
                        mod_bias(1)
                        dve.wait_ge(mod_ready, 2)
                    if d < KD:
                        if d >= 2:
                            dve.wait_ge(hlo_done, KD * n + d - 1)
                        nc.vector.scalar_tensor_tensor(tmp[:, d % 2, :], x[:, d, :], scale[:, KD * n + d:KD * n + d + 1],
                                                       rb(n), ALU.mult, ALU.mult).then_inc(htmp_done, 1)
                    if d:
                        dve.wait_ge(hhi_done, KD * n + d)
                        nc.vector.scalar_tensor_tensor(hlo[:, d - 1, :], tmp[:, (d - 1) % 2, :], mod(SHIFT[n], d - 1),
                                                       hhi[:, d - 1, :], ALU.add, ALU.subtract).then_inc(hlo_done, 1)

            def up_step(n, f, fp, i, mod_j=None):
                j = (U_FFN1, U_FFN2)[n] // 2 + 2 * i + fp
                ks = range(4 * fp, 4 * fp + 4) if mod_j is not None else ()
                lo(j + 1, 0)
                for k in ks[0:2]:
                    ada_add(mod_j, k)
                dve.wait_ge(unit_used, 2 * j + 2)
                dve.wait_ge(silu_done, f + (KF * n + 1))
                if not (isinstance(f, int) and KF * n + f == 0):
                    dve.wait_ge(glo_done, f + KF * n)
                nc.vector.tensor_tensor(g32[:], silu_sb[:], bank[2 + fp], ALU.mult).then_inc(gate_prod, 1)
                lo(j + 1, 1)
                dve.wait_ge(ghi_done, f + (KF * n + 1))
                nc.vector.tensor_tensor(glo[:, bass.ds(f, 1), :].rearrange("p a t -> p (a t)"), g32[:],
                                        ghi[:, bass.ds(f, 1), :].rearrange("p a t -> p (a t)"),
                                        ALU.subtract).then_inc(glo_done, 1)
                for k in ks[2:4]:
                    ada_add(mod_j, k)

            def update(n, d, src):
                if n == 1:
                    dve.wait_ge(unit_used, U_OUT + max(OUT_BLOCKS.index((KD - 1, d)) // 8 + 1, 5 + (d > 1)))
                else:
                    dve.wait_ge(unit_used, (U_FFN1, U_FFN2)[n // 2] + 2 * KF + HALF_UNITS
                                + (0 if d < 4 else PAIR_UNITS + d - 3))
                nc.vector.scalar_tensor_tensor(x[:, d, :], src, gates[:, KD * n + d:KD * n + d + 1], x[:, d, :],
                                               ALU.mult, ALU.add).then_inc(x_ready, 1)

            def columns(n):
                g, sc = ("g1", "g2", "g3")[n], ("sc2", "sc3")[n] if n < 2 else None
                dve.wait_ge(mod_ready, N_MOD)
                nc.vector.tensor_scalar(gates[:, KD * n:KD * n + KD], mod(g, 0, KD), (0.5, 1.0, 0.5)[n], None,
                                        ALU.mult).then_inc(cols_ready, 1)
                if sc:
                    nc.vector.scalar_tensor_tensor(scale[:, KD * (n + 1):KD * (n + 2)], mod(sc, 0, KD), 1.0,
                                                   vec(f"norm{n + 1}", 0, KD), ALU.add, ALU.mult).then_inc(cols_ready, 1)

            def ffn_down(n):
                branch, u0 = (0, 2)[n], (U_FFN1, U_FFN2)[n] + 2 * KF
                columns(branch)
                dve.wait_ge(cols_ready, (3, 6)[n])
                for half in range(2):
                    u = u0 + HALF_UNITS * half
                    lo_u(u + 2)
                    if n == 0 and half == 0:
                        small_values()
                    if half:
                        for d in range(4):
                            update(branch, d, bank[4 + d])
                    with dve.Fori(0, (PAIR_UNITS if half else HALF_UNITS - 1) // 2) as i:
                        for s in range(2):
                            v = u + 3 + s
                            lo(i + v // 2, v % 2)
                for d in range(4, KD):
                    if d < 7:
                        lo_u(u + PAIR_UNITS + d - 2)
                    update(branch, d, bank[d - 4])
                rms_inverse((1, 3)[n], rms_done, rinv_done, diag_done)
                lo_u(u + HALF_UNITS + 1)

            nc.vector.memset(ones[:], 1.0).then_inc(ones_set, 1)
            nc.vector.memset(epst[:], EPS).then_inc(ones_set, 1)
            dve.wait_ge(vecs_loaded, 32)
            chain = [0]

            def step(ins):
                chain[0] += 1
                ins.then_inc(cum_step, 1)
                dve.wait_ge(cum_step, chain[0])

            lam, y_, ym, s_, s2, q_ = (small[:, 8 * i:8 * i + 8] for i in (10, 4, 11, 12, 13, 14))
            lb_e, t8, t9 = small[:, 40:56], small[:, 120:128], small[:, 128:136]
            step(nc.vector.tensor_scalar(lam, vec("lam", 0, 8), -1.0, None, ALU.mult))
            step(nc.vector.tensor_tensor(y_, lam, vec("lam", 0, 8), ALU.min))
            lb0, lb1 = vec("lb", 0, 8), vec("lb", 8, 8)
            step(nc.vector.tensor_tensor(t8, lb0, lb1, ALU.max))
            step(nc.vector.tensor_tensor(lb_e[:, 0:8], lb0, t8, ALU.subtract))
            nc.vector.tensor_tensor(lb_e[:, 8:16], lb1, t8, ALU.subtract).then_inc(small_done, 1)
            def small_values():
                dve.wait_ge(cs_done, 3)
                step(nc.vector.tensor_scalar(ym, y_, 2.0, None, ALU.add))
                step(nc.vector.reciprocal(s_, ym))
                step(nc.vector.tensor_tensor(s_, s_, y_, ALU.mult))
                step(nc.vector.tensor_tensor(s2, s_, s_, ALU.mult))
                step(nc.vector.tensor_scalar(q_, s2, 1.0 / 17, None, ALU.mult))
                for o in (15, 13, 11, 9, 7, 5, 3):
                    step(nc.vector.scalar_tensor_tensor(q_, q_, 1.0 / o, s2, ALU.add, ALU.mult))
                step(nc.vector.scalar_tensor_tensor(q_, q_, 1.0, s_, ALU.add, ALU.mult))
                step(nc.vector.tensor_scalar(lam, lam, 0.0, None, ALU.max))
                step(nc.vector.scalar_tensor_tensor(q_, q_, 2.0, lam, ALU.mult, ALU.add))
                step(nc.vector.tensor_scalar(nsp4, q_, -4.0, None, ALU.mult))
                step(nc.vector.tensor_scalar(sp4, q_, 4.0, None, ALU.mult))
                step(nc.vector.tensor_scalar(half_b, vec("ba", 0, 16), 0.5, None, ALU.mult))
                step(nc.vector.tensor_scalar(half_gain, vec("hg_norm"), 0.5, None, ALU.mult))
                step(nc.vector.tensor_tensor(t8, lb_e[:, 0:8], lb_e[:, 8:16], ALU.add))
                step(nc.vector.reciprocal(t8, t8))
                step(nc.vector.tensor_tensor(lb_e[:, 0:8], lb_e[:, 0:8], t8, ALU.mult))
                step(nc.vector.tensor_tensor(lb_e[:, 8:16], lb_e[:, 8:16], t8, ALU.mult))
                step(nc.vector.tensor_tensor(t9, lb_e[:, 0:8], lb_e[:, 8:16], ALU.add))
                step(nc.vector.tensor_tensor(t9, t9, lb_e[:, 0:8], ALU.subtract))
                step(nc.vector.tensor_scalar(omh, t9, -0.5, 0.5, ALU.mult, ALU.add))
                step(nc.vector.tensor_tensor(lbm, t9, omh, ALU.add))
                nc.vector.tensor_scalar(nomh, omh, -1.0, None, ALU.mult)
                nc.vector.tensor_scalar(omk, lbm, -1.0, 1.0, ALU.mult, ALU.add).then_inc(small_done, 1)

            dve.wait_ge(cs_done, 1)
            for k in range(8):
                ada_add(0, k)
            for k in range(8):
                ada_add(1, k)
                if k == 3:
                    mod_bias(0)
                if k == 4:
                    rms_inverse(0, rms_done, rinv_done, diag_done)
            dve.wait_ge(mod_ready, 1)
            nc.vector.scalar_tensor_tensor(scale[:, 0:KD], mod("sc1", 0, KD), 1.0, vec("norm0", 0, KD), ALU.add,
                                           ALU.mult).then_inc(cols_ready, 1)
            h_split(0)
            for fp in range(2):
                up_step(0, fp, fp, 0, 2)
            with dve.Fori(1, 7) as i:
                for fp in range(2):
                    up_step(0, 2 * i + fp, fp, i, i + 2)
                mod_bias(i + 1)
            for fp in range(2):
                up_step(0, 14 + fp, fp, 7)
            mod_bias(8)
            with dve.Fori(8, KF // 2) as i:
                for fp in range(2):
                    up_step(0, 2 * i + fp, fp, i)
            ffn_down(0)
            h_split(1)

            zi = {u: m for m, u in enumerate(Z_UNITS)}
            nc.vector.memset(rxp[:, :, 0:2], 0.0).then_inc(rxp_zero, 1)
            nc.vector.memset(rxp[:, :, 2 + T:4 + T], 0.0).then_inc(rxp_zero, 1)

            conv = [0]

            def convolve(ct):
                dve.wait_ge(z_evac, ct + 1)
                dve.wait_ge(rxp_zero, 2)
                for j in range(4):
                    tap = vec("conv_w", 4 * j + ct)
                    src = rxp[:, ct, j:j + T]
                    if j == 0:
                        ins = nc.vector.tensor_scalar(xc[:, ct, :], src, tap, vec("conv_b", ct), ALU.mult, ALU.add)
                    else:
                        ins = nc.vector.scalar_tensor_tensor(xc[:, ct, :], src, tap, xc[:, ct, :], ALU.mult, ALU.add)
                    if j < 3:
                        conv[0] += 1
                        ins.then_inc(conv_step, 1)
                        dve.wait_ge(conv_step, conv[0])
                ins.then_inc(xc_ready, 1)

            def one_minus_a2(dr, ct):
                dve.wait_ge(a2_done, RT * dr + ct + 1)
                nc.vector.scalar_tensor_tensor(rt[:, ct, :], a2[:, ct % 2, :], 1.0, rt[:, ct, :], ALU.add,
                                               ALU.mult).then_inc(one_a2, 1)

            rg = [0]

            def recur(dr, ct):
                def rstep(ins):
                    rg[0] += 1
                    ins.then_inc(rg_step, 1)
                    dve.wait_ge(rg_step, rg[0])
                rstep(nc.vector.scalar_tensor_tensor(ri[:, ct, :], ri[:, ct, :], 1.0, xc[:, ct, :], ALU.add, ALU.mult))
                dve.wait_ge(root_done, RT * dr + ct + 1)
                rstep(nc.vector.tensor_tensor(ri[:, ct, :], ri[:, ct, :], rt[:, ct, :], ALU.mult))
                if dr == 0:
                    nc.vector.tensor_tensor_scan(hr[:, ct, :], ra[:, ct, :], ri[:, ct, :], 0.0, ALU.mult,
                                                 ALU.add).then_inc(rg_scanned, 1)
                else:
                    rstep(nc.vector.tensor_tensor_scan(rt[:, ct, ::-1], ra[:, ct, ::-1], ri[:, ct, ::-1], 0.0, ALU.mult,
                                                       ALU.add))
                    nc.vector.tensor_tensor(hr[:, ct, :], hr[:, ct, :], rt[:, ct, :], ALU.add).then_inc(rg_scanned, 1)

            def z_post(m):
                what, i = Z_UNITS[m]
                lo_u(U_MIX + m + 2)
                if what in "qg":
                    dst = w3[:, i % 2, 1, :] if what == "q" else sg[:, i, :]
                    dve.wait_ge(z_evac, EVACS[m])
                    nc.vector.scalar_tensor_tensor(dst, dst, 1.0, bank[m % 2], ALU.add, ALU.mult).then_inc(zq_done, 1)
                if what in "fb":
                    t = w3[:, i % 2, 2 * "fb".index(what), :]
                    dve.wait_ge(z_evac, EVACS[m])
                    nc.vector.tensor_scalar(t, t, TANH_MIN, None, ALU.max).then_inc(clamped, 1)

            def sum_logs(h):
                p = h % 2
                dve.wait_ge(ln_done, 2 * h + 2)
                if h >= 1:
                    dve.wait_ge(dif_done, 8 * (h - 1) + 1)
                    dve.wait_ge(etot_done, h)
                if h >= 2:
                    dve.wait_ge(dec_done, 9 * (h - 1))
                late = lg[:, 516:516 + T + 1]
                step(nc.vector.tensor_copy(lgend[:], late[:, P:T + 1:P]))
                step(nc.vector.memset(late[:, 0:T:P], 0.0))
                nc.vector.tensor_tensor_scan(cum[:, p, 0, :], resets[:], lg[:, 0:T], 0.0, ALU.mult,
                                             ALU.add).then_inc(cum_ready, 1)
                nc.vector.tensor_tensor_scan(cum[:, p, 1, :], resets[:], late[:, 0:T], 0.0, ALU.mult,
                                             ALU.add).then_inc(cum_ready, 1)
                dve.wait_ge(cum_ready, 2 * h + 2)
                nc.vector.tensor_copy(tot[:, 0, :], cum[:, p, 0, P - 1:T:P]).then_inc(tot_ready, 1)
                nc.vector.tensor_tensor(tot[:, 1, :], cum[:, p, 1, P - 1:T:P], lgend[:], ALU.add).then_inc(tot_ready, 1)

            def decayed(h, e):
                p = h % 2
                if e in (0, 1) and h:
                    dve.wait_ge(scored, STEPS * (h - 1) + 10 + e)
                elif e in (2, 3):
                    dve.wait_ge(scored, STEPS * h + 3)
                elif e >= 4:
                    dve.wait_ge(scored, STEPS * h + e)
                if e < 9:
                    dve.wait_ge(dec_done, 9 * h + e + 1)
                if e < 2:
                    if e == 0:
                        dve.wait_ge(k_done, 2 * h + 2)
                        dve.wait_ge(zq_done, QG_COUNT[("q", h)])
                    nc.vector.tensor_tensor(qk[:, e], dec[:, e], w3[:, p, 1 - e:3 - e, :], ALU.mult).then_inc(qk_done, 1)
                elif e < 9:
                    hw = LEVELS[e - 2]
                    q5 = qk[:, e % 2].rearrange("p l (n two w) -> p l n two w", two=2, w=hw)
                    d5 = dec[:, e % 2].rearrange("p l (n two w) -> p l n two w", two=2, w=hw)
                    w5 = w3[:, p].rearrange("p l (n two w) -> p l n two w", two=2, w=hw)
                    nc.vector.tensor_tensor(q5[:, :, :, 1, :], d5[:, :, :, 1, :], w5[:, 1:3, :, 1, :], ALU.mult)
                    nc.vector.tensor_tensor(q5[:, ::-1, :, 0, :], d5[:, :, :, 0, :], w5[:, 0:2, :, 0, :],
                                            ALU.mult).then_inc(qk_done, 1)
                else:
                    nc.vector.tensor_tensor(qk[:, 1, 1, :], w3[:, p, 0, :], w3[:, p, 2, :], ALU.add).then_inc(qk_done, 1)

            def decay_far(h):
                dve.wait_ge(qk_done, 10 * h + 2)
                dve.wait_ge(etot_done, h + 1)
                for i, (e, lane, c, by) in enumerate(((0, 0, 3, 2), (1, 0, 0, 1), (1, 1, 0, 1), (0, 1, 3, 2))):
                    ins = nc.vector.tensor_scalar(far[:, i, :], qk[:, e, lane, c * P:(c + 1) * P],
                                                  etot[:, h % 2, lane, by:by + 1], None, ALU.mult)
                ins.then_inc(far_done, 1)

            def far_scores(h):
                decayed(h, 0)
                decayed(h, 1)
                decay_far(h)

            def mask_in_block(h, s):
                dve.wait_ge(scored, STEPS * h + s + 1)
                if s == 4:
                    dve.wait_ge(blk_copied, 4 * h + 4)
                else:
                    dve.wait_ge(blk_masked, 7 * h + s - 4)
                nc.vector.copy_predicated(pt[:, 0:16:5, :], masks[:, s - 4:s - 3, :].broadcast_to([P, TC, P]),
                                          bank[4 + (STEPS * h + s) % 2].rearrange("p (b t) -> p b t", b=TC)
                                          ).then_inc(blk_masked, 1)

            def o_norm(h):
                dve.wait_ge(orb_done, h + 1)
                dve.wait_ge(osb_done, h + 1)
                nc.vector.scalar_tensor_tensor(on[:, h, :], osb, half_gain, rb(4), ALU.mult,
                                               ALU.mult).then_inc(on_step, 1)
                dve.wait_ge(on_step, h + 1)
                nc.vector.tensor_tensor(on[:, h, :], on[:, h, :], sg[:, h, :], ALU.mult).then_inc(on_done, 1)

            def y_rg(k):
                dve.wait_ge(gelu_done, k + 1)
                dve.wait_ge(rg_scanned, RT + k + 1)
                nc.vector.scalar_tensor_tensor(hr[:, k, :], hr[:, k, :], 0.5, gg[:, k, :], ALU.mult,
                                               ALU.mult).then_inc(yrg_done, 1)

            def y_lower(k):
                dve.wait_ge(yhi_done, k + 1)
                src = hr[:, k, :] if k < RT else on[:, k - RT, :]
                nc.vector.tensor_tensor(ylo[:, k, :], src, yhi[:, k, :], ALU.subtract).then_inc(y_ready, 1)

            z_post(0)
            z_post(1)
            for m in range(2, 6):
                z_post(m)
                convolve(m - 2)
            dve.wait_ge(mix_loaded, 48)
            nc.vector.tensor_copy(masks[:].rearrange("p a t -> p (a t)"), mask_f).then_inc(masks_set, 1)
            z_post(6)
            one_minus_a2(0, 0)
            z_post(7)
            one_minus_a2(0, 1)
            z_post(8)
            one_minus_a2(0, 2)
            one_minus_a2(0, 3)
            z_post(9)
            recur(0, 0)
            recur(0, 1)
            z_post(10)
            sum_logs(0)
            recur(0, 2)
            z_post(11)
            far_scores(0)
            recur(0, 3)
            z_post(12)
            for r in range(HEADS):
                first = zi[("q", r + 1)] if r < 3 else None
                gaps = STEPS_AT[r == 3]
                if r == 3:
                    y_lower(0)
                    y_lower(1)
                    y_rg(2)
                    y_rg(3)
                for g, steps in enumerate(gaps):
                    for s in steps:
                        if s >= 2 and s < STEPS - 1:
                            decayed(r, s)
                        if s >= 5:
                            mask_in_block(r, s - 1)
                    if r < 3 and g and g % 2 == 0:
                        z_post(first + g // 2 - 1)
                    if r == 3 and g in (3, 5):
                        lo_u(U_OUT + g // 2 + 1)
                    if r < 3 and g == 7:
                        sum_logs(r + 1)
                    if r and g == (6 if r == 3 else 5):
                        rms_inverse(r - 1, orms_done, orinv_done, odiag_done)
                    if 0 < r < 3 and g == 7:
                        o_norm(r - 1)
                    if r == 0 and 5 <= g < 9:
                        one_minus_a2(1, g - 5)
                    if r == 1 and g in (5, 8):
                        recur(1, g // 8)
                    if r == 2 and g in (2, 4):
                        recur(1, 1 + g // 2)
                        y_rg(g // 2 - 1)
                    if r == 3 and g == 1:
                        y_lower(2)
                        y_lower(3)
                    if r == 3 and g == 3:
                        y_lower(4)
                        y_lower(5)
                mask_in_block(r, STEPS - 1)
                if r < 3:
                    far_scores(r + 1)
                    z_post(first + 4)
                else:
                    o_norm(2)
                    lo_u(U_OUT + 4)
            y_lower(6)
            rms_inverse(3, orms_done, orinv_done, odiag_done)
            o_norm(3)
            lo_u(U_OUT + 5)
            y_lower(7)
            columns(1)
            dve.wait_ge(cols_ready, 5)
            for d in range(KD):
                if d in (0, 4, 7):
                    lo_u(U_OUT + (6 if d == 0 else 7 if d == 4 else 8))
                update(1, d, bank[d])
            rms_inverse(2, rms_done, rinv_done, diag_done)
            lo_u(U_OUT + 9)
            h_split(2)
            for fp in range(2):
                up_step(1, fp, fp, 0)
            with dve.Fori(1, KF // 2) as i:
                for fp in range(2):
                    up_step(1, 2 * i + fp, fp, i)
            ffn_down(1)
            dve.wait_ge(rb_done, 4)
            for d in range(KD):
                nc.vector.scalar_tensor_tensor(outt[:, d, :], x[:, d, :], vec("norm3", d), rb(3), ALU.mult,
                                               ALU.mult).then_inc(out_ready, 1)

        @block.tensor
        def _(pe):
            def three(dst, slot, col, rhi, rlo, start, stop):
                a, b = whi[:, slot, col:col + P], wlo[:, slot, col:col + P]
                nc.tensor.matmul(dst, a, rhi, start=start, stop=False)
                nc.tensor.matmul(dst, a, rlo, start=False, stop=False)
                return nc.tensor.matmul(dst, b, rhi, start=False, stop=stop)

            def up_step(n, f, fp, i):
                j = (U_FFN1, U_FFN2)[n] // 2 + 2 * i + fp
                if isinstance(f, int) and f == 0:
                    for t in range(KD + 2):
                        for s, k in ((0, t), (1, t - 2)):
                            if not 0 <= k < KD:
                                continue
                            if k == 0:
                                pe.wait_ge(lo_done, 2 * j + 1 + s)
                            if s == 0:
                                pe.wait_ge(hlo_done, KD * (0, 2)[n] + k + 1)
                            ins = three(bank[2 * s], s, k * P, hhi[:, k, :], hlo[:, k, :], k == 0, k == KD - 1)
                            if k == KD - 1:
                                ins.then_inc(unit_used, 1)
                    return
                for s in range(2):
                    pe.wait_ge(lo_done, 2 * j + (s + 1))
                    if not (isinstance(f, int) and f < 2) or n:
                        pe.wait_ge((silu_done, gate_prod)[s], f + (KF * n - 1))
                    for k in range(KD):
                        ins = three(bank[2 * s + fp], s, k * P, hhi[:, k, :], hlo[:, k, :], k == 0, k == KD - 1)
                    ins.then_inc(unit_used, 1)

            def mod_sum(j):
                pe.wait_ge(ada_added, 8 * j + 8)
                if not (isinstance(j, int) and j == 0):
                    pe.wait_ge(mod_ready, 1 * j)
                for t in range(KD):
                    ins = nc.tensor.matmul(modp[:, t:t + 1], fin[:, t * P:(t + 1) * P], ones[:, 0:1], start=True,
                                           stop=True)
                ins.then_inc(mod_summed, 1)

            def down_unit(half, slot, rhs, first, last, wait_for):
                wait_for()
                for t in range(2):
                    rhi, rlo = rhs(t)
                    for d in range(4):
                        ins = three(bank[(4, 0)[half] + d], slot, (4 * t + d) * P, rhi, rlo, first and t == 0,
                                    last and t == 1)
                ins.then_inc(unit_used, 1)

            def rhs_of(k):
                return lambda t: tuple(g[:, bass.ds(k + t, 1), :].rearrange("p a t -> p (a t)") for g in (ghi, glo))

            def ffn_down(n):
                u0 = (U_FFN1, U_FFN2)[n] + 2 * KF
                for half in range(2):
                    u = u0 + HALF_UNITS * half

                    def wait_for(u=u, half=half):
                        pe.wait_ge(lo_done, u + 1)
                        if half == 0:
                            pe.wait_ge(glo_done, KF * n + 2)
                            pe.wait_ge(mod_ready, N_MOD)
                        else:
                            pe.wait_ge(glo_done, KF * n + KF)

                    down_unit(half, u % 2, rhs_of(0), True, False, wait_for)
                    with pe.Fori(0, (PAIR_UNITS - 1 if half else HALF_UNITS - 3) // 2) as i:
                        for s in range(2):
                            v = u + 1 + s

                            def wait_in(v=v, s=s, half=half):
                                pe.wait_ge(lo_done, 2 * i + (v + 1))
                                if half == 0:
                                    pe.wait_ge(glo_done, 4 * i + (KF * n + 4 + 2 * s))
                            down_unit(half, v % 2, rhs_of(4 * i + (2 + 2 * s)), False, False, wait_in)
                    if half == 0:
                        for s in range(2):
                            v = u + HALF_UNITS - 2 + s

                            def wait_last(v=v, s=s):
                                pe.wait_ge(lo_done, v + 1)
                                pe.wait_ge(glo_done, KF * n + KF - 2 + 2 * s)
                            down_unit(0, v % 2, rhs_of(KF - 4 + 2 * s), False, s == 1, wait_last)
                norm_sums((1, 3)[n], 0)
                for d in range(4):
                    v = u0 + HALF_UNITS + PAIR_UNITS + d
                    pe.wait_ge(lo_done, v + 1)
                    for k in range(8):
                        rhi, rlo = rhs_of(KF - 8 + k)(0)
                        ins = three(bank[d], v % 2, k * P, rhi, rlo, False, k == 7)
                    ins.then_inc(unit_used, 1)

            def norm_sums(n, part):
                if part == 0 and n:
                    pe.wait_ge(x_ready, KD * (n - 1) + 4)
                if part < 2:
                    pe.wait_ge(sq_added, 4 * n + 2 + 2 * part)
                else:
                    pe.wait_ge(sq_done, KD * n + 8)
                slot = (0, 0, 3)[part]
                for c in range(TC):
                    ins = nc.tensor.matmul(sums(n)[:, c:c + 1], sq[:, slot, c * P:(c + 1) * P], ones[:, 0:1],
                                           start=(part == 0 and c == 0), stop=(part == 2), skip_group_check=True)
                ins.then_inc(sq_used, 1)

            def keep_busy(b, n):
                for _ in range(n):
                    nc.tensor.matmul(bank[b][:, 0:P], ident[:], ones[:], start=True, stop=True)

            def norm_turn(n, b):
                norm_sums(n, 1)
                keep_busy(b, 3)
                norm_sums(n, 2)
                keep_busy(b, 5)
                norm_rb(n)
                if n < 3:
                    keep_busy(b, 11)

            def norm_rb(n):
                pe.wait_ge(diag_done, n + 1)
                nc.tensor.matmul(rb(n), ones[:], diag[:].rearrange("p c t -> p (c t)"), start=True,
                                 stop=True).then_inc(rb_done, 1)

            pe.wait_ge(vecs_loaded, 32)
            pe.wait_ge(ones_set, 2)
            pe.wait_ge(sq_done, 1)
            keep_busy(4, 11)
            norm_sums(0, 0)
            mod_sum(0)
            keep_busy(4, 7)
            norm_sums(0, 1)
            norm_sums(0, 2)
            keep_busy(4, 3)
            norm_rb(0)
            keep_busy(4, 8)
            mod_sum(1)
            keep_busy(4, 8)
            for fp in range(2):
                up_step(0, fp, fp, 0)
            with pe.Fori(1, 8) as i:
                up_step(0, 2 * i, 0, i)
                mod_sum(i + 1)
                up_step(0, 2 * i + 1, 1, i)
            with pe.Fori(8, KF // 2) as i:
                for fp in range(2):
                    up_step(0, 2 * i + fp, fp, i)
            ffn_down(0)
            norm_turn(1, 5)

            zi = {u: m for m, u in enumerate(Z_UNITS)}

            def z_half(m, part):
                u = U_MIX + m
                what, i = Z_UNITS[m]
                if part == 0:
                    pe.wait_ge(lo_done, u + 1)
                if what == "v":
                    k = 2 * i + part
                    if i == 0:
                        pe.wait_ge(hlo_done, KD + k + 1)
                    elif part == 0:
                        pe.wait_ge(hlo_done, KD + 2 * i + 2)
                    a, b = (w[:, u % 2, part * T:(part + 1) * T] for w in (whi, wlo))
                    for c in range(TC):
                        dst, cc = bank[2 + c], slice(c * P, (c + 1) * P)
                        nc.tensor.matmul(dst, hhi[:, k, cc], a, start=(k == 0), stop=False)
                        nc.tensor.matmul(dst, hhi[:, k, cc], b, start=False, stop=False)
                        ins = nc.tensor.matmul(dst, hlo[:, k, cc], a, start=False, stop=(k == KD - 1))
                else:
                    if part == 0 and m >= 4:
                        pe.wait_ge(z_evac, EVACS[m - 2])
                        if Z_UNITS[m - 2] in QG_COUNT:
                            pe.wait_ge(zq_done, QG_COUNT[Z_UNITS[m - 2]])
                    for k in range(4 * part, 4 * part + 4):
                        if m == 2:
                            pe.wait_ge(hlo_done, KD + k + 1)
                        ins = three(bank[m % 2], u % 2, k * P, hhi[:, k, :], hlo[:, k, :], k == 0, k == KD - 1)
                if part == 1:
                    ins.then_inc(unit_used, 1)

            def z_unit(m):
                z_half(m, 0)
                z_half(m, 1)

            def gate_sums(dr, ct):
                gi = RT * dr + ct
                pe.wait_ge(xc_ready, ct + 1)
                pe.wait_ge(mix_loaded, 48)
                if gi:
                    pe.wait_ge(gate_evac, 2 * (gi - (dr and ct > 0)))
                if dr:
                    pe.wait_ge(v_copied, 2)
                for w in range(2):
                    ins = nc.tensor.matmul(bank[gate_bank(dr, ct) + w], bd[:, 2 * dr + w, ct, :], xc[:, ct, :],
                                           start=True, stop=True)
                ins.then_inc(gates_summed, 1)

            def scores(h, s):
                before = step_before(h, s, 2)
                if before is None:
                    pe.wait_ge(v_copied, TC)
                else:
                    evac_wait(pe, *before)
                dst = bank[4 + (STEPS * h + s) % 2]
                QF, KB, KF_, QB = qk[:, 0, 0, :], qk[:, 0, 1, :], qk[:, 1, 0, :], qk[:, 1, 1, :]

                def c(a, i):
                    return a[:, i * P:(i + 1) * P]
                if s == 0:
                    pe.wait_ge(qk_done, 10 * h + 2)
                    pairs = [(c(KF_, 0), c(QF, 1)), (c(KB, 1), c(QB, 0)), (c(KF_, 2), c(QF, 3)), (c(KB, 3), c(QB, 2))]
                elif s == 1:
                    pe.wait_ge(far_done, h + 1)
                    pairs = [(k, q) for k in (far[:, 1, :], c(KF_, 1)) for q in (c(QF, 2), far[:, 0, :])]
                elif s == 2:
                    pairs = [(k, q) for k in (c(KB, 2), far[:, 3, :]) for q in (far[:, 2, :], c(QB, 1))]
                else:
                    pe.wait_ge(qk_done, 10 * h + s)
                    e = s - 1
                    q = qk[:, e % 2, 0, :] if s < STEPS - 1 else w3[:, h % 2, 1, :]
                    pairs = [(c(qk[:, e % 2, 1, :], i), c(q, i)) for i in range(TC)]
                for i, (k, q) in enumerate(pairs):
                    ins = nc.tensor.matmul(dst[:, i * P:(i + 1) * P], k, q, start=True, stop=True)
                ins.then_inc(scored, 1)

            def pv(h):
                pe.wait_ge(blk_copied, 4 * h + 4)
                pe.wait_ge(blk_masked, 7 * h + 7)
                if h:
                    pe.wait_ge(osb_done, h)
                    pe.wait_ge(osq_done, h)
                else:
                    pe.wait_ge(gate_evac, 16)
                for c in range(TC):
                    ins = nc.tensor.matmul(bank[6], vn[:, c, h * P:(h + 1) * P],
                                           pt[:, 4 * c:4 * c + 4, :].rearrange("p b t -> p (b t)"), start=(c == 0),
                                           stop=(c == TC - 1))
                ins.then_inc(pv_done, 1)

            def o_sums(h):
                pe.wait_ge(osq_done, h + 1)
                if h:
                    pe.wait_ge(on_done, h)
                for c in range(TC):
                    ins = nc.tensor.matmul(sums(4)[:, c:c + 1], osq[:, c * P:(c + 1) * P], ones[:, 0:1], start=True,
                                           stop=True)
                ins.then_inc(osum_done, 1)

            def o_rb(h):
                pe.wait_ge(odiag_done, h + 1)
                nc.tensor.matmul(rb(4), ones[:], diag[:].rearrange("p c t -> p (c t)"), start=True,
                                 stop=True).then_inc(orb_done, 1)

            def out_blocks(first, behind):
                for n in range(first, behind):
                    k, o = OUT_BLOCKS[n]
                    u = U_OUT + n // 8
                    if n % 8 == 0:
                        pe.wait_ge(lo_done, u + 1)
                    if n == 0:
                        pe.wait_ge(z_evac, EVACS[-1])
                        pe.wait_ge(gate_evac, 16)
                    if n == OUT_BLOCKS.index((0, 4)):
                        evac_wait(pe, 3, STEPS - 1)
                    if n == OUT_BLOCKS.index((0, 6)):
                        pe.wait_ge(on_done, HEADS)
                    if o == 0:
                        pe.wait_ge(y_ready, k + 1)
                    ins = three(bank[o], u % 2, n % 8 * P, yhi[:, k, :], ylo[:, k, :], k == 0, k == KD - 1)
                    if n % 8 == 7:
                        ins.then_inc(unit_used, 1)

            for m in range(13):
                z_unit(m)
                if 4 <= m < 8:
                    gate_sums(0, m - 4)
            for r in range(HEADS):
                first = zi[("q", r + 1)] if r < 3 else None
                for g, steps in enumerate(STEPS_AT[r == 3]):
                    if r < 3:
                        z_half(first + g // 2, g % 2)
                    elif g:
                        out_blocks(4 * (g - 1), 4 * g)
                    if r and g == 0:
                        pv(r - 1)
                    for s in steps:
                        scores(r, s)
                    if r and g == (1 if r == 3 else 3):
                        o_sums(r - 1)
                    if 0 < r < 3 and g == 6:
                        o_rb(r - 1)
                    if r == 0 and 3 <= g < 7:
                        gate_sums(1, g - 3)
            o_rb(2)
            pv(3)
            out_blocks(24, 26)
            o_sums(3)
            out_blocks(26, 28)
            o_rb(3)
            out_blocks(28, 58)
            norm_sums(2, 0)
            out_blocks(58, 64)
            norm_turn(2, 2)
            for fp in range(2):
                up_step(1, fp, fp, 0)
            with pe.Fori(1, KF // 2) as i:
                for fp in range(2):
                    up_step(1, 2 * i + fp, fp, i)
            ffn_down(1)
            norm_turn(3, 5)


def _block_units(w, blocks):
    b = w.reshape(-1, P, KD, P).transpose(0, 2, 1, 3)
    k, o = (np.array(v) for v in zip(*blocks))
    return b[k, o].reshape(-1, 8, P, P).transpose(0, 2, 1, 3).reshape(-1, P, UNIT)


def _col_units(w):
    n = w.shape[1] // P
    return w.reshape(KD, P, n, P).transpose(2, 1, 0, 3).reshape(n, P, UNIT)


def _cols(v):
    return np.ascontiguousarray(v).reshape(-1, P).T


def layout(inputs):
    i = {k: np.asarray(v) for k, v in inputs.items()}
    units = []

    down = ([(k, o) for k in range(KF) for o in range(4)] + [(k, o) for k in range(2 * PAIR_UNITS) for o in range(4, KD)]
            + [(k, o) for o in range(4, KD) for k in range(2 * PAIR_UNITS, KF)])

    def ffn(w1, w3, w2):
        units.append(np.stack([_col_units(w1), _col_units(w3)], axis=1).reshape(2 * KF, P, UNIT))
        units.append(_block_units(w2, down))

    ffn(i["ffn1_w1"][0], i["ffn1_w3"][0], i["ffn1_w2"][0])
    w_in = i["w_in"][0]
    v = w_in[:, Z_COLUMN["v"]:Z_COLUMN["v"] + T].reshape(4, 2, P, T).transpose(0, 2, 1, 3).reshape(4, P, UNIT)
    z = _col_units(w_in)
    units.append(np.stack([v[t] if what == "v" else z[Z_COLUMN[what] // P + t] for what, t in Z_UNITS]))
    w_out = i["w_out"][0]
    units.append(_block_units(np.concatenate([w_out[T:], w_out[:T]]), OUT_BLOCKS))
    ffn(i["ffn2_w1"][0], i["ffn2_w3"][0], i["ffn2_w2"][0])
    order = [MOD_AT[m] for m in MODS]
    wada = i["w_ada"][0].reshape(KD, P, N_MOD, D).transpose(2, 0, 1, 3)[order].reshape(N_MOD * KD, P, D)
    vecs = [_cols(i["c"][0]), _cols(i["b_ada"][0].reshape(N_MOD, D)[order].reshape(-1)),
            _cols(i["ffn1_norm"][0]), _cols(i["mix_norm"][0]), _cols(i["ffn2_norm"][0]), _cols(i["final_norm"]),
            _cols(i["hg_lb_fwd"][0]), _cols(i["hg_lb_bwd"][0]), _cols(i["hg_lb_fwd"][1]), _cols(i["hg_lb_bwd"][1]),
            _cols(i["hg_out_norm"][0]), _cols(i["rg_conv_w"][0].reshape(-1)), _cols(i["rg_conv_b"][0])]
    for a, b in (("rg_ba_fwd", "rg_ba_bwd"), ("rg_bx_fwd", "rg_bx_bwd"), ("rg_lam_fwd", "rg_lam_bwd")):
        vecs += [_cols(i[a][0]), _cols(i[b][0])]
    bd = np.zeros((P, 4, RT, P), np.float32)
    for w, name in enumerate(("rg_wa_fwd", "rg_wx_fwd", "rg_wa_bwd", "rg_wx_bwd")):
        for n in range(8):
            o = 64 * (n % 2)
            bd[o:o + 64, w, n // 2, o:o + 64] = i[name][0, n]
    xor = np.arange(P)[:, None] ^ np.arange(P)[None, :]
    mask = np.stack([xor < w for w in (64, 32, 16, 8, 4, 2, 1)], axis=1).astype(np.float32)
    resets = np.ones((P, T), np.float32)
    resets[:, ::P] = 0.0
    return {
        "xt": np.ascontiguousarray(i["x"][0].T), "wu": np.ascontiguousarray(np.concatenate(units)),
        "wada": np.ascontiguousarray(wada), "vecs": np.ascontiguousarray(np.concatenate(vecs, axis=1)),
        "bd": bd, "consts": np.concatenate([np.eye(P, dtype=np.float32), resets, mask.reshape(P, 7 * P)], axis=1),
    }


def kernel(**inputs):
    import concourse.bacc as bacc
    from concourse.bass_utils import run_bass_kernel_spmd

    nc = bacc.Bacc("TRN2", target_bir_lowering=False, num_devices=1)
    arrays = layout(inputs)
    aps = [nc.dram_tensor(n, a.shape, mybir.dt.from_np(a.dtype), kind="ExternalInput").ap() for n, a in arrays.items()]
    out = nc.dram_tensor("out", (D, T), F32, kind="ExternalOutput").ap()
    build(nc, *aps, out)
    r = run_bass_kernel_spmd(nc, [arrays], core_ids=[0])
    return np.ascontiguousarray(r.results[0]["out"].T)[None]
```
